# Optimizing a Trainium2 kernel written in Bass

```python
import math
import jax, jax.numpy as jnp
from jax import lax
import numpy as np

D_MODEL = 1024
BATCH = 1
SEQ = 128
DEPTH = 2
DEC_BATCH = 1
DEC_SEQ = 128
PAST_LEN = 128

GRID_W = 64
N_EVEN = (DEPTH + 1) // 2
N_ODD = DEPTH // 2

A_WIDTH = D_MODEL // 2
A_HEAD = 64
A_HEADS = A_WIDTH // A_HEAD
DECAY_LORA = 64
ICLR_LORA = 64
GATE_LORA = 128
GN_EPS = 64e-5
B_WIDTH = D_MODEL - A_WIDTH
CONV_W = 31
A_COLS = 3 * A_WIDTH + 2 * DECAY_LORA + 2 * ICLR_LORA + GATE_LORA
A_SPLITS = (A_WIDTH, 2 * A_WIDTH, 3 * A_WIDTH, 3 * A_WIDTH + 2 * DECAY_LORA,
            3 * A_WIDTH + 2 * DECAY_LORA + 2 * ICLR_LORA)
EVEN_IN = A_COLS + 2 * B_WIDTH
C_HEAD = 64
C_HEADS = D_MODEL // (2 * C_HEAD)
C_INNER = C_HEADS * 2 * C_HEAD
ROPE_BASE = 10000.0
RMS_EPS = 1e-5
N_GROUPS = 4
EXPERTS_PER_GROUP = 8
N_EXPERTS = N_GROUPS * EXPERTS_PER_GROUP
TOP_K_INNER = 2
EXPERT_FF = 256
LN_EPS = 1e-5
DEEPNORM_ALPHA = (2 * DEPTH) ** 0.25
DEEPNORM_BETA = (8 * DEPTH) ** -0.25

F32 = jnp.float32

kernel_name = 'hybrid_rwkv7_conformer_diffattn_hmoe_dit_step'

def layer_norm(x, g, b, eps=LN_EPS):
    xf = x.astype(F32)
    mu = jnp.mean(xf, -1, keepdims=True)
    var = jnp.mean(jnp.square(xf - mu), -1, keepdims=True)
    y = (xf - mu) * lax.rsqrt(var + eps) * g.astype(F32) + b.astype(F32)
    return y.astype(x.dtype)

def ada_params(cond, w, b):
    m = jnp.einsum('nd,de->ne', jax.nn.silu(cond), w) + b
    return [t[:, None, :] for t in jnp.split(m, 6, axis=-1)]

def modulate(x, shift, scale):
    return x * (1 + scale) + shift

def post_norm(x, y, g, b):
    return layer_norm(DEEPNORM_ALPHA * x + y, g, b)

def token_shift(p):
    pad = jnp.pad(p, ((0, 0), (1, 1), (0, 0)))
    return 0.5 * (pad[:, :-2] + pad[:, 2:])

def wkv_scan(r, w, k, v, kk, a, s0, reverse):
    def step(s, inp):
        r_t, w_t, k_t, v_t, kk_t, a_t = inp
        sa = jnp.einsum('bhvk,bhk->bhv', s, -kk_t)
        s = (s * w_t[:, :, None, :] + sa[..., None] * (kk_t * a_t)[:, :, None, :]
             + v_t[..., None] * k_t[:, :, None, :])
        return s, jnp.einsum('bhvk,bhk->bhv', s, r_t)
    xs = tuple(jnp.swapaxes(t, 0, 1) for t in (r, w, k, v, kk, a))
    s_fin, y = lax.scan(step, s0, xs, reverse=reverse)
    return jnp.swapaxes(y, 0, 1), s_fin

def even_mixer(h, in_w, pw_b, ts_mu, w0, w_up, a0, a_up, g_up, k_k, k_a, r_k,
               gn_g, gn_b, dw_w, dw_b, cln_g, cln_b, out_w, s0):
    nb, nt, _ = h.shape
    proj = jnp.einsum('btd,de->bte', h, in_w)
    pa = proj[..., :A_COLS]
    pa = pa + ts_mu * (token_shift(pa) - pa)
    pb = proj[..., A_COLS:] + pw_b
    r, k, v, wd, ad, gd = jnp.split(pa, A_SPLITS, axis=-1)
    wd = wd.reshape(nb, nt, 2, DECAY_LORA)
    ad = ad.reshape(nb, nt, 2, ICLR_LORA)
    w_pre = (w0 + jnp.einsum('btzl,zlc->btzc', jnp.tanh(wd), w_up)).astype(F32)
    decay = jnp.exp(-jnp.exp(-jax.nn.softplus(-w_pre) - 0.5))
    a = jax.nn.sigmoid((a0 + jnp.einsum('btzl,zlc->btzc', ad, a_up)).astype(F32))
    g = jnp.einsum('btl,lc->btc', jax.nn.sigmoid(gd), g_up).astype(F32)
    heads = lambda t: t.reshape(nb, nt, A_HEADS, A_HEAD)
    rf, kf, vf = heads(r.astype(F32)), heads(k.astype(F32)), heads(v.astype(F32))
    kk = heads((k * k_k).astype(F32))
    kk = kk * lax.rsqrt(jnp.maximum(jnp.sum(kk * kk, -1, keepdims=True), 1e-24))
    ka = k_a.astype(F32).reshape(A_HEADS, A_HEAD)
    rk = r_k.astype(F32)
    ys, bonuses, finals = [], [], []
    for z in range(2):
        a_z = heads(a[:, :, z])
        k_z = kf * (1 + (a_z - 1) * ka)
        y_z, s_z = wkv_scan(rf, heads(decay[:, :, z]), k_z, vf, kk, a_z,
                            s0[:, z].astype(F32), reverse=(z == 1))
        ys.append(y_z)
        bonuses.append(jnp.sum(rf * k_z * rk, -1, keepdims=True) * vf)
        finals.append(s_z)
    y = ys[0] + ys[1]
    mu = jnp.mean(y, -1, keepdims=True)
    var = jnp.mean(jnp.square(y - mu), -1, keepdims=True)
    yn = ((y - mu) * lax.rsqrt(var + GN_EPS) * gn_g.astype(F32).reshape(A_HEADS, A_HEAD)
          + gn_b.astype(F32).reshape(A_HEADS, A_HEAD))
    out_a = ((yn + bonuses[0] + bonuses[1]).reshape(nb, nt, A_WIDTH) * g).astype(h.dtype)
    glu = pb[..., :B_WIDTH] * jax.nn.sigmoid(pb[..., B_WIDTH:])
    conv = lax.conv_general_dilated(glu, dw_w[:, None, :].astype(glu.dtype), (1,),
                                    [(CONV_W // 2, CONV_W // 2)],
                                    dimension_numbers=('NWC', 'WIO', 'NWC'),
                                    feature_group_count=B_WIDTH) + dw_b
    out_b = jax.nn.silu(layer_norm(conv, cln_g, cln_b)).astype(h.dtype)
    out = jnp.einsum('bte,ed->btd', jnp.concatenate([out_a, out_b], axis=-1), out_w)
    return out, jnp.stack(finals, axis=1)

def rope_2d(x, row, col):
    half = C_HEAD // 2
    nf = half // 2
    inv = ROPE_BASE ** (-jnp.arange(nf, dtype=F32) / nf)
    def rot(xp, pos):
        ang = pos.astype(F32)[:, None] * inv
        cos = jnp.cos(ang)[None, :, None, None, :]
        sin = jnp.sin(ang)[None, :, None, None, :]
        x1 = xp[..., :nf].astype(F32)
        x2 = xp[..., nf:].astype(F32)
        return jnp.concatenate([x1 * cos - x2 * sin, x1 * sin + x2 * cos], axis=-1)
    return jnp.concatenate([rot(x[..., :half], row), rot(x[..., half:], col)], axis=-1).astype(x.dtype)

def diff_qkv(h, in_w):
    nb, nt, _ = h.shape
    q, k, v = jnp.split(jnp.einsum('btd,de->bte', h, in_w), 3, axis=-1)
    return (q.reshape(nb, nt, C_HEADS, 2, C_HEAD), k.reshape(nb, nt, C_HEADS, 2, C_HEAD),
            v.reshape(nb, nt, C_HEADS, 2 * C_HEAD))

def diff_lambda(lq1, lk1, lq2, lk2, lam_init):
    return (jnp.exp(jnp.sum(lq1.astype(F32) * lk1.astype(F32)))
            - jnp.exp(jnp.sum(lq2.astype(F32) * lk2.astype(F32))) + lam_init)

def diff_attend(q, k, v, lam, lam_init, subln_g):
    nb, nq = q.shape[0], q.shape[1]
    s = jnp.einsum('bqhzd,bkhzd->bhzqk', q, k).astype(F32) * (C_HEAD ** -0.5)
    p = jax.nn.softmax(s, axis=-1)
    attn = p[:, :, 0] - lam * p[:, :, 1]
    o = jnp.einsum('bhqk,bkhe->bqhe', attn, v.astype(F32))
    o = o * lax.rsqrt(jnp.mean(o * o, -1, keepdims=True) + RMS_EPS) * subln_g.astype(F32) * (1.0 - lam_init)
    return o.reshape(nb, nq, C_INNER).astype(q.dtype)

def hier_moe(h, rg_w, rg_b, re_w, re_b, w_gate, w_up, w_down):
    nb, nt, d = h.shape
    hf = h.reshape(nb * nt, d)
    g_logits = (hf @ rg_w + rg_b).astype(F32)
    g_idx = jnp.argmax(g_logits, axis=-1)
    g_p = jnp.take_along_axis(jax.nn.softmax(g_logits, axis=-1), g_idx[:, None], axis=-1)
    e_logits = (hf @ re_w + re_b).astype(F32).reshape(-1, N_GROUPS, EXPERTS_PER_GROUP)
    e_in = jnp.take_along_axis(e_logits, g_idx[:, None, None], axis=1)[:, 0]
    top_v, top_i = lax.top_k(e_in, TOP_K_INNER)
    w_sel = g_p * jax.nn.softmax(top_v, axis=-1)
    eid = g_idx[:, None] * EXPERTS_PER_GROUP + top_i
    gates = jnp.sum(jax.nn.one_hot(eid, N_EXPERTS, dtype=F32) * w_sel[..., None], axis=1)
    hid = jax.nn.silu(jnp.einsum('nd,edf->nef', hf, w_gate)) * jnp.einsum('nd,edf->nef', hf, w_up)
    out = jnp.einsum('nef,efd->nd', hid * gates[..., None].astype(hid.dtype), w_down)
    return out.reshape(nb, nt, d).astype(h.dtype)

def setup_inputs(seed: int = 0) -> dict:
    key = jax.random.key(seed)
    ks = iter(jax.random.split(key, 64))
    D = D_MODEL
    def nrm(shape, scale=1.0):
        return scale * jax.random.normal(next(ks), shape, F32)
    def uni(shape, lo, hi):
        return jax.random.uniform(next(ks), shape, F32, lo, hi)
    inp = {}
    inp['x_prompt'] = nrm((BATCH, SEQ, D))
    inp['x_sample'] = nrm((DEC_BATCH, DEC_SEQ, D))
    inp['state_wkv'] = nrm((DEC_BATCH, N_EVEN, 2, A_HEADS, A_HEAD, A_HEAD))
    inp['cache_k'] = nrm((DEC_BATCH, N_ODD, PAST_LEN, C_HEADS, 2 * C_HEAD))
    inp['cache_v'] = nrm((DEC_BATCH, N_ODD, PAST_LEN, C_HEADS, 2 * C_HEAD))
    inp['c'] = nrm((DEC_BATCH, D))
    inp['c_ctx'] = nrm((D,))
    inp['mod_w'] = nrm((DEPTH, D, 6 * D), 0.5 * D ** -0.5)
    inp['mod_b'] = nrm((DEPTH, 6 * D), 0.02)
    inp['ln1_g'] = 1.0 + nrm((DEPTH, D), 0.05)
    inp['ln1_b'] = nrm((DEPTH, D), 0.02)
    inp['ln2_g'] = 1.0 + nrm((DEPTH, D), 0.05)
    inp['ln2_b'] = nrm((DEPTH, D), 0.02)
    inp['ev_in_w'] = nrm((N_EVEN, D, EVEN_IN), D ** -0.5)
    inp['ev_pw_b'] = nrm((N_EVEN, 2 * B_WIDTH), 0.02)
    inp['ev_ts_mu'] = uni((N_EVEN, A_COLS), 0.2, 0.8)
    inp['ev_w0'] = -2.0 + nrm((N_EVEN, 2, A_WIDTH), 1.0)
    inp['ev_w_up'] = nrm((N_EVEN, 2, DECAY_LORA, A_WIDTH), 0.1)
    inp['ev_a0'] = nrm((N_EVEN, 2, A_WIDTH), 0.5)
    inp['ev_a_up'] = nrm((N_EVEN, 2, ICLR_LORA, A_WIDTH), 0.1)
    inp['ev_g_up'] = nrm((N_EVEN, GATE_LORA, A_WIDTH), GATE_LORA ** -0.5)
    inp['ev_k_k'] = 0.85 + nrm((N_EVEN, A_WIDTH), 0.05)
    inp['ev_k_a'] = 1.0 + nrm((N_EVEN, A_WIDTH), 0.05)
    inp['ev_r_k'] = nrm((N_EVEN, A_HEADS, A_HEAD), 0.1)
    inp['ev_gn_g'] = 1.0 + nrm((N_EVEN, A_WIDTH), 0.05)
    inp['ev_gn_b'] = nrm((N_EVEN, A_WIDTH), 0.02)
    inp['ev_dw_w'] = nrm((N_EVEN, CONV_W, B_WIDTH), CONV_W ** -0.5)
    inp['ev_dw_b'] = nrm((N_EVEN, B_WIDTH), 0.02)
    inp['ev_cln_g'] = 1.0 + nrm((N_EVEN, B_WIDTH), 0.05)
    inp['ev_cln_b'] = nrm((N_EVEN, B_WIDTH), 0.02)
    inp['ev_out_w'] = nrm((N_EVEN, A_WIDTH + B_WIDTH, D), DEEPNORM_BETA * (A_WIDTH + B_WIDTH) ** -0.5)
    inp['od_in_w'] = nrm((N_ODD, D, 3 * C_INNER), D ** -0.5)
    inp['od_lq1'] = nrm((N_ODD, C_HEAD), 0.1)
    inp['od_lk1'] = nrm((N_ODD, C_HEAD), 0.1)
    inp['od_lq2'] = nrm((N_ODD, C_HEAD), 0.1)
    inp['od_lk2'] = nrm((N_ODD, C_HEAD), 0.1)
    inp['od_subln_g'] = 1.0 + nrm((N_ODD, 2 * C_HEAD), 0.05)
    inp['od_out_w'] = nrm((N_ODD, C_INNER, D), DEEPNORM_BETA * C_INNER ** -0.5)
    inp['rg_w'] = nrm((DEPTH, D, N_GROUPS), D ** -0.5)
    inp['rg_b'] = nrm((DEPTH, N_GROUPS), 0.01)
    inp['re_w'] = nrm((DEPTH, D, N_EXPERTS), D ** -0.5)
    inp['re_b'] = nrm((DEPTH, N_EXPERTS), 0.01)
    inp['ffn_w_gate'] = nrm((DEPTH, N_EXPERTS, D, EXPERT_FF), D ** -0.5)
    inp['ffn_w_up'] = nrm((DEPTH, N_EXPERTS, D, EXPERT_FF), D ** -0.5)
    inp['ffn_w_down'] = nrm((DEPTH, N_EXPERTS, EXPERT_FF, D), DEEPNORM_BETA * EXPERT_FF ** -0.5)
    return inp

def reference(x_prompt, x_sample, state_wkv, cache_k, cache_v, c, c_ctx,
              mod_w, mod_b, ln1_g, ln1_b, ln2_g, ln2_b,
              ev_in_w, ev_pw_b, ev_ts_mu, ev_w0, ev_w_up, ev_a0, ev_a_up, ev_g_up,
              ev_k_k, ev_k_a, ev_r_k, ev_gn_g, ev_gn_b, ev_dw_w, ev_dw_b, ev_cln_g, ev_cln_b, ev_out_w,
              od_in_w, od_lq1, od_lk1, od_lq2, od_lk2, od_subln_g, od_out_w,
              rg_w, rg_b, re_w, re_b, ffn_w_gate, ffn_w_up, ffn_w_down):
    nbp = x_prompt.shape[0]
    n_lat = x_sample.shape[1]
    rows = n_lat // GRID_W
    row = jnp.repeat(jnp.arange(rows), GRID_W)
    col = jnp.tile(jnp.arange(GRID_W), rows)
    cond_ctx = c_ctx[None, :]
    xp, xs = x_prompt, x_sample
    new_wkv, new_k, new_v = [], [], []
    for l in range(DEPTH):
        mp = ada_params(cond_ctx, mod_w[l], mod_b[l])
        ms = ada_params(c, mod_w[l], mod_b[l])
        hp = modulate(xp, mp[0], mp[1])
        hs = modulate(xs, ms[0], ms[1])
        if l % 2 == 0:
            i = l // 2
            ev = (ev_in_w[i], ev_pw_b[i], ev_ts_mu[i], ev_w0[i], ev_w_up[i], ev_a0[i], ev_a_up[i],
                  ev_g_up[i], ev_k_k[i], ev_k_a[i], ev_r_k[i], ev_gn_g[i], ev_gn_b[i], ev_dw_w[i],
                  ev_dw_b[i], ev_cln_g[i], ev_cln_b[i], ev_out_w[i])
            s0 = jnp.zeros((nbp, 2, A_HEADS, A_HEAD, A_HEAD), F32)
            mix_p, st = even_mixer(hp, *ev, s0)
            mix_s, _ = even_mixer(hs, *ev, state_wkv[:, i])
            new_wkv.append(st)
        else:
            j = l // 2
            lam_init = 0.8 - 0.6 * math.exp(-0.3 * l)
            lam = diff_lambda(od_lq1[j], od_lk1[j], od_lq2[j], od_lk2[j], lam_init)
            qp, kp, vp = diff_qkv(hp, od_in_w[j])
            mix_p = jnp.einsum('bte,ed->btd', diff_attend(qp, kp, vp, lam, lam_init, od_subln_g[j]), od_out_w[j])
            new_k.append(kp.reshape(nbp, -1, C_HEADS, 2 * C_HEAD))
            new_v.append(vp)
            qs, kls, vls = diff_qkv(hs, od_in_w[j])
            qs = rope_2d(qs, row, col)
            kls = rope_2d(kls, row, col)
            ck = cache_k[:, j]
            keys = jnp.concatenate([ck.reshape(ck.shape[0], ck.shape[1], C_HEADS, 2, C_HEAD).astype(kls.dtype), kls], axis=1)
            vals = jnp.concatenate([cache_v[:, j].astype(vls.dtype), vls], axis=1)
            mix_s = jnp.einsum('bte,ed->btd', diff_attend(qs, keys, vals, lam, lam_init, od_subln_g[j]), od_out_w[j])
        xp = post_norm(xp, mp[2] * mix_p, ln1_g[l], ln1_b[l])
        xs = post_norm(xs, ms[2] * mix_s, ln1_g[l], ln1_b[l])
        moe = (rg_w[l], rg_b[l], re_w[l], re_b[l], ffn_w_gate[l], ffn_w_up[l], ffn_w_down[l])
        xp = post_norm(xp, mp[5] * hier_moe(modulate(xp, mp[3], mp[4]), *moe), ln2_g[l], ln2_b[l])
        xs = post_norm(xs, ms[5] * hier_moe(modulate(xs, ms[3], ms[4]), *moe), ln2_g[l], ln2_b[l])
    y_prompt = xp
    y_sample = xs
    new_state_wkv = jnp.stack(new_wkv, axis=1)
    new_cache_k = jnp.stack(new_k, axis=1)
    new_cache_v = jnp.stack(new_v, axis=1)
    return (y_prompt, y_sample, new_state_wkv, new_cache_k, new_cache_v)


_drawn_inputs = setup_inputs


def setup_inputs(seed=0):
    import zlib

    import numpy as np

    out = dict(_drawn_inputs(seed))
    spreads = {}
    factors = {'state_wkv': 4.185,
     'ev_pw_b': 8.0,
     'ev_r_k': 3.676,
     'ev_gn_g': 25.506,
     'ev_gn_b': 50.104,
     'ev_dw_b': 8.0,
     'ev_cln_g': 26.376,
     'ev_cln_b': 42.772,
     'od_lq1': 8.0,
     'od_lk1': 8.0,
     'od_lq2': 8.0,
     'od_lk2': 5.826,
     'od_subln_g': 8.0,
     'rg_b': 200.0,
     're_b': 55.755}
    for name, (base, spread) in spreads.items():
        noise = np.random.default_rng([zlib.crc32(name.encode()), seed]).standard_normal(out[name].shape)
        drawn = base * np.exp(spread * noise) if base else spread * noise
        out[name] = __import__('jax').numpy.asarray(drawn.astype(out[name].dtype))
    for name, factor in factors.items():
        out[name] = (out[name] * factor).astype(out[name].dtype)
    return out
```

```python
from contextlib import ExitStack

import numpy as np
import concourse.bass as bass
from concourse import mybir

F32 = mybir.dt.float32
I32 = mybir.dt.int32
ALU = mybir.AluOpType
ACT = mybir.ActivationFunctionType
AX = mybir.AxisListType.X

P = 128
D = 1024
KT = D // P
T = 128
NS = 2
H = 8
HD = 64
AW = 512
AT = AW // P
CONV_W = 31
PADC = CONV_W // 2
GN_EPS = 64e-5
LN_EPS = 1e-5
RMS_EPS = 1e-5
ALPHA = 4 ** 0.25
NG, EPG = 4, 8
NE = NG * EPG
FF = 256
CH = 64
GRID_W = 64
ROPE_BASE = 10000.0
LAM_INIT = 0.8 - 0.6 * float(np.exp(-0.3))
E_HALF = float(np.exp(-0.5))

WD, AD, GD = 12, 13, 14
TILES = [WD, AD, GD] + [4, 5, 6, 7] + [0, 1, 2, 3] + [8, 9, 10, 11]
for _t in range(AT):
    TILES += [15 + _t, 19 + _t]
NPA = 15

V_MU, V_PW, V_A0, V_KK, V_KA, V_RK, V_DB, V_DW = 0, 15, 23, 31, 35, 39, 43, 47
NVEC = V_DW + CONV_W * AT

C_ID, C_SU, C_SL, C_UI, C_LI = 0, 128, 256, 384, 512
C_CUM, C_BLK, C_HSEL, C_IOTA, C_ONE = 640, 770, 898, 930, 1058
C_SEL, C_G4 = 1186, 1442
NCST = C_G4 + 64


def constants():
    c = np.zeros((P, NCST), np.float32)
    r, q = np.arange(P)[:, None], np.arange(P)[None, :]
    c[:, C_ID:C_ID + P] = r == q
    c[:, C_SU:C_SU + P] = r < q
    c[:, C_SL:C_SL + P] = r > q
    c[:, C_UI:C_UI + P] = r <= q
    c[:, C_LI:C_LI + P] = r >= q
    c[:, C_CUM:C_CUM + T + 1] = -E_HALF * (r < np.arange(T + 1)[None, :])
    c[:, C_BLK:C_BLK + P] = (r // HD) == (q // HD)
    for t in range(AT):
        for h in range(H):
            c[:, C_HSEL + t * H + h] = (2 * t + np.arange(P) // HD) == h
    c[:, C_IOTA:C_IOTA + P] = q
    c[:, C_ONE:C_ONE + P] = 1.0
    for s in range(NS):
        c[s::32, C_SEL + s * P:C_SEL + (s + 1) * P] = 1.0
    c[:, C_G4:C_G4 + 4] = np.arange(4)
    c[:, C_G4 + 4:C_G4 + 12] = np.arange(8)
    c[:, C_G4 + 12:C_G4 + 52] = np.arange(40)
    return c


def rope_tables():
    nf = HD // 4
    inv = ROPE_BASE ** (-np.arange(nf, dtype=np.float64) / nf)
    tok = np.arange(T)
    pos = np.stack([tok // GRID_W, tok % GRID_W], 1)
    ang = pos[:, :, None] * inv[None, None, :]
    return np.stack([np.cos(ang), np.sin(ang)], 1).reshape(T, 4 * nf).astype(np.float32)


class Banks:

    def __init__(self, ps, banks, filled, drained):
        self.ps, self.banks, self.filled, self.drained = ps, banks, filled, drained
        self.no, self.by, self.nth, self.order = {}, {}, {}, []
        self.count = {e: 0 for e in drained}
        self.seen = {}

    def add(self, key, by):
        assert key not in self.no, key
        self.no[key] = len(self.order)
        self.order.append(key)
        self.by[key] = by
        self.count[by] += 1
        self.nth[key] = self.count[by]

    def bank(self, key):
        return self.ps[:, self.banks[self.no[key] % len(self.banks)], :]

    def wait_free(self, pe, key):
        n = self.no[key] - len(self.banks)
        if n >= 0:
            old = self.order[n]
            pe.wait_ge(self.drained[self.by[old]], self.nth[old])

    def wait_filled(self, eng, key):
        eng.wait_ge(self.filled, self.no[key] + 1)

    def drained_by(self, ins, key):
        by = self.by[key]
        self.seen[by] = self.seen.get(by, 0) + 1
        assert self.seen[by] == self.nth[key], key
        ins.then_inc(self.drained[by], 1)

    def wait_drained(self, eng, key):
        eng.wait_ge(self.drained[self.by[key]], self.nth[key])


def copy3(eng, BK, key, hT, s, k0):
    BK.wait_filled(eng, key)
    dst = hT[:, k0:k0 + 4, s * T:(s + 1) * T]
    src = BK.bank(key).rearrange("p (k n) -> p k n", k=4)
    if BK.by[key] == "act":
        BK.drained_by(eng.activation(dst, src, ACT.Copy), key)
    else:
        BK.drained_by(eng.tensor_copy(dst, src), key)


class Steps:

    def __init__(self, eng, sem):
        self.eng, self.sem, self.n = eng, sem, 0

    def inc(self, ins):
        self.n += 1
        ins.then_inc(self.sem, 1)
        return self.n

    def wait(self, n=None):
        self.eng.wait_ge(self.sem, self.n if n is None else n)

    def link(self, ins):
        self.inc(ins)
        self.wait()


ARENA = 53110


def build(nc, a, o, dbg=None):
    ctx = ExitStack()
    sems = {}

    def S(name):
        if name not in sems:
            sems[name] = ctx.enter_context(nc.semaphore(name))
        return sems[name]

    arena = ctx.enter_context(nc.sbuf_tensor("arena", [P, ARENA], F32))
    meta = ctx.enter_context(nc.sbuf_tensor("meta", [1, 2, 48], I32))
    ps = ctx.enter_context(nc.psum_tensor("ps", [P, 8, 512], F32))
    top = [0]

    def region(n):
        at = top[0]
        top[0] += n
        assert top[0] <= ARENA, top[0]
        return at

    def view(at, n, pattern=None, **sizes):
        v = arena[:, at:at + n]
        return v.rearrange(pattern, **sizes) if pattern else v

    cst = view(region(NCST), NCST)
    vec = view(region(NVEC), NVEC)
    nvec = view(region(64), 64)
    x = view(region(2 * D), 2 * D, "p (s n) -> p s n", s=NS)
    hT = view(region(KT * 256), KT * 256, "p (k n) -> p k n", k=KT)
    rowbuf = view(region(D), D)
    gaterow = view(region(D), D)
    mbias = view(region(3 * 512), 3 * 512, "p (g n) -> p g n", g=3)
    gbc_at = region(2 * D)
    gbc = view(gbc_at, 2 * D, "p (s n) -> p s n", s=NS)
    lnp_at = region(2 * D)
    lnp = view(lnp_at, 2 * D, "p (g n) -> p g n", g=2)
    modT = view(region(192), 192, "p (l m k s) -> p l m k s", l=2, m=6, s=NS)
    cond = view(region(16), 16, "p (k s) -> p k s", s=NS)
    condw = view(region(32), 32)
    small = view(region(320), 320)
    rope = view(region(64), 64)
    ring_at = region(3 * 4096)
    ring = view(ring_at, 3 * 4096, "p (g n) -> p g n", g=3)
    scr = top[0]
    SCR = ARENA - scr

    def sv(at, n, pattern=None, **sizes):
        assert at + n <= SCR, (at + n, SCR)
        return view(scr + at, n, pattern, **sizes)

    ident = cst[:, C_ID:C_ID + P]
    SU, SL = cst[:, C_SU:C_SU + P], cst[:, C_SL:C_SL + P]
    UI, LI = cst[:, C_UI:C_UI + P], cst[:, C_LI:C_LI + P]
    blk = cst[:, C_BLK:C_BLK + P]
    iota = cst[:, C_IOTA:C_IOTA + P]
    ones = cst[:, C_ONE:C_ONE + P]

    filled = S("filled")
    BK = Banks(ps, [0, 1, 2, 3, 4, 5], filled, {"act": S("drained_act"), "dve": S("drained_dve")})

    chunks = []

    def chunk(name, src, cols, last):
        chunks.append((name, src, cols, last))

    for c in range(4):
        chunk(("mod", 0, c), a["mod_w"][0, c], 512, ("mod", 0, c))
    for c in range(6):
        n = min(4, 23 - 4 * c) * P
        last = 4 * c + n // P - 1
        key = ("pa", last) if last < NPA else ("pb", (last - NPA - 1) // 2 if (last - NPA) % 2 else (last - NPA) // 2)
        src = a["ev_in_w"][:, c * 4096:c * 4096 + 8 * n]
        chunk(("evin", c), src, n, key)
    for c in range(4, 12):
        chunk(("mod", 0, c), a["mod_w"][0, c], 512, ("mod", 0, c))
    for c in range(4):
        chunk(("mod", 1, c), a["mod_w"][1, c], 512, ("mod", 1, c))
    for c in range(4, 12):
        chunk(("mod", 1, c), a["mod_w"][1, c], 512, ("mod", 1, c))
    for c in range(2):
        chunk(("out", 0, c), a["ev_out_w"][c], 512, ("mix", 0, 1, c))
    FIRST_OF_1 = len(chunks)
    for c in range(6):
        chunk(("odin", c), a["od_in_w"][c], 512, ("qkv", 1, c))
    for c in range(2):
        chunk(("out", 1, c), a["od_out_w"][c], 512, ("mix", 1, 1, c))
    at_chunk = {name: i for i, (name, *_) in enumerate(chunks)}
    ring_ld = [S(f"ring_loaded{i}") for i in range(3)]

    def slot(name):
        i = at_chunk[name]
        cols = chunks[i][2]
        return ring[:, i % 3, 0:8 * cols].rearrange("p (k n) -> p k n", k=KT)

    def wait_chunk(pe, name):
        i = at_chunk[name]
        pe.wait_ge(ring_ld[i % 3], 16 * (i // 3 + 1))

    def load_chunk(sp, i):
        name, src, cols, _ = chunks[i]
        if i >= 3:
            BK.wait_filled(sp, chunks[i - 3][3])
        sp.dma_start(ring[:, i % 3, 0:8 * cols], src).then_inc(ring_ld[i % 3], 16)

    TAIL = [("mod", 0, c) for c in range(4, 12)] + [("mod", 1, c) for c in range(12)]

    def plan_mod(l, c):
        BK.add(("mod", l, c), "dve")
        if c % 2 and c // 2 not in (2, 5):
            BK.add(("modT", l, c // 2), "dve")

    def gate_slot(l, part):
        return {(0, 2): 0, (0, 5): 1, (1, 2): 2, (1, 5): 3}[(l, part)]

    for c in range(4):
        plan_mod(0, c)
    for s in range(NS):
        for h2 in range(2):
            BK.add(("xT", "m0", s, h2), "act" if h2 == 0 else "dve")
    LORA = 3
    for i in range(NPA):
        BK.add(("pa", i), "act")
    for t in range(AT):
        BK.add(("pb", t), "dve")
    for s in range(NS):
        for z in range(2):
            BK.add(("w", s, z), "dve")
    for tp in range(2):
        BK.add(("ss", tp), "dve")
    for z in range(2):
        for tp in range(2):
            BK.add(("a", z, tp), "act")
    for z in range(2):
        for t in range(AT):
            BK.add(("cum", z, t), "act")
    for s in range(NS):
        BK.add(("V", s), "act")
    BK.add("bonus", "dve")
    for c in range(4, 12):
        plan_mod(0, c)
    PAIRS = [(s, z) for s in range(NS) for z in range(2)]
    LEVELS = 7
    mod_between = {}
    slots_between = [(s, z, j) for (s, z) in PAIRS for j in (1, 3, 5)]
    for n, c in enumerate(range(12)):
        mod_between[slots_between[n]] = c
    for (s, z) in PAIRS:
        for g in range(2):
            for i in range(4):
                BK.add(("gram", s, z, g, i), "dve")
            BK.add(("L", s, z, g, 0), "dve")
        for g in range(2):
            BK.add(("B", s, z, g), "act")
        for j in range(LEVELS):
            for g in range(2):
                BK.add(("X", s, z, g, j), "dve")
                if j < LEVELS - 1:
                    BK.add(("L", s, z, g, j + 1), "act")
                    BK.add(("LT", s, z, g, j + 1), "dve")
            if (s, z, j) in mod_between:
                plan_mod(1, mod_between[(s, z, j)])
        if s == 0:
            for g in range(2):
                BK.add(("fT", z, g), "act")
                BK.add(("st", z, g), "act")
        if z == 1:
            BK.add(("g", s), "dve")
    for s in range(NS):
        BK.add(("cT", s), "dve")
    for s in range(NS):
        for n in range(2):
            BK.add(("gbc", 0, 0, s, n), "act")
    for s in range(NS):
        for h2 in range(2):
            BK.add(("oT", 0, s, h2), "act" if h2 == 0 else "dve")

    def plan_mix(l):
        for s in range(NS):
            for n in range(2):
                BK.add(("mix", l, s, n), "dve")

    def plan_moe(l):
        for s in range(NS):
            for h2 in range(2):
                BK.add(("xT", f"e{l}", s, h2), "act" if h2 == 0 else "dve")
        BK.add(("lg", l), "dve")
        for s in range(NS):
            for h2 in range(2):
                BK.add(("hb", l, s, h2), "act")
        for s in range(NS):
            for n in range(2):
                BK.add(("gbc", l, 1, s, n), "act")
        BK.add(("pos", l), "dve")
        BK.add(("base", l), "dve")
        BK.add(("eid", l), "dve")

    plan_mix(0)
    plan_moe(0)
    for s in range(NS):
        for h2 in range(2):
            BK.add(("xT", "m1", s, h2), "act" if h2 == 0 else "dve")
    for c in range(6):
        for s in range(NS):
            BK.add(("qkv", s, c), "act")
    for h2 in range(2):
        BK.add(("cT1", h2), "act")
    for s in range(NS):
        for q in range(2):
            for h2 in range(2):
                BK.add(("qkT", s, q, h2), "act")
    PAIRS1 = [(s, hp) for s in range(NS) for hp in range(H // 2)]
    for n in range(len(PAIRS1) + 1):
        if n < len(PAIRS1):
            for z in range(2):
                BK.add(("sc",) + PAIRS1[n] + (z,), "act")
        if n >= 1:
            BK.add(("aT",) + PAIRS1[n - 1], "act")
            if n % 2 == 0:
                BK.add(("pv", PAIRS1[n - 1][0], PAIRS1[n - 1][1] // 2), "dve")
    for s in range(NS):
        for n in range(2):
            BK.add(("gbc", 1, 0, s, n), "act")
    for s in range(NS):
        for h2 in range(2):
            BK.add(("oT", 1, s, h2), "act" if h2 == 0 else "dve")
    plan_mix(1)
    plan_moe(1)

    MOD_ORDER = [(k[1], k[2]) for k in BK.order if k[0] == "mod"]
    MODS = [("mod", l, c) for l, c in MOD_ORDER]
    assert MODS == [n for n, *_ in chunks if n[0] == "mod"]

    OPS = sv(0, 8192, "p (z t s c n) -> p z t s c n", z=2, t=AT, s=NS, c=4)
    wup, aup = sv(0, 512), sv(512, 512)
    lw = sv(1024, 2048, "p (s z n) -> p s z n", s=NS, z=2)
    raw = sv(3072, 4 * 260, "p (b s n) -> p b s n", b=4, s=NS)
    nbr = sv(4112, 512, "p (b n) -> p b n", b=2)
    eg = sv(4624, 512, "p (b n) -> p b n", b=2)
    sq = sv(5136, 1024)
    PA_at = 8192
    PA = sv(PA_at, 3840, "p (t n) -> p t n", t=NPA)
    K_, R_, V_ = PA[:, 3:7, :], PA[:, 7:11, :], PA[:, 11:15, :]
    cln = sv(PA_at + 768, 1024, "p (g n) -> p g n", g=2)
    gnp = sv(PA_at + 1792, 1024, "p (g n) -> p g n", g=2)
    fint = view(gbc_at + 1024, 1024, "p (t c n) -> p t c n", t=AT, c=2)
    finq = sv(PA_at + 2816, 1024, "p (g t c n) -> p g t c n", g=2, t=AT, c=2)
    OB = sv(12032, 1024, "p (s n) -> p s n", s=NS)
    VT = sv(13056, 1024, "p (s n) -> p s n", s=NS)
    PRE = 14080
    FG = sv(PRE, 4128, "p (f z t s n) -> p f z t s n", f=2, z=2, t=AT, s=NS)
    Ab = sv(PRE + 4128, 2048, "p (z t n) -> p z t n", z=2, t=AT)
    KZ = sv(PRE + 6176, 2048, "p (z t n) -> p z t n", z=2, t=AT)
    KK = sv(PRE + 8224, 1024, "p (t n) -> p t n", t=AT)
    MAT = sv(PRE, 4096, "p (g i c n) -> p g i c n", g=2, i=4, c=4)
    LS = sv(PRE + 4096, 2048, "p (g b i n) -> p g b i n", g=2, b=2, i=4)
    LT = sv(PRE + 6144, 2048, "p (g b i n) -> p g b i n", g=2, b=2, i=4)
    XS = sv(PRE + 8192, 1024, "p (g b n) -> p g b n", g=2, b=2)
    S0 = sv(PRE + 9248, 512, "p (z t n) -> p z t n", z=2, t=AT)
    STS = sv(PRE + 9760, 512, "p (b n) -> p b n", b=2)
    w0b = view(gbc_at, 1024, "p (z n) -> p z n", z=2)
    CONV = view(gbc_at, 1024, "p (t n) -> p t n", t=AT)
    prod = view(gbc_at + 1024, 1024, "p (t n) -> p t n", t=AT)
    yb, tb = view(gbc_at + 1024, 512), view(gbc_at + 1536, 512)
    glu = view(lnp_at, 1264, "p (t s n) -> p t s n", t=AT, s=NS)
    gup = view(lnp_at + 1264, 512)
    cb = small[:, 0:32].rearrange("p (g z t s) -> p g z t s", g=2, z=2, t=AT)
    bon = small[:, 32:48]
    fsc = small[:, 48:64].rearrange("p (z t s) -> p z t s", z=2, t=AT)
    st8 = small[:, 64:112]
    bns = small[:, 112:144]
    lns = small[:, 144:160]
    zl = sv(0, 2048, "p (s n) -> p s n", s=NS)

    QKV = sv(0, 6144, "p (s n) -> p s n", s=NS)
    QR = sv(6144, 2048, "p (q n) -> p q n", q=2)
    rt = sv(8192, 2048, "p (q n) -> p q n", q=4)
    QT = sv(10240, 2048, "p (s h n) -> p s h n", s=NS, h=H)
    KTp = sv(12288, 1024, "p (h n) -> p h n", h=H)
    KTs = sv(13312, 2048, "p (h n) -> p h n", h=H)
    CV = sv(15360, 1024)
    CK = sv(16384, 1024)
    PB = sv(17408, 2048, "p (b z m n) -> p b z m n", b=2, z=2, m=2)
    AB = sv(19456, 1024, "p (b m n) -> p b m n", b=2, m=2)
    ATb = sv(20480, 1024, "p (b n) -> p b n", b=2)
    OO = sv(21504, 2048, "p (s n) -> p s n", s=NS)
    t1k = sv(8192, 1024)
    subg = sv(23552, 128)
    lqk = sv(23680, 256, "p (g n) -> p g n", g=4)
    lam = small[:, 160:168]
    sm1 = small[:, 168:232].rearrange("p (n c) -> p n c", c=16)
    zl1 = sv(6144, 2048, "p (s n) -> p s n", s=NS)

    EW = sv(0, 4 * 6144, "p (b n) -> p b n", b=4)
    er = ring_at + 4096

    def ev(at, n, pattern=None, **sizes):
        assert at + n <= 8192
        return view(er + at, n, pattern, **sizes)

    hb = ev(0, 2048, "p (s n) -> p s n", s=NS)
    xg = ev(2048, 1024, "p (k n) -> p k n", k=KT)
    ysb = ev(3072, 1024)
    zm = ev(3072, 2048, "p (s n) -> p s n", s=NS)
    sel = ev(5120, 256, "p (s n) -> p s n", s=NS)
    gsel = ev(5376, 512, "p (c s n) -> p c s n", c=2, s=NS)
    hid = ev(5888, 512, "p (c n) -> p c n", c=2)
    tT = [ev(6400, 512), sv(24576, 512)]
    rw = ev(6912, 288, "p (k n) -> p k n", k=KT)
    rb = ev(7200, 36)
    rt_ = ev(7240, 952)
    R_LG, R_A, R_OHG, R_EX, R_T4, R_EIN, R_O1, R_O2, R_OH, R_NB, R_CMP, R_SL, R_ZERO, R_S, R_P1 = (
        0, 72, 80, 88, 96, 160, 176, 192, 208, 272, 400, 440, 504, 632, 696)
    R_P2, R_T = 760, 824


    block = ctx.enter_context(nc.Block())

    def norm_no(l, w, s):
        return (l * 2 + w) * 2 + s

    @block.sync
    def _(sp):
        sp.dma_start(cond, a["cond"]).then_inc(S("ld_cond"), 16)
        sp.dma_start(cst, a["cst"]).then_inc(S("ld_cst"), 16)
        for i in range(3):
            load_chunk(sp, i)
        sp.dma_start(x[:, 0, :], a["x_prompt"]).then_inc(S("ld_x"), 16)
        sp.dma_start(x[:, 1, :], a["x_sample"]).then_inc(S("ld_x"), 16)
        sp.dma_start(vec, a["vec"]).then_inc(S("ld_vec"), 16)
        sp.dma_start(wup, a["ev_w_up"]).then_inc(S("ld_up"), 16)
        sp.dma_start(aup, a["ev_a_up"]).then_inc(S("ld_up"), 16)
        sp.dma_start(gup, a["ev_g_up"]).then_inc(S("ld_up"), 16)
        sp.dma_start(S0, a["s0t"]).then_inc(S("ld_s0"), 16)
        for i in range(3, FIRST_OF_1):
            load_chunk(sp, i)
        for l in range(2):
            BK.wait_filled(sp, ("mix", l, 1, 1))
            sp.dma_start(rw, a["r_w"][l].rearrange("p (k n) -> p k n", k=KT)).then_inc(S("ld_rw"), 16)
            sp.wait_ge(S("x_new"), norm_no(l, 0, 1) + 1)
            sp.wait_ge(S(f"meta{l}"), 1)
            if l == 1:
                sp.wait_ge(S("cache_out"), 32)
            trips = sp.value_load(meta[0:1, l, 0:1], min_val=1, max_val=10)
            with sp.Fori(0, trips) as it:
                for u in range(2):
                    expert = [sp.value_load(meta[0:1, l, bass.ds(it * 4 + (2 * u + c + 4), 1)],
                                            min_val=0, max_val=NE - 1) for c in range(2)]
                    for part, (lo, hi), done, each in (("gate_up", (0, 4096), "gu_done", 1), ("down", (4096, 6144), "down", 2)):
                        sp.wait_ge(S(f"{done}{l}"), (it * 2 + (u + 1)) * each)
                        for c in range(2):
                            sp.dma_start(EW[:, 2 * u + c, lo:hi],
                                         a["w_exp"][l, bass.ds(expert[c], 1), :, lo:hi].rearrange("e p n -> p (e n)"))\
                                .then_inc(S(f"{part}_loaded{l}_{u}"), 16)
            if l == 0:
                sp.wait_ge(S("x_new"), norm_no(0, 1, 1) + 1)
                sp.dma_start(CK, a["cache_k"]).then_inc(S("ld_cache"), 16)
                sp.dma_start(CV, a["cache_v"]).then_inc(S("ld_cache"), 16)
                for i in range(FIRST_OF_1, len(chunks)):
                    load_chunk(sp, i)

    @block.gpsimd
    def _(pool):
        mb = 0

        def bias_load(l, c):
            nonlocal mb
            if mb >= 3:
                BK.wait_drained(pool, MODS[mb - 3])
            pool.dma_start(mbias[0:2, mb % 3, :], a["mod_b"][l:l + 1, c * 512:(c + 1) * 512]
                           .partition_broadcast(2)).then_inc(S(f"ld_mbias{mb % 3}"), 16)
            mb += 1

        pool.memset(raw, 0.0).then_inc(S("zeroed"), 1)
        pool.memset(glu, 0.0).then_inc(S("zeroed"), 1)
        pool.dma_start(w0b, a["ev_w0"].partition_broadcast(P)).then_inc(S("ld_w0"), 16)
        pool.dma_start(rope, a["rope"]).then_inc(S("ld_rope"), 16)
        for l, c in MOD_ORDER[:10]:
            bias_load(l, c)
        pool.wait_ge(S("ops"), 8)
        pool.wait_ge(S("prod"), 1)
        BK.wait_filled(pool, ("V", 1))
        pool.dma_start(cln, a["ev_cln"].partition_broadcast(P)).then_inc(S("ld_cln"), 16)
        pool.dma_start(gnp, a["ev_gn"].partition_broadcast(P)).then_inc(S("ld_gn"), 16)
        states = 0
        for l, c in MOD_ORDER[10:]:
            bias_load(l, c)
            while states < 4 and BK.no[("st", states // 2, states % 2)] < BK.no[("mod", l, c)]:
                z, g = states // 2, states % 2
                BK.wait_drained(pool, ("st", z, g))
                pool.dma_start(o["state"][z, g::2].rearrange("h v k -> v h k"),
                               STS[0:HD, states % 2, :].rearrange("v (h k) -> v h k", h=4))\
                    .then_inc(S("state_out"), 16)
                states += 1

        def ln_load(l, w):
            n = l * 2 + w
            if n == 0:
                pool.wait_ge(S("conv"), CONV_W * AT)
                BK.wait_drained(pool, ("g", 1))
            else:
                pool.wait_ge(S("x_new"), 2 * n)
            pool.dma_start(lnp, a["ln"][n].partition_broadcast(P)).then_inc(S("ld_ln"), 16)

        ln_load(0, 0)
        for l in range(2):
            BK.wait_filled(pool, ("mix", l, 1, 1))
            pool.dma_start(rb, a["r_b"][l].partition_broadcast(P)).then_inc(S("ld_rb"), 16)
            ln_load(l, 1)
            if l == 0:
                ln_load(1, 0)
                pool.dma_start(subg, a["subln"].partition_broadcast(P)).then_inc(S("ld_sub"), 16)
                pool.dma_start(lqk, a["lqk"].partition_broadcast(P)).then_inc(S("ld_sub"), 16)
                BK.wait_drained(pool, ("qkv", 0, 3))
                pool.dma_start(o["cache_k"], QKV[:, 0, D:2 * D]).then_inc(S("cache_out"), 16)
                BK.wait_drained(pool, ("qkv", 0, 5))
                pool.dma_start(o["cache_v"], QKV[:, 0, 2 * D:3 * D]).then_inc(S("cache_out"), 16)
        for s in range(NS):
            pool.wait_ge(S("x_new"), norm_no(1, 1, s) + 1)
            pool.dma_start(o["y"][s], x[:, s, :]).then_inc(S("y_out"), 16)
        pool.wait_ge(S("state_out"), 64)
        pool.wait_ge(S("cache_out"), 32)
        pool.wait_ge(S("y_out"), 32)

    @block.tensor
    def _(pe):
        def mod(l, c):
            key = ("mod", l, c)
            wait_chunk(pe, key)
            BK.wait_free(pe, key)
            w, bank = slot(key), BK.bank(key)
            for k in range(KT):
                mm = pe.matmul(bank[0:2, :], cond[:, k, :], w[:, k, :], start=(k == 0), stop=(k == KT - 1))
            mm.then_inc(filled, 1)
            if c % 2 and c // 2 not in (2, 5):
                tkey = ("modT", l, c // 2)
                BK.wait_free(pe, tkey)
                BK.wait_drained(pe, key)
                bank = BK.bank(tkey)
                for k in range(KT):
                    mm = pe.transpose(bank[:, 2 * k:2 * k + 2], rowbuf[0:2, k * P:(k + 1) * P], ident[0:2, 0:2])
                mm.then_inc(filled, 1)

        def transposes(key, tiles, wait=None):
            BK.wait_free(pe, key)
            bank = BK.bank(key)
            for n, t in enumerate(tiles):
                mm = pe.transpose(bank[:, n * P:(n + 1) * P], t, ident)
            mm.then_inc(filled, 1)

        def x_transposes(tag):
            for s in range(NS):
                for h2 in range(2):
                    transposes(("xT", tag, s, h2), [x[:, s, (4 * h2 + n) * P:(4 * h2 + n + 1) * P] for n in range(4)])

        def wait_hT(tag):
            for h2 in range(2):
                BK.wait_drained(pe, ("xT", tag, 1, h2))

        def gate_rows(l, w):
            part = 2 if w == 0 else 5
            for s in range(NS):
                for n in range(2):
                    key = ("gbc", l, w, s, n)
                    BK.wait_free(pe, key)
                    if s == 0:
                        BK.wait_drained(pe, ("mod", l, 2 * part + n))
                    q = 32 * gate_slot(l, part)
                    pe.matmul(BK.bank(key), cst[q:q + 2, C_SEL + s * P:C_SEL + (s + 1) * P],
                              gaterow[q:q + 2, n * 512:(n + 1) * 512],
                              start=True, stop=True).then_inc(filled, 1)

        def project_out(l):
            for s in range(NS):
                for h2 in range(2):
                    BK.wait_drained(pe, ("oT", l, s, h2))
                for n in range(2):
                    key = ("mix", l, s, n)
                    if s == 0:
                        wait_chunk(pe, ("out", l, n))
                    BK.wait_free(pe, key)
                    for k in range(KT):
                        mm = pe.matmul(BK.bank(key), hT[:, k, s * T:(s + 1) * T], slot(("out", l, n))[:, k, :],
                                       start=(k == 0), stop=(k == KT - 1))
                    mm.then_inc(filled, 1)

        pe.wait_ge(S("cond"), 1)
        pe.wait_ge(S("ld_cst"), 16)
        for c in range(4):
            mod(0, c)
        pe.wait_ge(S("ld_x"), 32)
        x_transposes("m0")
        wait_hT("m0")
        for i in range(NPA):
            key = ("pa", i)
            wait_chunk(pe, ("evin", i // 4))
            BK.wait_free(pe, key)
            for k in range(KT):
                mm = pe.matmul(BK.bank(key)[:, 0:256], slot(("evin", i // 4))[:, k, (i % 4) * P:(i % 4 + 1) * P],
                               hT[:, k, :], start=(k == 0), stop=(k == KT - 1))
            mm.then_inc(filled, 1)
        for t in range(AT):
            key = ("pb", t)
            BK.wait_free(pe, key)
            for half in range(2):
                i = NPA + 2 * t + half
                wait_chunk(pe, ("evin", i // 4))
                for k in range(KT):
                    mm = pe.matmul(BK.bank(key)[:, half * 256:half * 256 + 256],
                                   slot(("evin", i // 4))[:, k, (i % 4) * P:(i % 4 + 1) * P],
                                   hT[:, k, :], start=(k == 0), stop=(k == KT - 1))
            mm.then_inc(filled, 1)

        pe.wait_ge(S("ld_up"), 48)
        pe.wait_ge(S("lora"), 1)
        for s in range(NS):
            for z in range(2):
                key = ("w", s, z)
                BK.wait_free(pe, key)
                pe.matmul(BK.bank(key), PA[64 * z:64 * z + 64, 0, s * T:(s + 1) * T], wup[64 * z:64 * z + 64, :],
                          start=True, stop=True).then_inc(filled, 1)
        pe.wait_ge(S("sq"), 1)
        for tp in range(2):
            key = ("ss", tp)
            BK.wait_free(pe, key)
            pe.matmul(BK.bank(key), blk, sq[:, tp * 512:(tp + 1) * 512], start=True, stop=True).then_inc(filled, 1)
        for z in range(2):
            for tp in range(2):
                key = ("a", z, tp)
                BK.wait_free(pe, key)
                for t2 in range(2):
                    t = 2 * tp + t2
                    mm = pe.matmul(BK.bank(key)[:, t2 * 256:t2 * 256 + 256], aup[64 * z:64 * z + 64, t * P:(t + 1) * P],
                                   PA[64 * z:64 * z + 64, 1, :], start=True, stop=True)
                mm.then_inc(filled, 1)
        pe.wait_ge(S("sigw"), 4)
        for z in range(2):
            for t in range(AT):
                key = ("cum", z, t)
                BK.wait_free(pe, key)
                for s in range(NS):
                    mm = pe.matmul(BK.bank(key)[:, s * 130:s * 130 + 129], lw[:, s, z, t * P:(t + 1) * P],
                                   cst[:, C_CUM:C_CUM + T + 1], start=True, stop=True)
                mm.then_inc(filled, 1)
        pe.wait_ge(S("shifted"), NPA)
        for s in range(NS):
            transposes(("V", s), [V_[:, t, s * T:(s + 1) * T] for t in range(AT)])
        BK.wait_free(pe, "bonus")
        pe.wait_ge(S("prod"), 1)
        for s in range(NS):
            for t in range(AT):
                mm = pe.matmul(BK.bank("bonus")[:, s * 8:s * 8 + 8], prod[:, t, s * T:(s + 1) * T],
                               cst[:, C_HSEL + t * H:C_HSEL + (t + 1) * H], start=(t == 0), stop=(t == AT - 1))
        mm.then_inc(filled, 1)
        for c in range(4, 12):
            mod(0, c)

        for (s, z) in PAIRS:
            pe.wait_ge(S("ops"), 4 * z + 4)
            for g in range(2):
                for i in range(4):
                    t, b = i, 64 * g
                    key = ("gram", s, z, g, i)
                    BK.wait_free(pe, key)
                    bank, op = BK.bank(key), OPS[b:b + 64, z, t, s]
                    pe.matmul(bank[:, 0:256], op[:, 2, :], op[:, 0:2, :], start=True, stop=True)
                    pe.matmul(bank[:, 256:512], op[:, 3, :], op[:, 0:2, :], start=True, stop=True)\
                        .then_inc(filled, 1)
                key = ("L", s, z, g, 0)
                BK.wait_free(pe, key)
                for i in range(4):
                    t, b = i, 64 * g
                    op = OPS[b:b + 64, z, t, s]
                    mm = pe.matmul(BK.bank(key)[:, i * P:(i + 1) * P], op[:, 0, :], op[:, 2, :], start=True, stop=True)
                mm.then_inc(filled, 1)
            if s == 0 and z == 0:
                BK.wait_drained(pe, ("V", 1))
            if s == 1 and z == 0:
                pe.wait_ge(S("s0"), 1)
            for g in range(2):
                key = ("B", s, z, g)
                BK.wait_free(pe, key)
                BK.wait_drained(pe, ("gram", s, z, g, 3))
                for i in range(4):
                    h, t, b = 2 * i + g, i, 64 * g
                    dst = BK.bank(key)[:, i * HD:(i + 1) * HD]
                    mm = pe.matmul(dst, MAT[:, g, i, 2, :], VT[:, s, h * HD:(h + 1) * HD], start=True, stop=(s == 0))
                    if s == 1:
                        mm = pe.matmul(dst, OPS[b:b + 64, z, t, s, 0, :], S0[b:b + 64, z, t, :], start=False, stop=True)
                mm.then_inc(filled, 1)
            for j in range(LEVELS):
                for g in range(2):
                    lt = [MAT[:, g, i, 0, :] if j == 0 else LT[:, g, j % 2, i, :] for i in range(4)]
                    if j == 0:
                        BK.wait_drained(pe, ("B", s, z, g))
                        BK.wait_drained(pe, ("L", s, z, g, 0))
                    else:
                        BK.wait_drained(pe, ("LT", s, z, g, j))
                        BK.wait_drained(pe, ("X", s, z, g, j - 1))
                    key = ("X", s, z, g, j)
                    BK.wait_free(pe, key)
                    for i in range(4):
                        mm = pe.matmul(BK.bank(key)[:, i * HD:(i + 1) * HD], lt[i], XS[:, g, j % 2, i * HD:(i + 1) * HD],
                                       start=True, stop=True)
                    mm.then_inc(filled, 1)
                    if j < LEVELS - 1:
                        if j:
                            BK.wait_drained(pe, ("L", s, z, g, j))
                        key = ("L", s, z, g, j + 1)
                        BK.wait_free(pe, key)
                        for i in range(4):
                            mm = pe.matmul(BK.bank(key)[:, i * P:(i + 1) * P], lt[i], LS[:, g, j % 2, i, :],
                                           start=True, stop=True)
                        mm.then_inc(filled, 1)
                        key = ("LT", s, z, g, j + 1)
                        BK.wait_free(pe, key)
                        for i in range(4):
                            mm = pe.matmul(BK.bank(key)[:, i * P:(i + 1) * P], LS[:, g, j % 2, i, :], lt[i],
                                           start=True, stop=True)
                        mm.then_inc(filled, 1)
                if (s, z, j) in mod_between:
                    mod(1, mod_between[(s, z, j)])
            for g in range(2):
                BK.wait_drained(pe, ("X", s, z, g, LEVELS - 1))
                if s == 1 and (z or g):
                    pe.wait_ge(S("y_even"), z + 1) if g else pe.wait_ge(S("y_done"), 3)
                for i in range(4):
                    h, t, b = 2 * i + g, i, 64 * g
                    dst = ps[:, 6 + s, h * HD:(h + 1) * HD]
                    pe.matmul(dst, MAT[:, g, i, 1, :], XS[:, g, LEVELS % 2, i * HD:(i + 1) * HD],
                              start=(z == 0 and h == 0), stop=False, skip_group_check=True)
                    mm = pe.matmul(dst, MAT[:, g, i, 3, :], VT[:, s, h * HD:(h + 1) * HD],
                                   start=False, stop=(s == 0 and z == 1), skip_group_check=True)
                    if s == 1:
                        mm = pe.matmul(dst, OPS[b:b + 64, z, t, s, 1, :], S0[b:b + 64, z, t, :],
                                       start=False, stop=(z == 1), skip_group_check=True)
                if s == 1 and g == 0:
                    mm.then_inc(S("y_even"), 1)
            mm.then_inc(S("y_done"), 1)
            if s == 0:
                pe.wait_ge(S("fin"), z + 1)
                for g in range(2):
                    b = 64 * g
                    key = ("fT", z, g)
                    BK.wait_free(pe, key)
                    for i in range(4):
                        for c in range(2):
                            mm = pe.transpose(BK.bank(key)[:, (2 * i + c) * HD:(2 * i + c + 1) * HD],
                                              fint[b:b + 64, i, c, :], ident[b:b + 64, b:b + 64])
                    mm.then_inc(filled, 1)
                    key = ("st", z, g)
                    BK.wait_free(pe, key)
                    BK.wait_drained(pe, ("fT", z, g))
                    for i in range(4):
                        h, dst = 2 * i + g, BK.bank(key)[0:HD, i * HD:(i + 1) * HD]
                        pe.matmul(dst, XS[:, g, LEVELS % 2, i * HD:(i + 1) * HD], finq[:, g, i, 0, :],
                                  start=True, stop=False)
                        mm = pe.matmul(dst, VT[:, s, h * HD:(h + 1) * HD], finq[:, g, i, 1, :],
                                       start=False, stop=True)
                    mm.then_inc(filled, 1)
            if z == 1:
                key = ("g", s)
                BK.wait_free(pe, key)
                pe.wait_ge(S("lora"), 2)
                pe.matmul(BK.bank(key), PA[:, 2, s * T:(s + 1) * T], gup, start=True, stop=True).then_inc(filled, 1)

        for s in range(NS):
            pe.wait_ge(S("conv"), CONV_W * AT)
            transposes(("cT", s), [CONV[:, t, s * T:(s + 1) * T] for t in range(AT)])
        gate_rows(0, 0)
        for s in range(NS):
            for h2 in range(2):
                pe.wait_ge(S("mixed_a" if h2 == 0 else "mixed_b"), s + 1)
                src = VT if h2 == 0 else OB
                transposes(("oT", 0, s, h2), [src[:, s, t * P:(t + 1) * P] for t in range(AT)])
        project_out(0)

        def moe(l):
            for s in range(NS):
                pe.wait_ge(S("x_new"), norm_no(l, 0, s) + 1)
                for h2 in range(2):
                    transposes(("xT", f"e{l}", s, h2), [x[:, s, (4 * h2 + n) * P:(4 * h2 + n + 1) * P] for n in range(4)])
            wait_hT(f"e{l}")
            key = ("lg", l)
            BK.wait_free(pe, key)
            pe.wait_ge(S("ld_rw"), 16 * (l + 1))
            for s in range(NS):
                for k in range(KT):
                    mm = pe.matmul(BK.bank(key)[:, s * 64:s * 64 + 36], hT[:, k, s * T:(s + 1) * T], rw[:, k, :],
                                   start=(k == 0), stop=(k == KT - 1))
            mm.then_inc(filled, 1)
            for s in range(NS):
                for h2 in range(2):
                    transposes(("hb", l, s, h2), [hT[:, 4 * h2 + n, s * T:(s + 1) * T] for n in range(4)])
            gate_rows(l, 1)
            key = ("pos", l)
            BK.wait_free(pe, key)
            pe.wait_ge(S("chosen"), l + 1)
            bank, OH = BK.bank(key), rt_[:, R_OH:R_OH + 64]
            pe.matmul(bank[:, 0:32], SU, OH[:, 0:32], start=True, stop=True)
            pe.matmul(bank[:, 32:64], SU, OH[:, 32:64], start=True, stop=False)
            pe.matmul(bank[:, 32:64], ones, OH[:, 0:32], start=False, stop=True)
            pe.matmul(bank[0:32, 64:65], OH[:, 0:32], ones[:, 0:1], start=True, stop=False)
            pe.matmul(bank[0:32, 64:65], OH[:, 32:64], ones[:, 0:1], start=False, stop=True).then_inc(filled, 1)
            key = ("base", l)
            BK.wait_free(pe, key)
            pe.wait_ge(S("nchunks"), l + 1)
            bank, nb = BK.bank(key), rt_[0:32, R_NB:R_NB + P]
            pe.matmul(bank[:, 0:32], nb, SU[0:32, 0:32], start=True, stop=True)
            pe.matmul(bank[:, 32:33], nb, ones[0:32, 0:1], start=True, stop=True)
            pe.matmul(bank[0:32, 64:65], UI[0:32, 0:32], nb[:, 0:1], start=True, stop=True).then_inc(filled, 1)
            key = ("eid", l)
            BK.wait_free(pe, key)
            pe.wait_ge(S("ended"), l + 1)
            pe.matmul(BK.bank(key)[0:1, 0:40], ones[0:32, 0:1], rt_[0:32, R_CMP:R_CMP + 40], start=True, stop=True)\
                .then_inc(filled, 1)
            BK.wait_drained(pe, ("eid", l))
            BK.wait_drained(pe, ("gbc", l, 1, 1, 1))
            pe.wait_ge(S("zero"), l + 1)
            for n in range(4):
                mm = pe.matmul(ps[:, n, :], rt_[:, R_ZERO:R_ZERO + P], cst[:, 0:512], start=True, stop=False,
                               skip_group_check=True)
                if n == 0:
                    mm.then_inc(S(f"gu_done{l}"), 2)
                elif n == 1:
                    mm.then_inc(S(f"down{l}"), 4)

            def gather(n):
                pe.wait_ge(S(f"selected{l}"), n + 1)
                for k in range(KT):
                    for s in range(NS):
                        mm = pe.matmul(ps[:, 4 + k // 4, (k % 4) * P:(k % 4 + 1) * P], hb[:, s, k * P:(k + 1) * P],
                                       sel[:, s, :], start=(s == 0), stop=(s == 1))
                    if k % 4 == 3:
                        mm.then_inc(S(f"gathered{l}"), 1)

            def scatter(n, u, last=False):
                pe.wait_ge(S(f"y_read{l}"), n + 2)
                pe.wait_ge(S(f"y_read_dve{l}"), n + 2)
                for s in range(NS):
                    for half in range(2):
                        mm = pe.matmul(ps[:, 2 * s + half, :], tT[u][:, (2 + s) * P:(3 + s) * P],
                                       ysb[:, half * 512:(half + 1) * 512], start=False, stop=last,
                                       skip_group_check=True)
                return mm

            gather(0)
            pe.wait_ge(S(f"meta{l}"), 1)
            trips = pe.value_load(meta[0:1, l, 0:1], min_val=1, max_val=10)
            with pe.Fori(0, trips) as it:
                for u in range(2):
                    n = it * 2 + u
                    pe.wait_ge(S(f"xg_act{l}"), n + 1)
                    pe.wait_ge(S(f"xg_dve{l}"), n + 1)
                    pe.wait_ge(S(f"gate_up_loaded{l}_{u}"), it * 32 + 32)
                    for k in range(KT):
                        for c in range(2):
                            mm = pe.matmul(ps[64 * c:64 * c + 64, 6, :], xg[:, k, 64 * c:64 * c + 64],
                                           EW[:, 2 * u + c, k * 512:(k + 1) * 512],
                                           start=(k == 0), stop=(k == KT - 1), skip_group_check=True)
                    mm.then_inc(S(f"gu_done{l}"), 1)
                    pe.wait_ge(S(f"y_read{l}"), n + 1)
                    pe.wait_ge(S(f"y_read_dve{l}"), n + 1)
                    gather(n + 1)
                    pe.wait_ge(S(f"gates{l}"), n + 1)
                    for s in range(NS):
                        pe.transpose(ps[:, 7, (2 + s) * P:(3 + s) * P], gsel[:, 0, s, :], ident)
                    pe.wait_ge(S(f"hid{l}"), n + 1)
                    for f in range(2):
                        mm = pe.transpose(ps[:, 7, f * P:(f + 1) * P], hid[:, 1, f * P:(f + 1) * P], ident)
                    mm.then_inc(S(f"turned{l}"), 1)
                    scatter(n - 1, 1 - u)
                    pe.wait_ge(S(f"tT{l}"), n + 1)
                    pe.wait_ge(S(f"xg_act{l}"), n + 2)
                    pe.wait_ge(S(f"xg_dve{l}"), n + 2)
                    pe.wait_ge(S(f"down_loaded{l}_{u}"), it * 32 + 32)
                    for half in range(2):
                        for f in range(2):
                            for c in range(2):
                                w = EW[:, 2 * u + c, 4096 + f * D + half * 512:4096 + f * D + half * 512 + 512]
                                mm = pe.matmul(ps[64 * c:64 * c + 64, 4 + half, :],
                                               tT[u][:, f * P + 64 * c:f * P + 64 * c + 64], w,
                                               start=(f == 0), stop=(f == 1), skip_group_check=True)
                        mm.then_inc(S(f"down{l}"), 1)
            scatter(trips * 2 - 1, 1, last=True).then_inc(S("summed"), 1)

        moe(0)

        for s in range(NS):
            pe.wait_ge(S("x_new"), norm_no(0, 1, s) + 1)
            for h2 in range(2):
                transposes(("xT", "m1", s, h2), [x[:, s, (4 * h2 + n) * P:(4 * h2 + n + 1) * P] for n in range(4)])
        wait_hT("m1")
        for c in range(6):
            wait_chunk(pe, ("odin", c))
            for s in range(NS):
                key = ("qkv", s, c)
                BK.wait_free(pe, key)
                for k in range(KT):
                    mm = pe.matmul(BK.bank(key), hT[:, k, s * T:(s + 1) * T], slot(("odin", c))[:, k, :],
                                   start=(k == 0), stop=(k == KT - 1))
                mm.then_inc(filled, 1)
        pe.wait_ge(S("ld_cache"), 32)
        for h2 in range(2):
            transposes(("cT1", h2), [CK[:, (4 * h2 + n) * P:(4 * h2 + n + 1) * P] for n in range(4)])
        for s in range(NS):
            for q in range(2):
                if s == 0:
                    BK.wait_drained(pe, ("qkv", 0, 2 * q + 1))
                else:
                    pe.wait_ge(S("roped"), q + 1)
                src = QKV[:, 0, q * D:(q + 1) * D] if s == 0 else QR[:, q, :]
                for h2 in range(2):
                    transposes(("qkT", s, q, h2), [src[:, (4 * h2 + n) * P:(4 * h2 + n + 1) * P] for n in range(4)])
        for n in range(len(PAIRS1) + 1):
            if n < len(PAIRS1):
                s, hp = PAIRS1[n]
                BK.wait_drained(pe, ("qkT", s, 1, hp // 2))
                for z in range(2):
                    key = ("sc", s, hp, z)
                    BK.wait_free(pe, key)
                    for m in range(2):
                        h = 2 * hp + m
                        keys = KTp[64 * z:64 * z + 64, h, :] if s == 0 else KTs[64 * z:64 * z + 64, h, :]
                        mm = pe.matmul(BK.bank(key)[:, m * 256:m * 256 + T * (s + 1)], QT[64 * z:64 * z + 64, s, h, :],
                                       keys, start=True, stop=True)
                    mm.then_inc(filled, 1)
            if n >= 1:
                s, hp = PAIRS1[n - 1]
                b = (n - 1) % 2
                pe.wait_ge(S("attn"), 2 * n)
                transposes(("aT", s, hp), [AB[:, b, m, i * P:(i + 1) * P] for m in range(2) for i in range(s + 1)])
                if n % 2 == 0:
                    key = ("pv", s, hp // 2)
                    BK.wait_free(pe, key)
                    BK.wait_drained(pe, ("aT", s, hp))
                    for m in range(4):
                        hh = 2 * hp - 2 + m
                        for i in range(s + 1):
                            own_v = QKV[:, s, 2 * D + hh * P:2 * D + (hh + 1) * P]
                            vals = CV[:, hh * P:(hh + 1) * P] if (s, i) == (1, 0) else own_v
                            at = (m % 2) * (s + 1) + i
                            mm = pe.matmul(BK.bank(key)[:, m * P:(m + 1) * P], ATb[:, m // 2, at * P:(at + 1) * P], vals,
                                           start=(i == 0), stop=(i == s))
                    mm.then_inc(filled, 1)
        gate_rows(1, 0)
        for s in range(NS):
            pe.wait_ge(S("attended"), s + 1)
            for h2 in range(2):
                transposes(("oT", 1, s, h2), [OO[:, s, (4 * h2 + n) * P:(4 * h2 + n + 1) * P] for n in range(4)])
        project_out(1)
        moe(1)


    @block.scalar
    def _(act):
        A = nc.scalar.activation
        own = Steps(act, S("act_steps"))

        def take(key):
            BK.wait_filled(act, key)
            return BK.bank(key)

        def copy(key, out, n=512):
            BK.drained_by(A(out, take(key)[:, 0:n], ACT.Copy), key)

        def modulated(key, s, k0, l, part):
            bank = take(key)
            BK.wait_drained(act, ("modT", l, part + 1))
            for n in range(4):
                k = k0 + n
                ins = A(hT[:, k, s * T:(s + 1) * T], bank[:, n * P:(n + 1) * P], ACT.Identity,
                        bias=modT[:, l, part, k, s:s + 1], scale=modT[:, l, part + 1, k, s:s + 1])
            BK.drained_by(ins, key)

        def rsqrt(out, src, ready, n, done):
            act.wait_ge(S(ready), n)
            own.link(A(out, src, ACT.Ln))
            A(out, out, ACT.Exp, scale=-0.5).then_inc(S(done), 1)

        def gate_rows(l, w):
            for s in range(NS):
                for n in range(2):
                    if s == 0 and n == 0 and w == 0 and l == 0:
                        act.wait_ge(S("convT"), 2)
                        act.wait_ge(S("mixed_a"), 2)
                    copy(("gbc", l, w, s, n), gbc[:, s, n * 512:(n + 1) * 512])

        act.wait_ge(S("ld_cond"), 16)
        A(condw[:, 0:16], cond.rearrange("p k s -> p (k s)"), ACT.Exp, scale=-1.0).then_inc(S("cond_exp"), 1)
        for s in range(NS):
            modulated(("xT", "m0", s, 0), s, 0, 0, 0)
        act.wait_ge(S("zeroed"), 1)
        act.wait_ge(S("vecs"), 1)
        for i in range(NPA):
            key = ("pa", i)
            bank = take(key)
            if i >= 4:
                act.wait_ge(S("shifted"), i - 3)
            A(raw[:, i % 4, :, 1:129], bank[:, 0:256].rearrange("p (s n) -> p s n", s=NS), ACT.Copy)\
                .then_inc(S("act_raw"), 1)
            BK.drained_by(A(PA[:, i, :], bank[:, 0:256], ACT.Copy, scale=nvec[:, TILES[i]:TILES[i] + 1]), key)
            if i == 4:
                act.wait_ge(S("shifted"), 1)
                A(PA[:, 0, :], PA[:, 0, :], ACT.Exp, scale=-2.0).then_inc(S("lora_exp"), 1)
                act.wait_ge(S("shifted"), 3)
                A(PA[:, 2, :], PA[:, 2, :], ACT.Exp, scale=-1.0).then_inc(S("lora_exp"), 1)
            if i == 10:
                act.wait_ge(S("kk"), 1)
                A(sq, KK.rearrange("p t n -> p (t n)"), ACT.Square).then_inc(S("sq"), 1)
        for t in range(AT):
            bank = take(("pb", t))
            if t >= 2:
                BK.wait_drained(act, ("pb", t - 2))
            A(eg[:, t % 2, :], bank[:, 256:512], ACT.Exp, bias=nvec[:, 38 + 4 + t:39 + 4 + t], scale=-1.0)\
                .then_inc(S("eg"), 1)
        for n, (s, z) in enumerate([(s, z) for s in range(NS) for z in range(2)]):
            BK.wait_drained(act, ("w", s, z))
            A(lw[:, s, z, :], lw[:, s, z, :], ACT.Exp, scale=-1.0).then_inc(S("lw_exp"), 1)
        BK.wait_drained(act, ("ss", 1))
        own.link(A(sq, sq, ACT.Ln, scale=float(2 ** 32)))
        A(sq, sq, ACT.Exp, scale=-0.5).then_inc(S("rs"), 1)
        for z in range(2):
            for tp in range(2):
                bank = take(("a", z, tp))
                for t2 in range(2):
                    t = 2 * tp + t2
                    ins = A(Ab[:, z, t, :], bank[:, t2 * 256:t2 * 256 + 256], ACT.Exp,
                            bias=nvec[:, 30 + 4 * z + t:31 + 4 * z + t], scale=-1.0)
                BK.drained_by(ins, ("a", z, tp))
        n = 0
        for z in range(2):
            for t in range(AT):
                n += 1
                bank = take(("cum", z, t))
                act.wait_ge(S("centres"), n)
                for s in range(NS):
                    A(FG[:, 0, z, t, s, :], bank[:, s * 130:s * 130 + 129], ACT.Exp, bias=cb[:, 0, z, t, s:s + 1])\
                        .then_inc(S("act_steps"), 1)
                    own.n += 1
                    ins = A(FG[:, 1, z, t, s, :], bank[:, s * 130:s * 130 + 129], ACT.Exp,
                            bias=cb[:, 1, z, t, s:s + 1], scale=-1.0)
                    if s == 0:
                        own.inc(ins)
                BK.drained_by(ins, ("cum", z, t))
        act.wait_ge(S("sigw"), 4)
        for s in range(NS):
            copy(("V", s), VT[:, s, :])

        for (s, z) in PAIRS:
            for g in range(2):
                copy(("B", s, z, g), XS[:, g, 0, :], 256)
            for j in range(LEVELS - 1):
                for g in range(2):
                    copy(("L", s, z, g, j + 1), LS[:, g, (j + 1) % 2].rearrange("p i n -> p (i n)"))
            if s == 0:
                for g in range(2):
                    copy(("fT", z, g), finq[:, g].rearrange("p t c n -> p (t c n)"))
                    key = ("st", z, g)
                    bank = take(key)
                    if z == 1:
                        act.wait_ge(S("state_out"), 16 * (g + 1)) if g == 1 else act.wait_ge(S("state_out"), 16)
                    if z == 1 and g == 0:
                        act.wait_ge(S("state_out"), 32)
                    BK.drained_by(A(STS[0:HD, g, :], bank[0:HD, 0:256], ACT.Copy), key)
            if z == 1:
                rsqrt(st8[:, 16:24], st8[:, 8:16], "gn_var", s + 1, "gn_rstd")
        for s in range(NS):
            rsqrt(st8[:, 32 + s:33 + s], st8[:, 34 + s:35 + s], "cln_var", s + 1, "cln_rstd")
            act.wait_ge(S("cln_y"), s + 1)
            A(tb, tb, ACT.Exp, scale=-1.0).then_inc(S("cln_exp"), 1)

        def norm_rsqrt(l, w, s):
            n = norm_no(l, w, s)
            rsqrt(lns[:, 8 + s:9 + s], lns[:, 4 + s:5 + s], "ln_var", n + 1, "ln_rstd")

        gate_rows(0, 0)
        for s in range(NS):
            copy3(act, BK, ("oT", 0, s, 0), hT, s, 0)
        for s in range(NS):
            norm_rsqrt(0, 0, s)

        def moe(l):
            for s in range(NS):
                modulated(("xT", f"e{l}", s, 0), s, 0, l, 3)
            act.wait_ge(S("routed1"), l + 1)
            A(rt_[:, R_EX:R_EX + 8], rt_[:, R_EX:R_EX + 8], ACT.Exp).then_inc(S("route_exp"), 1)
            for s in range(NS):
                for h2 in range(2):
                    copy(("hb", l, s, h2), hb[:, s, h2 * 512:(h2 + 1) * 512])
            act.wait_ge(S("routed2"), l + 1)
            A(rt_[:, R_S + 16:R_S + 18], rt_[:, R_S + 16:R_S + 18], ACT.Exp).then_inc(S("route_exp"), 1)
            gate_rows(l, 1)
            act.wait_ge(S(f"meta{l}"), 1)
            trips = act.value_load(meta[0:1, l, 0:1], min_val=1, max_val=10)
            act.sem_inc(S(f"y_read{l}"), 1)

            def gathered(n):
                act.wait_ge(S(f"gathered{l}"), n * 2 + 1)
                A(xg[:, 0:4, :].rearrange("p k n -> p (k n)"), ps[:, 4, :], ACT.Copy).then_inc(S(f"xg_act{l}"), 1)

            gathered(0)
            with act.Fori(0, trips) as it:
                for u in range(2):
                    n = it * 2 + u
                    act.wait_ge(S(f"gu_done{l}"), n + 3)
                    A(hid[:, 0, :], ps[:, 6, 0:256], ACT.Exp, scale=-1.0).then_inc(S(f"gate_exp{l}"), 1)
                    gathered(n + 1)
                    act.wait_ge(S(f"turned{l}"), n + 1)
                    A(tT[u], ps[:, 7, :], ACT.Copy).then_inc(S(f"tT{l}"), 1)
                    act.wait_ge(S(f"down{l}"), n * 2 + 5)
                    A(ysb[:, 0:512], ps[:, 4, :], ACT.Copy).then_inc(S(f"y_read{l}"), 1)
            for s in range(NS):
                norm_rsqrt(l, 1, s)

        moe(0)

        for s in range(NS):
            modulated(("xT", "m1", s, 0), s, 0, 1, 0)
        for c in range(6):
            for s in range(NS):
                copy(("qkv", s, c), QKV[:, s, c * 512:(c + 1) * 512])
        act.wait_ge(S("lam_dot"), 1)
        A(lam[:, 2:4], lam[:, 0:2], ACT.Exp).then_inc(S("lam_exp"), 1)

        def keys_out(key, dst):
            BK.drained_by(A(dst, take(key).rearrange("p (h n) -> p h n", h=4), ACT.Copy), key)

        for h2 in range(2):
            keys_out(("cT1", h2), KTs[:, 4 * h2:4 * h2 + 4, 0:P])
        for s in range(NS):
            for q in range(2):
                for h2 in range(2):
                    hs = slice(4 * h2, 4 * h2 + 4)
                    dst = QT[:, s, hs, :] if q == 0 else (KTp[:, hs, :] if s == 0 else KTs[:, hs, P:2 * P])
                    keys_out(("qkT", s, q, h2), dst)
        for n in range(len(PAIRS1) + 1):
            if n < len(PAIRS1):
                s, hp = PAIRS1[n]
                nk = T * (s + 1)
                for z in range(2):
                    bank = take(("sc", s, hp, z))
                    act.wait_ge(S("smax"), 2 * n + z + 1)
                    if n >= 2:
                        act.wait_ge(S("attn"), 2 * n - 2)
                    for m in range(2):
                        ins = A(PB[:, n % 2, z, m, 0:nk], bank[:, m * 256:m * 256 + nk], ACT.Exp,
                                bias=sm1[:, n % 4, 4 + 2 * z + m:5 + 2 * z + m], scale=HD ** -0.5,
                                accum_out=sm1[:, n % 4, 8 + 2 * z + m:9 + 2 * z + m])
                        if m == 0:
                            own.inc(ins)
                    BK.drained_by(ins, ("sc", s, hp, z))
            if n >= 1:
                s, hp = PAIRS1[n - 1]
                b = (n - 1) % 2
                if n >= 3:
                    BK.wait_filled(act, ("pv", PAIRS1[n - 3][0], PAIRS1[n - 3][1] // 2))
                w = 2 * T * (s + 1)
                BK.drained_by(A(ATb[:, b, 0:w], take(("aT", s, hp))[:, 0:w], ACT.Copy), ("aT", s, hp))
        gate_rows(1, 0)
        for s in range(NS):
            rsqrt(st8[:, 16:24], st8[:, 8:16], "at_var", s + 1, "at_rstd")
            copy3(act, BK, ("oT", 1, s, 0), hT, s, 0)
        for s in range(NS):
            norm_rsqrt(1, 0, s)
        moe(1)

    @block.vector
    def _(dve):
        V = nc.vector
        TT, TS, STT = V.tensor_tensor, V.tensor_scalar, V.scalar_tensor_tensor
        own = Steps(dve, S("dve_steps"))
        mods = [0]

        def take(key):
            BK.wait_filled(dve, key)
            return BK.bank(key)

        def sig(ins, name):
            ins.then_inc(S(name), 1)

        def mod(l, c):
            n = mods[0]
            mods[0] += 1
            part, half = c // 2, c % 2
            bank = take(("mod", l, c))
            dve.wait_ge(S(f"ld_mbias{n % 3}"), 16 * (n // 3 + 1))
            if part in (2, 5):
                q = 32 * gate_slot(l, part)
                dst = gaterow[q:q + 2, half * 512:half * 512 + 512]
            else:
                dst = rowbuf[0:2, half * 512:half * 512 + 512]
            BK.drained_by(TT(dst, bank[0:2, :], mbias[0:2, n % 3, :], ALU.add), ("mod", l, c))
            if half and part not in (2, 5):
                key = ("modT", l, part)
                src = take(key)[:, 0:16]
                dst = modT[:, l, part].rearrange("p k s -> p (k s)")
                BK.drained_by(TS(dst, src, 1.0 if part in (1, 4) else 0.0, None, ALU.add), key)

        def modulated(key, s, k0, l, part):
            bank = take(key)
            BK.wait_drained(dve, ("modT", l, part + 1))
            for n in range(4):
                k = k0 + n
                ins = TS(hT[:, k, s * T:(s + 1) * T], bank[:, n * P:(n + 1) * P], modT[:, l, part + 1, k, s:s + 1],
                         modT[:, l, part, k, s:s + 1], ALU.mult, ALU.add)
            BK.drained_by(ins, key)

        def layer_norm(l, w, s, z, src):
            n = norm_no(l, w, s)
            if n == 0 or s == 0:
                BK.wait_drained(dve, ("gbc", l, w, 1, 1))
            for half in range(2):
                ins = TT(z[:, s, half * 512:(half + 1) * 512], gbc[:, s, half * 512:(half + 1) * 512], src(half), ALU.mult)
                if w == 0:
                    BK.drained_by(ins, ("mix", l, s, half))
                    BK.wait_drained(dve, ("mix", l, s, half))
                else:
                    own.link(ins)
            own.link(STT(z[:, s, :], x[:, s, :], ALPHA, z[:, s, :], ALU.mult, ALU.add))
            for half in range(2):
                own.inc(V.bn_stats(bns[:, half * 6:half * 6 + 6], z[:, s, half * 512:(half + 1) * 512]))
            own.wait()
            own.link(V.bn_aggr(lns[:, 0:2], bns[:, 0:12].rearrange("p (n c) -> p n c", c=6)))
            sig(TS(lns[:, 4 + s:5 + s], lns[:, 1:2], LN_EPS, None, ALU.add), "ln_var")
            dve.wait_ge(S("ln_rstd"), n + 1)
            own.link(TS(z[:, s, :], z[:, s, :], lns[:, 0:1], lns[:, 8 + s:9 + s], ALU.subtract, ALU.mult))
            dve.wait_ge(S("ld_ln"), 16 * (l * 2 + w + 1))
            own.link(TT(z[:, s, :], z[:, s, :], lnp[:, 0, :], ALU.mult))
            sig(TT(x[:, s, :], z[:, s, :], lnp[:, 1, :], ALU.add), "x_new")
            dve.wait_ge(S("x_new"), n + 1)

        dve.wait_ge(S("cond_exp"), 1)
        cw = condw[:, 0:16]
        own.link(TS(cw, cw, 1.0, None, ALU.add))
        own.link(V.reciprocal(condw[:, 16:32], cw))
        cflat = cond.rearrange("p k s -> p (k s)")
        sig(TT(cflat, cflat, condw[:, 16:32], ALU.mult), "cond")
        dve.wait_ge(S("ld_vec"), 16)
        own.inc(TS(nvec[:, 0:15], vec[:, V_MU:V_MU + 15], -1.0, 1.0, ALU.mult, ALU.add))
        own.inc(TS(nvec[:, 15:30], vec[:, V_MU:V_MU + 15], 0.5, None, ALU.mult))
        own.inc(TS(nvec[:, 30:38], vec[:, V_A0:V_A0 + 8], -1.0, None, ALU.mult))
        own.inc(TS(nvec[:, 38:46], vec[:, V_PW:V_PW + 8], -1.0, None, ALU.mult))
        sig(TS(nvec[:, 46:50], vec[:, V_KA:V_KA + 4], -1.0, 1.0, ALU.mult, ALU.add), "vecs")
        dve.wait_ge(S("vecs"), 1)
        for c in range(4):
            mod(0, c)
        for s in range(NS):
            modulated(("xT", "m0", s, 1), s, 4, 0, 0)

        for i in range(NPA):
            BK.wait_drained(dve, ("pa", i))
            nb = nbr[:, i % 2, :].rearrange("p (s n) -> p s n", s=NS)
            own.link(TT(nb, raw[:, i % 4, :, 0:128], raw[:, i % 4, :, 2:130], ALU.add))
            m = 15 + TILES[i]
            sig(STT(PA[:, i, :], nbr[:, i % 2, :], nvec[:, m:m + 1], PA[:, i, :], ALU.mult, ALU.add), "shifted")
            if i == 6:
                dve.wait_ge(S("lora_exp"), 2)
                for q in (0, 2):
                    own.link(TS(PA[:, q, :], PA[:, q, :], 1.0, None, ALU.add))
                    if q == 0:
                        own.link(V.reciprocal(PA[:, 0, :], PA[:, 0, :]))
                        sig(TS(PA[:, 0, :], PA[:, 0, :], 2.0, -1.0, ALU.mult, ALU.add), "lora")
                    else:
                        sig(V.reciprocal(PA[:, 2, :], PA[:, 2, :]), "lora")
                dve.wait_ge(S("shifted"), 7)
                for t in range(AT):
                    ins = TS(KK[:, t, :], K_[:, t, :], vec[:, V_KK + t:V_KK + t + 1], None, ALU.mult)
                    if t < AT - 1:
                        own.inc(ins)
                sig(ins, "kk")
        for t in range(AT):
            bank = take(("pb", t))
            dve.wait_ge(S("eg"), t + 1)
            e = eg[:, t % 2, :]
            own.link(TS(e, e, 1.0, None, ALU.add))
            own.link(V.reciprocal(e, e))
            dve.wait_ge(S("zeroed"), 2)
            ins = STT(glu[:, t, :, PADC:PADC + T], bank[:, 0:256].rearrange("p (s n) -> p s n", s=NS),
                      vec[:, V_PW + t:V_PW + t + 1], e.rearrange("p (s n) -> p s n", s=NS), ALU.add, ALU.mult)
            BK.drained_by(ins, ("pb", t))

        dve.wait_ge(S("ld_w0"), 16)
        SZ = [(s, z) for s in range(NS) for z in range(2)]
        for n in range(5):
            if n < 4:
                s, z = SZ[n]
                BK.drained_by(TT(lw[:, s, z, :], take(("w", s, z)), w0b[:, z, :], ALU.add), ("w", s, z))
            if n >= 1:
                s, z = SZ[n - 1]
                dve.wait_ge(S("lw_exp"), n)
                own.link(TS(lw[:, s, z, :], lw[:, s, z, :], 1.0, None, ALU.add))
                sig(V.reciprocal(lw[:, s, z, :], lw[:, s, z, :]), "sigw")
        dve.wait_ge(S("sq"), 1)
        for tp in range(2):
            bank = take(("ss", tp))
            if tp == 0:
                BK.wait_filled(dve, ("ss", 1))
            BK.drained_by(TS(sq[:, tp * 512:(tp + 1) * 512], bank, 1e-24, None, ALU.max), ("ss", tp))
        for z in range(2):
            BK.wait_drained(dve, ("a", z, 1))
            az = Ab[:, z].rearrange("p t n -> p (t n)")
            own.link(TS(az, az, 1.0, None, ALU.add))
            own.link(V.reciprocal(az, az))
        for z in range(2):
            for t in range(AT):
                bank = take(("cum", z, t))
                mid = bank[:, 0:260].rearrange("p (s n) -> p s n", s=NS)[:, :, 64:65].rearrange("p s n -> p (s n)")
                own.inc(TS(cb[:, 0, z, t, :], mid, -1.0, None, ALU.mult))
                sig(TS(cb[:, 1, z, t, :], mid, 1.0, None, ALU.mult), "centres")
        flat = lambda v: v.rearrange("p t n -> p (t n)")
        dve.wait_ge(S("rs"), 1)
        own.link(STT(flat(KK), flat(KK), float(2 ** 16), sq, ALU.mult, ALU.mult))
        for z in range(2):
            for t in range(AT):
                own.inc(TS(KZ[:, z, t, :], Ab[:, z, t, :], vec[:, V_KA + t:V_KA + t + 1], nvec[:, 46 + t:47 + t],
                           ALU.mult, ALU.add))
            own.wait()
            own.inc(TT(flat(KZ[:, z]), flat(KZ[:, z]), flat(K_), ALU.mult))
            own.link(STT(flat(Ab[:, z]), flat(KK), -1.0, flat(Ab[:, z]), ALU.mult, ALU.mult))
        own.link(TT(flat(prod), flat(KZ[:, 0]), flat(KZ[:, 1]), ALU.add))
        for t in range(AT):
            ins = STT(prod[:, t, :], R_[:, t, :], vec[:, V_RK + t:V_RK + t + 1], prod[:, t, :], ALU.mult, ALU.mult)
            if t < AT - 1:
                own.inc(ins)
        sig(ins, "prod")
        BK.wait_drained(dve, ("cum", 1, 3))
        for z in range(2):
            for s in range(NS):
                f, at0 = (1, 0) if (z == 0) == (s == 1) else (0, 128)
                own.inc(V.tensor_copy(fsc[:, z, :, s], FG[:, f, z, :, s, at0]))
        BK.wait_filled(dve, ("cum", 1, 3))
        for z in range(2):
            up, dn = ((0, slice(1, 129)), (1, slice(1, 129))) if z == 0 else ((1, slice(0, 128)), (0, slice(0, 128)))
            pre = (0, slice(0, 128)) if z == 0 else (1, slice(1, 129))
            for c, (src, (f, r)) in enumerate([(KK, pre), (R_, up), (Ab[:, z], dn), (KZ[:, z], dn)]):
                out = OPS[:, z, :, :, c, :].rearrange("p t s n -> p (t s) n")
                sig(TT(out, src.rearrange("p t (s n) -> p (t s) n", s=NS),
                       FG[:, f, z, :, :, r].rearrange("p t s n -> p (t s) n"), ALU.mult), "ops")
        dve.wait_ge(S("ops"), 8)
        dve.wait_ge(S("ld_s0"), 16)
        for z in range(2):
            for t in range(AT):
                ins = TS(S0[:, z, t, :], S0[:, z, t, :], fsc[:, z, t, 1:2], None, ALU.mult)
                if (z, t) != (1, 3):
                    own.inc(ins)
        sig(ins, "s0")
        BK.drained_by(V.tensor_copy(bon, take("bonus")[:, 0:16]), "bonus")
        BK.wait_drained(dve, "bonus")
        for c in range(4, 12):
            mod(0, c)

        taps = [0]

        def conv(n):
            for _ in range(n):
                if taps[0] == CONV_W * AT:
                    return
                j, t = divmod(taps[0], AT)
                src, w = glu[:, t, :, j:j + T], vec[:, V_DW + j * AT + t:V_DW + j * AT + t + 1]
                out = CONV[:, t, :].rearrange("p (s n) -> p s n", s=NS)
                if j == 0:
                    ins = TS(out, src, w, vec[:, V_DB + t:V_DB + t + 1], ALU.mult, ALU.add)
                else:
                    dve.wait_ge(S("conv"), taps[0] - AT + 1)
                    ins = STT(out, src, w, out, ALU.mult, ALU.add)
                sig(ins, "conv")
                taps[0] += 1

        def group_norm(s):
            dve.wait_ge(S("y_done"), 2 * s + 2)
            BK.wait_filled(dve, ("fT", 1, 1))
            y3 = ps[:, 6 + s, :].rearrange("p (h n) -> p h n", h=H)
            yb3, tb3 = yb.rearrange("p (h n) -> p h n", h=H), tb.rearrange("p (h n) -> p h n", h=H)
            bc = lambda v: v.rearrange("p (h o) -> p h o", o=1).broadcast_to([P, H, HD])
            own.link(V.tensor_reduce(st8[:, 0:8], y3, AX, ALU.add))
            own.link(TS(st8[:, 0:8], st8[:, 0:8], 1.0 / HD, None, ALU.mult))
            own.link(TT(yb3, y3, bc(st8[:, 0:8]), ALU.subtract))
            own.link(TT(tb, yb, yb, ALU.mult))
            own.link(V.tensor_reduce(st8[:, 24:32], tb3, AX, ALU.add))
            sig(TS(st8[:, 8:16], st8[:, 24:32], 1.0 / HD, GN_EPS, ALU.mult, ALU.add), "gn_var")
            dve.wait_ge(S("gn_rstd"), s + 1)
            own.link(TT(yb3, yb3, bc(st8[:, 16:24]), ALU.mult))
            dve.wait_ge(S("ld_gn"), 16)
            own.inc(TT(yb, yb, gnp[:, 0, :], ALU.mult))
            own.link(TT(tb3, VT[:, s, :].rearrange("p (h n) -> p h n", h=H), bc(bon[:, s * 8:s * 8 + 8]), ALU.mult))
            own.link(TT(yb, yb, gnp[:, 1, :], ALU.add))
            own.link(TT(yb, yb, tb, ALU.add))
            bank = take(("g", s))
            BK.drained_by(TT(yb, yb, bank, ALU.mult), ("g", s))
            BK.wait_drained(dve, ("g", s))
            sig(V.tensor_copy(VT[:, s, :], yb), "mixed_a")

        mask_f = [[SU, UI], [SL, LI]]
        for (s, z) in PAIRS:
            for g in range(2):
                for i in range(4):
                    bank = take(("gram", s, z, g, i))
                    m = cst[:, C_SU:C_SU + 512].rearrange("p (c n) -> p c n", c=4)[:, z::2, :]
                    m = m.rearrange("p (o c) n -> p o c n", o=1).broadcast_to([P, 2, 2, P])
                    BK.drained_by(TT(MAT[:, g, i].rearrange("p (b c) n -> p b c n", b=2),
                                     bank.rearrange("p (b c n) -> p b c n", b=2, c=2), m, ALU.mult),
                                  ("gram", s, z, g, i))
                m = (SL if z == 0 else SU).rearrange("p (o n) -> p o n", o=1).broadcast_to([P, 4, P])
                BK.drained_by(TT(LS[:, g, 0], take(("L", s, z, g, 0)).rearrange("p (i n) -> p i n", i=4), m, ALU.mult),
                              ("L", s, z, g, 0))
            for j in range(LEVELS):
                for g in range(2):
                    key = ("X", s, z, g, j)
                    bank = take(key)
                    if j == 0:
                        BK.wait_drained(dve, ("B", s, z, g))
                    else:
                        BK.wait_drained(dve, ("X", s, z, g, j - 1))
                    BK.drained_by(TT(XS[:, g, (j + 1) % 2, :], bank[:, 0:256], XS[:, g, j % 2, :], ALU.add), key)
                    if j < LEVELS - 1:
                        key = ("LT", s, z, g, j + 1)
                        BK.drained_by(V.tensor_copy(LT[:, g, (j + 1) % 2].rearrange("p i n -> p (i n)"), take(key)), key)
                if (s, z, j) in mod_between:
                    mod(1, mod_between[(s, z, j)])
                conv(5)
            if s == 0:
                if z == 1:
                    BK.wait_filled(dve, ("fT", 0, 1))
                for t in range(AT):
                    for c in range(2):
                        ins = TS(fint[:, t, c, :], OPS[:, z, t, 0, 2 + c, :], fsc[:, z, t, 0:1], None, ALU.mult)
                        if (t, c) != (AT - 1, 1):
                            own.inc(ins)
                sig(ins, "fin")
            if z == 1:
                if s == 1:
                    conv(CONV_W * AT)
                group_norm(s)
        dve.wait_ge(S("ld_cln"), 16)
        for s in range(NS):
            bank = take(("cT", s))
            own.link(V.bn_stats(bns[:, 12:18], bank))
            own.link(V.bn_aggr(st8[:, 36:38], bns[:, 12:18].rearrange("p (n c) -> p n c", c=6)))
            sig(TS(st8[:, 34 + s:35 + s], st8[:, 37:38], LN_EPS, None, ALU.add), "cln_var")
            dve.wait_ge(S("cln_rstd"), s + 1)
            BK.drained_by(TS(yb, bank, st8[:, 36:37], st8[:, 32 + s:33 + s], ALU.subtract, ALU.mult), ("cT", s))
            BK.wait_drained(dve, ("cT", s))
            own.link(TT(yb, yb, cln[:, 0, :], ALU.mult))
            own.link(TT(yb, yb, cln[:, 1, :], ALU.add))
            sig(TS(tb, yb, -80.0, None, ALU.max), "cln_y")
            dve.wait_ge(S("cln_exp"), s + 1)
            own.link(TS(tb, tb, 1.0, None, ALU.add))
            own.link(V.reciprocal(tb, tb))
            sig(TT(OB[:, s, :], yb, tb, ALU.mult), "mixed_b")
            dve.wait_ge(S("mixed_b"), s + 1)
            sig(TS(st8[:, 40:41], st8[:, 36:37], 1.0, None, ALU.mult), "convT")
        for s in range(NS):
            copy3(dve, BK, ("oT", 0, s, 1), hT, s, 4)
        for s in range(NS):
            layer_norm(0, 0, s, zl, lambda half: take(("mix", 0, s, half)))

        def moe(l):
            rv = lambda at, n, pattern=None, **z: (rt_[:, at:at + n].rearrange(pattern, **z) if pattern else rt_[:, at:at + n])
            if l == 0:
                pass
            for s in range(NS):
                modulated(("xT", f"e{l}", s, 1), s, 4, l, 3)
            lg = rv(R_LG, 72, "p (s n) -> p s n", s=NS)
            bank = take(("lg", l))
            dve.wait_ge(S("ld_rb"), 16 * (l + 1))
            rb3 = rb.rearrange("p (o n) -> p o n", o=1).broadcast_to([P, NS, 36])
            BK.drained_by(TT(lg, bank[:, 0:128].rearrange("p (s n) -> p s n", s=NS)[:, :, 0:36], rb3, ALU.add), ("lg", l))
            BK.wait_drained(dve, ("lg", l))
            sc = rt_[:, R_S:R_S + 64]
            two = lambda at: sc[:, at:at + 2]
            bc2 = lambda at, n: two(at).rearrange("p (s o) -> p s o", o=1).broadcast_to([P, NS, n])
            row = lambda at, n: cst[:, at:at + n].rearrange("p (o n) -> p o n", o=1).broadcast_to([P, NS, n])

            def first_max(v, n, best, onehot, at_iota):
                own.link(V.tensor_reduce(two(best), v, AX, ALU.max))
                own.link(TT(onehot, v, bc2(best, n), ALU.is_equal))
                own.link(STT(onehot, onehot, -1000.0, row(at_iota, n), ALU.mult, ALU.add))
                own.link(V.tensor_reduce(two(30), onehot, AX, ALU.min))
                own.link(TS(two(30), two(30), 1000.0, None, ALU.add))
                own.link(TT(onehot, row(at_iota, n), bc2(30, n), ALU.is_equal))

            ohg = rv(R_OHG, 8, "p (s n) -> p s n", s=NS)
            ex = rv(R_EX, 8, "p (s n) -> p s n", s=NS)
            first_max(lg[:, :, 0:4], 4, 0, ohg, C_G4)
            sig(TT(ex, lg[:, :, 0:4], bc2(0, 4), ALU.subtract), "routed1")
            t4 = rv(R_T4, 64)
            for s in range(NS):
                own.inc(TT(t4[:, s * 32:(s + 1) * 32].rearrange("p (g e) -> p g e", g=NG),
                           lg[:, s, 4:36].rearrange("p (g e) -> p g e", g=NG),
                           ohg[:, s, :].rearrange("p (g o) -> p g o", o=1).broadcast_to([P, NG, EPG]), ALU.mult))
            own.wait()
            ein = rv(R_EIN, 16, "p (s n) -> p s n", s=NS)
            for s in range(NS):
                own.inc(V.tensor_reduce(ein[:, s, :], t4[:, s * 32:(s + 1) * 32].rearrange("p (g e) -> p e g", g=NG), AX, ALU.add))
            own.wait()
            o1, o2 = rv(R_O1, 16, "p (s n) -> p s n", s=NS), rv(R_O2, 16, "p (s n) -> p s n", s=NS)
            first_max(ein, 8, 2, o1, C_G4 + 4)
            own.link(STT(ein, o1, -1e30, ein, ALU.mult, ALU.add))
            first_max(ein, 8, 4, o2, C_G4 + 4)
            sig(TT(two(16), two(4), two(2), ALU.subtract), "routed2")
            P1, P2 = rv(R_P1, 64), rv(R_P2, 64)
            for dst, oh in ((P1, o1), (P2, o2)):
                for s in range(NS):
                    own.inc(TT(dst[:, s * 32:(s + 1) * 32].rearrange("p (g e) -> p g e", g=NG),
                               ohg[:, s, :].rearrange("p (g o) -> p g o", o=1).broadcast_to([P, NG, EPG]),
                               oh[:, s, :].rearrange("p (o e) -> p o e", o=1).broadcast_to([P, NG, EPG]), ALU.mult))
            own.wait()
            sig(TT(rv(R_OH, 64), P1, P2, ALU.add), "chosen")
            own.link(V.memset(rv(R_ZERO, P), 0.0))
            sig(V.memset(sc[:, 60:62], 0.0), "zero")
            dve.wait_ge(S("route_exp"), 2 * l + 2)
            own.link(V.tensor_reduce(two(20), ex, AX, ALU.add))
            own.link(V.reciprocal(two(22), two(20)))
            own.link(TS(two(24), two(16), 1.0, None, ALU.add))
            own.link(V.reciprocal(two(26), two(24)))
            own.link(TT(two(26), two(26), two(22), ALU.mult))
            own.link(TT(two(28), two(26), two(16), ALU.mult))
            bank = take(("pos", l))
            slot_of = rv(R_SL, 64)
            own.link(V.tensor_copy(sc[0:32, 32:33], bank[0:32, 64:65]))
            own.link(TS(sc[0:32, 33:34], sc[0:32, 32:33], 0.5, None, ALU.is_gt))
            for m in range(1, NS * T // CH):
                own.link(STT(sc[0:32, 33:34], sc[0:32, 32:33], m * CH + 0.5, sc[0:32, 33:34], ALU.is_gt, ALU.add))
            sig(TS(rt_[0:32, R_NB:R_NB + P], ones[0:32, :], sc[0:32, 33:34], None, ALU.mult), "nchunks")
            BK.drained_by(V.tensor_copy(slot_of, bank[:, 0:64]), ("pos", l))
            BK.wait_drained(dve, ("pos", l))
            bank = take(("base", l))
            own.inc(V.tensor_copy(sc[:, 40:41], bank[:, 32:33]))
            own.link(V.tensor_copy(sc[0:32, 41:42], bank[0:32, 64:65]))
            sig(TS(rt_[0:32, R_CMP:R_CMP + 40], cst[0:32, C_G4 + 12:C_G4 + 52], sc[0:32, 41:42], None, ALU.is_ge), "ended")
            own.link(TS(rv(R_T, 32), bank[:, 0:32], float(CH), None, ALU.mult))
            for s in range(NS):
                ins = TT(slot_of[:, s * 32:(s + 1) * 32], slot_of[:, s * 32:(s + 1) * 32], rv(R_T, 32), ALU.add)
                if s == 0:
                    own.inc(ins)
            BK.drained_by(ins, ("base", l))
            BK.wait_drained(dve, ("base", l))
            for pick, oh in ((0, P1), (1, P2)):
                own.link(TT(rv(R_T, 64), oh, slot_of, ALU.mult))
                own.link(V.tensor_reduce(sc[:, 42 + 2 * pick:44 + 2 * pick], rv(R_T, 64, "p (s n) -> p s n", s=NS), AX, ALU.add))
            own.link(TS(rt_[0:1, R_T:R_T + 10], cst[0:1, C_G4 + 12:C_G4 + 52:4], sc[0:1, 40:41], None, ALU.is_lt))
            own.link(V.tensor_reduce(sc[0:1, 46:47], rt_[0:1, R_T:R_T + 10], AX, ALU.add))
            own.link(V.tensor_copy(meta[0:1, l, 0:1], sc[0:1, 46:47]))
            own.link(TS(rt_[0:1, R_T:R_T + 40], take(("eid", l))[0:1, 0:40], float(NE - 1), None, ALU.min))
            BK.drained_by(V.tensor_copy(meta[0:1, l, 4:44], rt_[0:1, R_T:R_T + 40]), ("eid", l))
            BK.wait_drained(dve, ("eid", l))
            sig(V.memset(sc[:, 62:64], 0.0), f"meta{l}")
            dve.wait_ge(S(f"meta{l}"), 1)
            trips = dve.value_load(meta[0:1, l, 0:1], min_val=1, max_val=10)
            loop = S(f"dve_loop{l}")

            def chained(m, ins):
                ins.then_inc(loop, 1)
                dve.wait_ge(loop, m)

            def choose(n, m):
                for s in range(NS):
                    TS(sel[:, s, :], iota, sc[:, 42 + s:43 + s], None, ALU.is_equal).then_inc(loop, 1)
                dve.wait_ge(loop, m + 2)
                for s in range(NS):
                    ins = STT(sel[:, s, :], iota, sc[:, 44 + s:45 + s], sel[:, s, :], ALU.is_equal, ALU.add)
                    if s == 0:
                        ins.then_inc(loop, 1)
                ins.then_inc(S(f"selected{l}"), 1)
                dve.wait_ge(loop, m + 3)
                dve.wait_ge(S(f"selected{l}"), n + 1)

            def gates(n, m):
                for s in range(NS):
                    TS(gsel[:, 0, s, :], iota, sc[:, 42 + s:43 + s], sc[:, 26 + s:27 + s], ALU.is_equal, ALU.mult)\
                        .then_inc(loop, 1)
                    TS(gsel[:, 1, s, :], iota, sc[:, 44 + s:45 + s], sc[:, 28 + s:29 + s], ALU.is_equal, ALU.mult)\
                        .then_inc(loop, 1)
                dve.wait_ge(loop, m + 4)
                TT(gsel[:, 0, :, :], gsel[:, 0, :, :], gsel[:, 1, :, :], ALU.add).then_inc(S(f"gates{l}"), 1)
                chained(m + 5, TS(sc[:, 42:46], sc[:, 42:46], float(P), None, ALU.subtract))
                dve.wait_ge(S(f"gates{l}"), n + 1)

            def gathered(n):
                dve.wait_ge(S(f"gathered{l}"), n * 2 + 2)
                V.tensor_copy(xg[:, 4:8, :].rearrange("p k n -> p (k n)"), ps[:, 5, :]).then_inc(S(f"xg_dve{l}"), 1)

            V.memset(tT[1][:, 256:512], 0.0)
            V.memset(ysb, 0.0).then_inc(S(f"y_read_dve{l}"), 1)
            choose(0, 0)
            gates(0, 3)
            gathered(0)
            choose(1, 8)
            with dve.Fori(0, trips) as it:
                for u in range(2):
                    n = it * 2 + u
                    dve.wait_ge(S(f"gate_exp{l}"), n + 1)
                    V.tensor_scalar(hid[:, 0, :], hid[:, 0, :], 1.0, None, ALU.add).then_inc(S(f"dve_hid{l}"), 1)
                    dve.wait_ge(S(f"dve_hid{l}"), n * 3 + 1)
                    V.reciprocal(hid[:, 0, :], hid[:, 0, :]).then_inc(S(f"dve_hid{l}"), 1)
                    dve.wait_ge(S(f"dve_hid{l}"), n * 3 + 2)
                    TT(hid[:, 0, :], hid[:, 0, :], ps[:, 6, 0:256], ALU.mult).then_inc(S(f"dve_hid{l}"), 1)
                    dve.wait_ge(S(f"dve_hid{l}"), n * 3 + 3)
                    TT(hid[:, 1, :], hid[:, 0, :], ps[:, 6, 256:512], ALU.mult).then_inc(S(f"hid{l}"), 1)
                    gathered(n + 1)
                    dve.wait_ge(S(f"turned{l}"), n + 1)
                    gates(n + 1, n * 8 + 11)
                    choose(n + 2, n * 8 + 16)
                    dve.wait_ge(S(f"down{l}"), n * 2 + 6)
                    V.tensor_copy(ysb[:, 512:1024], ps[:, 5, :]).then_inc(S(f"y_read_dve{l}"), 1)
            dve.wait_ge(S("summed"), l + 1)
            for s in range(NS):
                layer_norm(l, 1, s, zm, lambda half: ps[:, 2 * s + half, :])

        moe(0)

        for s in range(NS):
            modulated(("xT", "m1", s, 1), s, 4, 1, 0)
        dve.wait_ge(S("ld_sub"), 32)
        for q in range(2):
            own.link(TT(lqk[:, 2 * q, :], lqk[:, 2 * q, :], lqk[:, 2 * q + 1, :], ALU.mult))
            ins = V.tensor_reduce(lam[:, q:q + 1], lqk[:, 2 * q, :], AX, ALU.add)
            if q == 0:
                own.inc(ins)
        sig(ins, "lam_dot")
        dve.wait_ge(S("ld_rope"), 16)

        def halves(v):
            v = v.rearrange("p (h a b f) -> p h a b f", h=16, a=2, b=2)
            return v[:, :, :, 0, :], v[:, :, :, 1, :]

        cosb = rope[:, 0:32].rearrange("p (o a f) -> p o a f", o=1, a=2).broadcast_to([P, 16, 2, 16])
        sinb = rope[:, 32:64].rearrange("p (o a f) -> p o a f", o=1, a=2).broadcast_to([P, 16, 2, 16])
        rv4 = [rt[:, q, :].rearrange("p (h a f) -> p h a f", h=16, a=2) for q in range(4)]
        for q in range(2):
            BK.wait_drained(dve, ("qkv", 1, 2 * q + 1))
            x1, x2 = halves(QKV[:, 1, q * D:(q + 1) * D])
            y1, y2 = halves(QR[:, q, :])
            if q == 1:
                dve.wait_ge(S("roped"), 1)
            own.inc(TT(rv4[0], x1, cosb, ALU.mult))
            own.inc(TT(rv4[1], x2, sinb, ALU.mult))
            own.inc(TT(rv4[2], x1, sinb, ALU.mult))
            own.inc(TT(rv4[3], x2, cosb, ALU.mult))
            own.wait()
            own.inc(TT(y1, rv4[0], rv4[1], ALU.subtract))
            sig(TT(y2, rv4[2], rv4[3], ALU.add), "roped")
        dve.wait_ge(S("lam_exp"), 1)
        own.link(TT(lam[:, 4:5], lam[:, 2:3], lam[:, 3:4], ALU.subtract))
        own.link(TS(lam[:, 5:6], lam[:, 4:5], LAM_INIT, None, ALU.add))
        for n in range(len(PAIRS1) + 1):
            if n < len(PAIRS1):
                s, hp = PAIRS1[n]
                nk = T * (s + 1)
                q = sm1[:, n % 4]
                for z in range(2):
                    bank = take(("sc", s, hp, z))
                    own.link(V.tensor_reduce(q[:, 2 * z:2 * z + 2], bank.rearrange("p (m n) -> p m n", m=2)[:, :, 0:nk],
                                             AX, ALU.max))
                    sig(TS(q[:, 4 + 2 * z:6 + 2 * z], q[:, 2 * z:2 * z + 2], -HD ** -0.5, None, ALU.mult), "smax")
            if n >= 1:
                s, hp = PAIRS1[n - 1]
                b = (n - 1) % 2
                nk = T * (s + 1)
                q = sm1[:, (n - 1) % 4]
                BK.wait_drained(dve, ("sc", s, hp, 1))
                own.link(V.reciprocal(q[:, 12:16], q[:, 8:12]))
                own.link(TS(q[:, 14:16], q[:, 14:16], lam[:, 5:6], None, ALU.mult))
                for m in range(2):
                    own.inc(TS(PB[:, b, 1, m, 0:nk], PB[:, b, 1, m, 0:nk], q[:, 14 + m:15 + m], None, ALU.mult))
                own.wait()
                if n >= 3:
                    BK.wait_filled(dve, ("aT",) + PAIRS1[n - 3])
                for m in range(2):
                    sig(STT(AB[:, b, m, 0:nk], PB[:, b, 0, m, 0:nk], q[:, 12 + m:13 + m], PB[:, b, 1, m, 0:nk],
                            ALU.mult, ALU.subtract), "attn")
            if n >= 1 and n % 2 == 0:
                s, hp = PAIRS1[n - 1]
                key = ("pv", s, hp // 2)
                BK.drained_by(V.tensor_copy(OO[:, s, (hp // 2) * 512:(hp // 2 + 1) * 512], take(key)), key)
        for s in range(NS):
            BK.wait_drained(dve, ("pv", 1, 1))
            o3 = OO[:, s, :].rearrange("p (h n) -> p h n", h=H)
            own.link(TT(t1k, OO[:, s, :], OO[:, s, :], ALU.mult))
            own.link(V.tensor_reduce(st8[:, 24:32], t1k.rearrange("p (h n) -> p h n", h=H), AX, ALU.add))
            sig(TS(st8[:, 8:16], st8[:, 24:32], 1.0 / P, RMS_EPS, ALU.mult, ALU.add), "at_var")
            dve.wait_ge(S("at_rstd"), s + 1)
            own.link(TT(o3, o3, st8[:, 16:24].rearrange("p (h o) -> p h o", o=1).broadcast_to([P, H, P]), ALU.mult))
            sg = subg.rearrange("p (o n) -> p o n", o=1).broadcast_to([P, H, P])
            sig(STT(o3, o3, 1.0 - LAM_INIT, sg, ALU.mult, ALU.mult), "attended")
            copy3(dve, BK, ("oT", 1, s, 1), hT, s, 4)
        for s in range(NS):
            layer_norm(1, 0, s, zl1, lambda half: take(("mix", 1, s, half)))
        moe(1)

    ctx.close()


def kernel(**inputs):
    import concourse.bacc as bacc
    from concourse.bass_utils import run_bass_kernel_spmd

    a = {k: np.asarray(v) for k, v in inputs.items()}
    tile = lambda w: np.ascontiguousarray(w.reshape(*w.shape[:-2], KT, P, w.shape[-1]).swapaxes(-3, -2))
    cut = lambda w: np.stack([tile(w[:, c:c + 512]) for c in range(0, w.shape[1], 512)]).reshape(-1, P, 4096)
    col = lambda v: np.ascontiguousarray(v.reshape(-1, P).T)
    ev = a["ev_in_w"][0]
    evc = np.concatenate([ev[:, t * P:(t + 1) * P] for t in TILES], 1)
    evp = np.concatenate([tile(evc[:, c:c + 512]).reshape(P, -1) for c in range(0, evc.shape[1], 512)], 1)
    vec = np.concatenate([
        col(a["ev_ts_mu"][0]), col(a["ev_pw_b"][0]), col(a["ev_a0"][0].reshape(-1)), col(a["ev_k_k"][0]),
        col(a["ev_k_a"][0]), col(a["ev_r_k"][0].reshape(-1)), col(a["ev_dw_b"][0]), col(a["ev_dw_w"][0].reshape(-1))], 1)
    s0 = a["state_wkv"][0, 0].transpose(0, 1, 3, 2)
    s0 = s0.reshape(2, AT, P, HD).transpose(2, 0, 1, 3)
    gate = a["ffn_w_gate"].reshape(2, NE, KT, P, FF)
    up = a["ffn_w_up"].reshape(2, NE, KT, P, FF)
    down = a["ffn_w_down"].reshape(2, NE, 2, P, D)
    exp = np.concatenate([
        np.concatenate([gate, up], -1).transpose(0, 1, 3, 2, 4).reshape(2, NE, P, KT * 2 * FF),
        down.transpose(0, 1, 3, 2, 4).reshape(2, NE, P, 2 * D)], -1)
    arrays = {
        "cst": constants(), "rope": rope_tables(), "vec": vec,
        "cond": np.stack([a["c_ctx"], a["c"][0]]).reshape(2, KT, P).transpose(2, 1, 0),
        "x_prompt": a["x_prompt"][0], "x_sample": a["x_sample"][0],
        "mod_w": np.stack([cut(a["mod_w"][l]) for l in range(2)]), "mod_b": a["mod_b"],
        "ev_in_w": evp, "ev_w_up": a["ev_w_up"][0].reshape(P, AW), "ev_a_up": a["ev_a_up"][0].reshape(P, AW),
        "ev_g_up": a["ev_g_up"][0], "s0t": s0, "ev_w0": a["ev_w0"][0],
        "ev_cln": np.stack([a["ev_cln_g"][0], a["ev_cln_b"][0]]), "ev_gn": np.stack([a["ev_gn_g"][0], a["ev_gn_b"][0]]),
        "ev_out_w": cut(a["ev_out_w"][0]), "od_in_w": cut(a["od_in_w"][0]), "od_out_w": cut(a["od_out_w"][0]),
        "ln": np.stack([np.stack([a[f"ln{w}_g"][l], a[f"ln{w}_b"][l]]) for l in range(2) for w in (1, 2)]),
        "lqk": np.stack([a["od_lq1"][0], a["od_lk1"][0], a["od_lq2"][0], a["od_lk2"][0]]),
        "subln": a["od_subln_g"][0],
        "cache_k": a["cache_k"][0, 0].reshape(T, D), "cache_v": a["cache_v"][0, 0].reshape(T, D),
        "r_w": np.stack([tile(np.concatenate([a["rg_w"][l], a["re_w"][l]], 1)).reshape(P, -1) for l in range(2)]),
        "r_b": np.concatenate([a["rg_b"], a["re_b"]], 1), "w_exp": exp,
    }
    outs = {"y": (NS, T, D), "state": (2, H, HD, HD), "cache_k": (T, D), "cache_v": (T, D)}
    nc = bacc.Bacc("TRN2", target_bir_lowering=False, num_devices=1)
    arrays = {f"in_{k}": np.ascontiguousarray(v) for k, v in arrays.items()}
    ins = {k[3:]: nc.dram_tensor(k, v.shape, F32, kind="ExternalInput").ap() for k, v in arrays.items()}
    o = {k: nc.dram_tensor(f"out_{k}", v, F32, kind="ExternalOutput").ap() for k, v in outs.items()}
    build(nc, ins, o)
    r = run_bass_kernel_spmd(nc, [arrays], core_ids=[0]).results[0]
    y = r["out_y"]
    return (y[0:1], y[1:2], r["out_state"].reshape(1, 1, 2, H, HD, HD),
            r["out_cache_k"].reshape(1, 1, T, H, P), r["out_cache_v"].reshape(1, 1, T, H, P))
```

```python
from contextlib import ExitStack

import numpy as np
import concourse.bass as bass
from concourse import mybir

F32 = mybir.dt.float32
I32 = mybir.dt.int32
ALU = mybir.AluOpType
ACT = mybir.ActivationFunctionType
AX = mybir.AxisListType.X

P = 128
D = 1024
KT = D // P
T = 128
NS = 2
H = 8
HD = 64
AW = 512
AT = AW // P
CONV_W = 31
PADC = CONV_W // 2
GN_EPS = 64e-5
LN_EPS = 1e-5
RMS_EPS = 1e-5
ALPHA = 4 ** 0.25
NG, EPG = 4, 8
NE = NG * EPG
FF = 256
CH = 64
GRID_W = 64
ROPE_BASE = 10000.0
LAM_INIT = 0.8 - 0.6 * float(np.exp(-0.3))
E_HALF = float(np.exp(-0.5))

WD, AD, GD = 12, 13, 14
TILES = [WD, AD, GD] + [4, 5, 6, 7] + [0, 1, 2, 3] + [8, 9, 10, 11]
for _t in range(AT):
    TILES += [15 + _t, 19 + _t]
NPA = 15

V_MU, V_PW, V_A0, V_KK, V_KA, V_RK, V_DB, V_DW = 0, 15, 23, 31, 35, 39, 43, 47
NVEC = V_DW + CONV_W * AT

C_ID, C_SU, C_SL, C_UI, C_LI = 0, 128, 256, 384, 512
C_CUM, C_BLK, C_HSEL, C_IOTA, C_ONE = 640, 770, 898, 930, 1058
C_SEL, C_G4 = 1186, 1442
NCST = C_G4 + 64


def constants():
    c = np.zeros((P, NCST), np.float32)
    r, q = np.arange(P)[:, None], np.arange(P)[None, :]
    c[:, C_ID:C_ID + P] = r == q
    c[:, C_SU:C_SU + P] = r < q
    c[:, C_SL:C_SL + P] = r > q
    c[:, C_UI:C_UI + P] = r <= q
    c[:, C_LI:C_LI + P] = r >= q
    c[:, C_CUM:C_CUM + T + 1] = -E_HALF * (r < np.arange(T + 1)[None, :])
    c[:, C_BLK:C_BLK + P] = (r // HD) == (q // HD)
    for t in range(AT):
        for h in range(H):
            c[:, C_HSEL + t * H + h] = (2 * t + np.arange(P) // HD) == h
    c[:, C_IOTA:C_IOTA + P] = q
    c[:, C_ONE:C_ONE + P] = 1.0
    for s in range(NS):
        c[s::32, C_SEL + s * P:C_SEL + (s + 1) * P] = 1.0
    c[:, C_G4:C_G4 + 4] = np.arange(4)
    c[:, C_G4 + 4:C_G4 + 12] = np.arange(8)
    c[:, C_G4 + 12:C_G4 + 52] = np.arange(40)
    return c


def rope_tables():
    nf = HD // 4
    inv = ROPE_BASE ** (-np.arange(nf, dtype=np.float64) / nf)
    tok = np.arange(T)
    pos = np.stack([tok // GRID_W, tok % GRID_W], 1)
    ang = pos[:, :, None] * inv[None, None, :]
    return np.stack([np.cos(ang), np.sin(ang)], 1).reshape(T, 4 * nf).astype(np.float32)


class Banks:

    def __init__(self, ps, banks, filled, drained):
        self.ps, self.banks, self.filled, self.drained = ps, banks, filled, drained
        self.no, self.by, self.nth, self.order = {}, {}, {}, []
        self.count = {e: 0 for e in drained}
        self.seen = {}

    def add(self, key, by):
        assert key not in self.no, key
        self.no[key] = len(self.order)
        self.order.append(key)
        self.by[key] = by
        self.count[by] += 1
        self.nth[key] = self.count[by]

    def bank(self, key):
        return self.ps[:, self.banks[self.no[key] % len(self.banks)], :]

    def wait_free(self, pe, key):
        n = self.no[key] - len(self.banks)
        if n >= 0:
            old = self.order[n]
            pe.wait_ge(self.drained[self.by[old]], self.nth[old])

    def wait_filled(self, eng, key):
        eng.wait_ge(self.filled, self.no[key] + 1)

    def drained_by(self, ins, key):
        by = self.by[key]
        self.seen[by] = self.seen.get(by, 0) + 1
        assert self.seen[by] == self.nth[key], key
        ins.then_inc(self.drained[by], 1)

    def wait_drained(self, eng, key):
        eng.wait_ge(self.drained[self.by[key]], self.nth[key])


def copy3(eng, BK, key, hT, s, k0):
    BK.wait_filled(eng, key)
    dst = hT[:, k0:k0 + 4, s * T:(s + 1) * T]
    src = BK.bank(key).rearrange("p (k n) -> p k n", k=4)
    if BK.by[key] == "act":
        BK.drained_by(eng.activation(dst, src, ACT.Copy), key)
    else:
        BK.drained_by(eng.tensor_copy(dst, src), key)


class Steps:

    def __init__(self, eng, sem):
        self.eng, self.sem, self.n = eng, sem, 0

    def inc(self, ins):
        self.n += 1
        ins.then_inc(self.sem, 1)
        return self.n

    def wait(self, n=None):
        self.eng.wait_ge(self.sem, self.n if n is None else n)

    def link(self, ins):
        self.inc(ins)
        self.wait()


ARENA = 53110


def build(nc, a, o, dbg=None):
    ctx = ExitStack()
    sems = {}

    def S(name):
        if name not in sems:
            sems[name] = ctx.enter_context(nc.semaphore(name))
        return sems[name]

    arena = ctx.enter_context(nc.sbuf_tensor("arena", [P, ARENA], F32))
    meta = ctx.enter_context(nc.sbuf_tensor("meta", [1, 2, 48], I32))
    ps = ctx.enter_context(nc.psum_tensor("ps", [P, 8, 512], F32))
    top = [0]

    def region(n):
        at = top[0]
        top[0] += n
        assert top[0] <= ARENA, top[0]
        return at

    def view(at, n, pattern=None, **sizes):
        v = arena[:, at:at + n]
        return v.rearrange(pattern, **sizes) if pattern else v

    cst = view(region(NCST), NCST)
    vec = view(region(NVEC), NVEC)
    nvec = view(region(64), 64)
    x = view(region(2 * D), 2 * D, "p (s n) -> p s n", s=NS)
    hT = view(region(KT * 256), KT * 256, "p (k n) -> p k n", k=KT)
    rowbuf = view(region(D), D)
    gaterow = view(region(D), D)
    mbias = view(region(3 * 512), 3 * 512, "p (g n) -> p g n", g=3)
    gbc_at = region(2 * D)
    gbc = view(gbc_at, 2 * D, "p (s n) -> p s n", s=NS)
    lnp_at = region(2 * D)
    lnp = view(lnp_at, 2 * D, "p (g n) -> p g n", g=2)
    modT = view(region(192), 192, "p (l m k s) -> p l m k s", l=2, m=6, s=NS)
    condw = view(region(48), 48)
    cond = view(region(KT * 32), KT * 32, "p (k n) -> p k n", k=KT)
    small = view(region(320), 320)
    rope = view(region(64), 64)
    ring_at = region(3 * 4096)
    ring = view(ring_at, 3 * 4096, "p (g n) -> p g n", g=3)
    scr = top[0]
    SCR = ARENA - scr

    def sv(at, n, pattern=None, **sizes):
        assert at + n <= SCR, (at + n, SCR)
        return view(scr + at, n, pattern, **sizes)

    ident = cst[:, C_ID:C_ID + P]
    SU, SL = cst[:, C_SU:C_SU + P], cst[:, C_SL:C_SL + P]
    UI, LI = cst[:, C_UI:C_UI + P], cst[:, C_LI:C_LI + P]
    blk = cst[:, C_BLK:C_BLK + P]
    iota = cst[:, C_IOTA:C_IOTA + P]
    ones = cst[:, C_ONE:C_ONE + P]

    filled = S("filled")
    BK = Banks(ps, [0, 1, 2, 3, 4, 5], filled, {"act": S("drained_act"), "dve": S("drained_dve")})

    chunks = []

    def chunk(name, src, cols, last):
        chunks.append((name, src, cols, last))

    for c in range(4):
        chunk(("mod", 0, c), a["mod_w"][0, c], 512, ("mod", 0, c))
    for c in range(6):
        n = min(4, 23 - 4 * c) * P
        last = 4 * c + n // P - 1
        key = ("pa", last) if last < NPA else ("pb", (last - NPA - 1) // 2 if (last - NPA) % 2 else (last - NPA) // 2)
        src = a["ev_in_w"][:, c * 4096:c * 4096 + 8 * n]
        chunk(("evin", c), src, n, key)
    for c in range(4, 12):
        chunk(("mod", 0, c), a["mod_w"][0, c], 512, ("mod", 0, c))
    for c in range(4):
        chunk(("mod", 1, c), a["mod_w"][1, c], 512, ("mod", 1, c))
    for c in range(4, 12):
        chunk(("mod", 1, c), a["mod_w"][1, c], 512, ("mod", 1, c))
    for c in range(2):
        chunk(("out", 0, c), a["ev_out_w"][c], 512, ("mix", 0, 1, c))
    FIRST_OF_1 = len(chunks)
    for c in range(6):
        chunk(("odin", c), a["od_in_w"][c], 512, ("qkv", 1, c))
    for c in range(2):
        chunk(("out", 1, c), a["od_out_w"][c], 512, ("mix", 1, 1, c))
    at_chunk = {name: i for i, (name, *_) in enumerate(chunks)}
    ring_ld = [S(f"ring_loaded{i}") for i in range(3)]

    def slot(name):
        i = at_chunk[name]
        cols = chunks[i][2]
        return ring[:, i % 3, 0:8 * cols].rearrange("p (k n) -> p k n", k=KT)

    def wait_chunk(pe, name):
        i = at_chunk[name]
        pe.wait_ge(ring_ld[i % 3], 16 * (i // 3 + 1))

    def load_chunk(sp, i):
        name, src, cols, _ = chunks[i]
        if i >= 3:
            BK.wait_filled(sp, chunks[i - 3][3])
        sp.dma_start(ring[:, i % 3, 0:8 * cols], src).then_inc(ring_ld[i % 3], 16)

    def plan_mod(l, c):
        BK.add(("mod", l, c), "dve")

    def plan_fold(l, c):
        if c // 2 in (2, 5):
            BK.add(("gate", l, c), "act")
        elif c % 2:
            BK.add(("modT", l, c // 2), "dve")

    def gate_slot(l, part):
        return {(0, 2): 0, (0, 5): 1, (1, 2): 2, (1, 5): 3}[(l, part)]

    for c in range(4):
        plan_mod(0, c)
        plan_fold(0, c)
    for s in range(NS):
        for h2 in range(2):
            BK.add(("xT", "m0", s, h2), "act" if h2 == 0 else "dve")
    pa, cum = (lambda *n: [("pa", i) for i in n]), (lambda z: [("cum", z, t) for t in range(AT)])
    PROJECTION = (pa(*range(11)) + [("w", 0, 0), ("w", 0, 1)] + pa(11) + [("w", 1, 0), ("w", 1, 1)] + pa(12)
                  + [("ss", 0), ("ss", 1)] + pa(13) + [("a", 0, 0), ("a", 0, 1)] + pa(14) + [("a", 1, 0), ("a", 1, 1)]
                  + [("pb", 0)] + cum(0) + [("pb", 1)] + cum(1) + [("V", 0), ("V", 1), ("pb", 2), ("pb", 3), ("bonus",)])
    for key in PROJECTION:
        BK.add(key, {"pb": "dve", "w": "dve", "ss": "dve", "bonus": "dve"}.get(key[0], "act"))
    PAIRS = [(s, z) for s in range(NS) for z in range(2)]
    LEVELS = 7
    slots = [(s, z, j) for (s, z) in PAIRS for j in range(LEVELS - 2)]
    rest = [(0, c) for c in range(4, 12)] + [(1, c) for c in range(12)]
    mod_after = dict(zip(slots, rest))
    fold_in = {(s, z, j + 1): lc for (s, z, j), lc in mod_after.items()}
    for (s, z) in PAIRS:
        for i in range(4):
            for g in range(2):
                BK.add(("gram", s, z, g, i), "dve")
        for g in range(2):
            BK.add(("L", s, z, g, 0), "dve")
        for g in range(2):
            BK.add(("B", s, z, g), "act")
        for j in range(LEVELS):
            for g in range(2):
                BK.add(("X", s, z, g, j), "dve")
                if j < LEVELS - 1:
                    BK.add(("L", s, z, g, j + 1), "act")
                    BK.add(("LT", s, z, g, j + 1), "dve")
                if g == 0 and (s, z, j) in fold_in:
                    plan_fold(*fold_in[(s, z, j)])
            if (s, z, j) in mod_after:
                plan_mod(*mod_after[(s, z, j)])
        if s == 0:
            for g in range(2):
                BK.add(("fT", z, g), "act")
                BK.add(("st", z, g), "act")
        if z == 1:
            BK.add(("g", s), "dve")
    for s in range(NS):
        BK.add(("cT", s), "dve")
    for s in range(NS):
        for n in range(2):
            BK.add(("gbc", 0, 0, s, n), "act")
    for s in range(NS):
        for h2 in range(2):
            BK.add(("oT", 0, s, h2), "act" if h2 == 0 else "dve")

    def plan_mix(l):
        for s in range(NS):
            for n in range(2):
                BK.add(("mix", l, s, n), "dve")

    def plan_moe(l):
        for s in range(NS):
            for h2 in range(2):
                BK.add(("xT", f"e{l}", s, h2), "act" if h2 == 0 else "dve")
        BK.add(("lg", l), "dve")
        for s in range(NS):
            for h2 in range(2):
                BK.add(("hb", l, s, h2), "act")
        for s in range(NS):
            for n in range(2):
                BK.add(("gbc", l, 1, s, n), "act")
        BK.add(("pos", l), "dve")
        BK.add(("base", l), "dve")
        BK.add(("eid", l), "dve")

    plan_mix(0)
    plan_moe(0)
    for s in range(NS):
        for h2 in range(2):
            BK.add(("xT", "m1", s, h2), "act" if h2 == 0 else "dve")
    for c in range(6):
        for s in range(NS):
            BK.add(("qkv", s, c), "act")
    for h2 in range(2):
        BK.add(("cT1", h2), "act")
    for s in range(NS):
        for q in range(2):
            for h2 in range(2):
                BK.add(("qkT", s, q, h2), "act")
    PAIRS1 = [(s, hp) for s in range(NS) for hp in range(H // 2)]
    for n in range(len(PAIRS1) + 1):
        if n < len(PAIRS1):
            for z in range(2):
                BK.add(("sc",) + PAIRS1[n] + (z,), "act")
        if n >= 1:
            BK.add(("aT",) + PAIRS1[n - 1], "act")
            if n % 2 == 0:
                BK.add(("pv", PAIRS1[n - 1][0], PAIRS1[n - 1][1] // 2), "dve")
    for s in range(NS):
        for n in range(2):
            BK.add(("gbc", 1, 0, s, n), "act")
    for s in range(NS):
        for h2 in range(2):
            BK.add(("oT", 1, s, h2), "act" if h2 == 0 else "dve")
    plan_mix(1)
    plan_moe(1)

    MOD_ORDER = [(k[1], k[2]) for k in BK.order if k[0] == "mod"]
    MODS = [("mod", l, c) for l, c in MOD_ORDER]
    assert MODS == [n for n, *_ in chunks if n[0] == "mod"]

    OPS = sv(0, 8192, "p (z t s c n) -> p z t s c n", z=2, t=AT, s=NS, c=4)
    wup, aup = sv(0, 512), sv(512, 512)
    lw = sv(1024, 2048, "p (s z n) -> p s z n", s=NS, z=2)
    raw = sv(3072, 4 * 260, "p (b s n) -> p b s n", b=4, s=NS)
    nbr = sv(4112, 512, "p (b n) -> p b n", b=2)
    eg = sv(4624, 512, "p (b n) -> p b n", b=2)
    sq = sv(5136, 1024)
    PA_at = 8192
    PA = sv(PA_at, 3840, "p (t n) -> p t n", t=NPA)
    K_, R_, V_ = PA[:, 3:7, :], PA[:, 7:11, :], PA[:, 11:15, :]
    cln = sv(PA_at + 768, 1024, "p (g n) -> p g n", g=2)
    gnp = sv(PA_at + 1792, 1024, "p (g n) -> p g n", g=2)
    fint = view(gbc_at + 1024, 1024, "p (t c n) -> p t c n", t=AT, c=2)
    finq = sv(PA_at + 2816, 1024, "p (g t c n) -> p g t c n", g=2, t=AT, c=2)
    OB = sv(12032, 1024, "p (s n) -> p s n", s=NS)
    VT = sv(13056, 1024, "p (s n) -> p s n", s=NS)
    PRE = 14080
    FG = sv(PRE, 4128, "p (f z t s n) -> p f z t s n", f=2, z=2, t=AT, s=NS)
    Ab = sv(PRE + 4128, 2048, "p (z t n) -> p z t n", z=2, t=AT)
    KZ = sv(PRE + 6176, 2048, "p (z t n) -> p z t n", z=2, t=AT)
    KK = sv(PRE + 8224, 1024, "p (t n) -> p t n", t=AT)
    MAT = sv(PRE, 4096, "p (g i c n) -> p g i c n", g=2, i=4, c=4)
    LS = sv(PRE + 4096, 2048, "p (g b i n) -> p g b i n", g=2, b=2, i=4)
    LT = sv(PRE + 6144, 2048, "p (g b i n) -> p g b i n", g=2, b=2, i=4)
    XS = sv(PRE + 8192, 1024, "p (g b n) -> p g b n", g=2, b=2)
    S0 = sv(PRE + 9248, 512, "p (z t n) -> p z t n", z=2, t=AT)
    STS = sv(PRE + 9760, 512, "p (b n) -> p b n", b=2)
    w0b = view(gbc_at, 1024, "p (z n) -> p z n", z=2)
    CONV = view(gbc_at, 1024, "p (t n) -> p t n", t=AT)
    prod = view(gbc_at + 1024, 1024, "p (t n) -> p t n", t=AT)
    yb, tb = view(gbc_at + 1024, 512), view(gbc_at + 1536, 512)
    glu = view(lnp_at, 1264, "p (t s n) -> p t s n", t=AT, s=NS)
    gup = view(lnp_at + 1264, 512)
    cb = small[:, 0:32].rearrange("p (g z t s) -> p g z t s", g=2, z=2, t=AT)
    bon = small[:, 32:48]
    fsc = small[:, 48:64].rearrange("p (z t s) -> p z t s", z=2, t=AT)
    st8 = small[:, 64:112]
    bns = small[:, 112:144]
    lns = small[:, 144:160]
    zl = sv(0, 2048, "p (s n) -> p s n", s=NS)

    QKV = sv(0, 6144, "p (s n) -> p s n", s=NS)
    QR = sv(6144, 2048, "p (q n) -> p q n", q=2)
    rt = sv(8192, 2048, "p (q n) -> p q n", q=4)
    QT = sv(10240, 2048, "p (s h n) -> p s h n", s=NS, h=H)
    KTp = sv(12288, 1024, "p (h n) -> p h n", h=H)
    KTs = sv(13312, 2048, "p (h n) -> p h n", h=H)
    CV = sv(15360, 1024)
    CK = sv(16384, 1024)
    PB = sv(17408, 2048, "p (b z m n) -> p b z m n", b=2, z=2, m=2)
    AB = sv(19456, 1024, "p (b m n) -> p b m n", b=2, m=2)
    ATb = sv(20480, 1024, "p (b n) -> p b n", b=2)
    OO = sv(21504, 2048, "p (s n) -> p s n", s=NS)
    t1k = sv(8192, 1024)
    subg = sv(23552, 128)
    lqk = sv(23680, 256, "p (g n) -> p g n", g=4)
    lam = small[:, 160:168]
    sm1 = small[:, 168:232].rearrange("p (n c) -> p n c", c=16)
    zl1 = sv(6144, 2048, "p (s n) -> p s n", s=NS)

    assert FIRST_OF_1 % 3 == 2
    EW = sv(0, 4 * 6144, "p (b n) -> p b n", b=4)
    er = ring_at

    def ev(at, n, pattern=None, **sizes):
        assert at + n <= 8192
        return view(er + at, n, pattern, **sizes)

    hb = ev(0, 2048, "p (s n) -> p s n", s=NS)
    xg = ev(2048, 1024, "p (k n) -> p k n", k=KT)
    ysb = ev(3072, 1024)
    zm = ev(3072, 2048, "p (s n) -> p s n", s=NS)
    sel = ev(5120, 256, "p (s n) -> p s n", s=NS)
    gsel = ev(5376, 512, "p (c s n) -> p c s n", c=2, s=NS)
    hid = ev(5888, 512, "p (c n) -> p c n", c=2)
    tT = [ev(6400, 512), sv(24576, 512)]
    rw = ev(6912, 288, "p (k n) -> p k n", k=KT)
    rb = ev(7200, 36)
    rt_ = ev(7240, 952)
    R_LG, R_A, R_OHG, R_EX, R_T4, R_EIN, R_O1, R_O2, R_OH, R_NB, R_CMP, R_SL, R_ZERO, R_S, R_P1 = (
        0, 72, 80, 88, 96, 160, 176, 192, 208, 272, 400, 440, 504, 632, 696)
    R_P2, R_T = 760, 824


    block = ctx.enter_context(nc.Block())

    def norm_no(l, w, s):
        return (l * 2 + w) * 2 + s

    def bias_dma(eng, n):
        l, c = MOD_ORDER[n]
        eng.dma_start(mbias[0:2, n % 3, :], a["mod_b"][l:l + 1, c * 512:(c + 1) * 512].partition_broadcast(2))\
            .then_inc(S(f"ld_mbias{n % 3}" if n >= 3 else "ld_mbias_first"), 16)

    @block.sync
    def _(sp):
        sp.dma_start(condw[:, 32:48], a["cond"].rearrange("p k s -> p (k s)")).then_inc(S("ld_cond"), 16)
        load_chunk(sp, 0)
        sp.wait_ge(S("mbias_zero"), 1)
        for n in range(3):
            bias_dma(sp, n)
        sp.dma_start(cst, a["cst"]).then_inc(S("ld_cst"), 16)
        load_chunk(sp, 1)
        load_chunk(sp, 2)
        sp.dma_start(x[:, 0, :], a["x_prompt"]).then_inc(S("ld_x"), 16)
        sp.dma_start(x[:, 1, :], a["x_sample"]).then_inc(S("ld_x"), 16)
        sp.dma_start(vec, a["vec"]).then_inc(S("ld_vec"), 16)
        sp.dma_start(wup, a["ev_w_up"]).then_inc(S("ld_up"), 16)
        sp.dma_start(aup, a["ev_a_up"]).then_inc(S("ld_up"), 16)
        sp.dma_start(gup, a["ev_g_up"]).then_inc(S("ld_up"), 16)
        sp.dma_start(S0, a["s0t"]).then_inc(S("ld_s0"), 16)
        for i in range(3, FIRST_OF_1 + 1):
            load_chunk(sp, i)
        for l in range(2):
            BK.wait_filled(sp, ("mix", l, 1, 1))
            sp.dma_start(rw, a["r_w"][l].rearrange("p (k n) -> p k n", k=KT)).then_inc(S("ld_rw"), 16)
            sp.wait_ge(S("x_new"), norm_no(l, 0, 1) + 1)
            sp.wait_ge(S(f"meta{l}"), 1)
            if l == 1:
                sp.wait_ge(S("cache_out"), 32)
            pairs, odd = (sp.value_load(meta[0:1, l, m:m + 1], min_val=lo, max_val=hi)
                          for m, lo, hi in ((0, 1, 10), (1, 0, 1)))
            def step(n, it, u):
                expert = [sp.value_load(meta[0:1, l, bass.ds(it * 4 + (2 * u + c + 4), 1)],
                                        min_val=0, max_val=NE - 1) for c in range(2)]
                for part, (lo, hi), done, each in (("gate_up", (0, 4096), "gu_done", 1), ("down", (4096, 6144), "down", 2)):
                    sp.wait_ge(S(f"{done}{l}"), (it * 2 + (u + 1)) * each)
                    for c in range(2):
                        sp.dma_start(EW[:, 2 * u + c, lo:hi],
                                     a["w_exp"][l, bass.ds(expert[c], 1), :, lo:hi].rearrange("e p n -> p (e n)"))\
                            .then_inc(S(f"{part}_loaded{l}_{u}"), 16)

            with sp.Fori(0, pairs) as it:
                for u in range(2):
                    step(it * 2 + u, it, u)
            with sp.If(odd):
                step(pairs * 2, pairs, 0)
            if l == 0:
                sp.wait_ge(S("x_new"), norm_no(0, 1, 1) + 1)
                sp.dma_start(CK, a["cache_k"]).then_inc(S("ld_cache"), 16)
                sp.dma_start(CV, a["cache_v"]).then_inc(S("ld_cache"), 16)
                for i in range(FIRST_OF_1 + 1, len(chunks)):
                    load_chunk(sp, i)

    @block.gpsimd
    def _(pool):
        def bias_load(n):
            BK.wait_drained(pool, MODS[n - 3])
            bias_dma(pool, n)

        pool.memset(raw, 0.0).then_inc(S("zeroed"), 1)
        pool.memset(glu, 0.0).then_inc(S("zeroed"), 1)
        pool.dma_start(w0b, a["ev_w0"].partition_broadcast(P)).then_inc(S("ld_w0"), 16)
        pool.dma_start(rope, a["rope"]).then_inc(S("ld_rope"), 16)
        for n in range(3, 7):
            bias_load(n)
        pool.wait_ge(S("ops"), 8)
        pool.wait_ge(S("prod"), 1)
        BK.wait_filled(pool, ("V", 1))
        pool.dma_start(cln, a["ev_cln"].partition_broadcast(P)).then_inc(S("ld_cln"), 16)
        pool.dma_start(gnp, a["ev_gn"].partition_broadcast(P)).then_inc(S("ld_gn"), 16)
        states = 0
        for n, (l, c) in enumerate(MOD_ORDER[7:], 7):
            bias_load(n)
            while states < 4 and BK.no[("st", states // 2, states % 2)] < BK.no[("mod", l, c)]:
                z, g = states // 2, states % 2
                BK.wait_drained(pool, ("st", z, g))
                pool.dma_start(o["state"][z, g::2].rearrange("h v k -> v h k"),
                               STS[0:HD, states % 2, :].rearrange("v (h k) -> v h k", h=4))\
                    .then_inc(S("state_out"), 16)
                states += 1

        def ln_load(l, w):
            n = l * 2 + w
            if n == 0:
                pool.wait_ge(S("conv"), CONV_W * AT)
                BK.wait_drained(pool, ("g", 1))
            else:
                pool.wait_ge(S("x_new"), 2 * n)
            pool.dma_start(lnp, a["ln"][n].partition_broadcast(P)).then_inc(S("ld_ln"), 16)

        ln_load(0, 0)
        for l in range(2):
            BK.wait_filled(pool, ("mix", l, 1, 1))
            pool.dma_start(rb, a["r_b"][l].partition_broadcast(P)).then_inc(S("ld_rb"), 16)
            ln_load(l, 1)
            if l == 0:
                ln_load(1, 0)
                pool.dma_start(subg, a["subln"].partition_broadcast(P)).then_inc(S("ld_sub"), 16)
                pool.dma_start(lqk, a["lqk"].partition_broadcast(P)).then_inc(S("ld_sub"), 16)
                BK.wait_drained(pool, ("qkv", 0, 3))
                pool.dma_start(o["cache_k"], QKV[:, 0, D:2 * D]).then_inc(S("cache_out"), 16)
                BK.wait_drained(pool, ("qkv", 0, 5))
                pool.dma_start(o["cache_v"], QKV[:, 0, 2 * D:3 * D]).then_inc(S("cache_out"), 16)
        for s in range(NS):
            pool.wait_ge(S("x_new"), norm_no(1, 1, s) + 1)
            pool.dma_start(o["y"][s], x[:, s, :]).then_inc(S("y_out"), 16)
        pool.wait_ge(S("state_out"), 64)
        pool.wait_ge(S("cache_out"), 32)
        pool.wait_ge(S("y_out"), 32)

    @block.tensor
    def _(pe):
        def mod(l, c):
            key = ("mod", l, c)
            wait_chunk(pe, key)
            BK.wait_free(pe, key)
            w, bank = slot(key), BK.bank(key)
            for k in range(KT):
                q = 32 * (k % 4)
                mm = pe.matmul(bank[q:q + 32, :], cond[:, k, :], w[:, k, :], start=(k < 4), stop=(k >= 4),
                               skip_group_check=True)
            mm.then_inc(filled, 1)

        def fold(l, c):
            part, half = c // 2, c % 2
            pick = cst[:, C_SEL:C_SEL + 2 * P:P]
            if part in (2, 5):
                key = ("gate", l, c)
                BK.wait_free(pe, key)
                BK.wait_drained(pe, ("mod", l, c))
                q = 32 * gate_slot(l, part)
                pe.matmul(BK.bank(key)[q:q + 2, :], pick, rowbuf[:, half * 512:half * 512 + 512], start=True, stop=True)\
                    .then_inc(filled, 1)
            elif half:
                key = ("modT", l, part)
                BK.wait_free(pe, key)
                BK.wait_drained(pe, ("mod", l, c))
                for k in range(KT):
                    mm = pe.matmul(BK.bank(key)[:, 2 * k:2 * k + 2], rowbuf[:, k * P:(k + 1) * P], pick,
                                   start=True, stop=True)
                mm.then_inc(filled, 1)

        def transposes(key, tiles, wait=None):
            BK.wait_free(pe, key)
            bank = BK.bank(key)
            for n, t in enumerate(tiles):
                mm = pe.transpose(bank[:, n * P:(n + 1) * P], t, ident)
            mm.then_inc(filled, 1)

        def x_transposes(tag):
            for s in range(NS):
                for h2 in range(2):
                    transposes(("xT", tag, s, h2), [x[:, s, (4 * h2 + n) * P:(4 * h2 + n + 1) * P] for n in range(4)])

        def wait_hT(tag):
            for h2 in range(2):
                BK.wait_drained(pe, ("xT", tag, 1, h2))

        def gate_rows(l, w):
            part = 2 if w == 0 else 5
            for s in range(NS):
                for n in range(2):
                    key = ("gbc", l, w, s, n)
                    BK.wait_free(pe, key)
                    if s == 0:
                        BK.wait_drained(pe, ("gate", l, 2 * part + n))
                    q = 32 * gate_slot(l, part)
                    pe.matmul(BK.bank(key), cst[q:q + 2, C_SEL + s * P:C_SEL + (s + 1) * P],
                              gaterow[q:q + 2, n * 512:(n + 1) * 512],
                              start=True, stop=True).then_inc(filled, 1)

        def project_out(l):
            for s in range(NS):
                for h2 in range(2):
                    BK.wait_drained(pe, ("oT", l, s, h2))
                for n in range(2):
                    key = ("mix", l, s, n)
                    if s == 0:
                        wait_chunk(pe, ("out", l, n))
                    BK.wait_free(pe, key)
                    for k in range(KT):
                        mm = pe.matmul(BK.bank(key), hT[:, k, s * T:(s + 1) * T], slot(("out", l, n))[:, k, :],
                                       start=(k == 0), stop=(k == KT - 1))
                    mm.then_inc(filled, 1)

        pe.wait_ge(S("cond"), 1)
        pe.wait_ge(S("ld_cst"), 16)
        for c in range(4):
            mod(0, c)
            fold(0, c)
        pe.wait_ge(S("ld_x"), 32)
        x_transposes("m0")
        wait_hT("m0")
        for key in PROJECTION:
            kind = key[0]
            if key == ("w", 0, 0):
                pe.wait_ge(S("ld_up"), 48)
                pe.wait_ge(S("lora"), 1)
            elif key == ("ss", 0):
                pe.wait_ge(S("sq"), 1)
            elif key == ("cum", 0, 0):
                pe.wait_ge(S("sigw"), 4)
            elif key == ("V", 0):
                pe.wait_ge(S("shifted"), NPA)
            elif kind == "bonus":
                pe.wait_ge(S("prod"), 1)
            if kind == "V":
                transposes(key, [V_[:, t, key[1] * T:(key[1] + 1) * T] for t in range(AT)])
                continue
            BK.wait_free(pe, key)
            bank = BK.bank(key)
            if kind in ("pa", "pb"):
                tiles = [key[1]] if kind == "pa" else [NPA + 2 * key[1], NPA + 2 * key[1] + 1]
                for n, i in enumerate(tiles):
                    wait_chunk(pe, ("evin", i // 4))
                    for k in range(KT):
                        mm = pe.matmul(bank[:, n * 256:n * 256 + 256],
                                       slot(("evin", i // 4))[:, k, (i % 4) * P:(i % 4 + 1) * P],
                                       hT[:, k, :], start=(k == 0), stop=(k == KT - 1))
            elif kind == "w":
                _, s, z = key
                mm = pe.matmul(bank, PA[64 * z:64 * z + 64, 0, s * T:(s + 1) * T], wup[64 * z:64 * z + 64, :],
                               start=True, stop=True)
            elif kind == "ss":
                mm = pe.matmul(bank, blk, sq[:, key[1] * 512:(key[1] + 1) * 512], start=True, stop=True)
            elif kind == "a":
                _, z, tp = key
                for t2 in range(2):
                    t = 2 * tp + t2
                    mm = pe.matmul(bank[:, t2 * 256:t2 * 256 + 256], aup[64 * z:64 * z + 64, t * P:(t + 1) * P],
                                   PA[64 * z:64 * z + 64, 1, :], start=True, stop=True)
            elif kind == "cum":
                _, z, t = key
                for s in range(NS):
                    mm = pe.matmul(bank[:, s * 130:s * 130 + 129], lw[:, s, z, t * P:(t + 1) * P],
                                   cst[:, C_CUM:C_CUM + T + 1], start=True, stop=True)
            else:
                for s in range(NS):
                    for t in range(AT):
                        mm = pe.matmul(bank[:, s * 8:s * 8 + 8], prod[:, t, s * T:(s + 1) * T],
                                       cst[:, C_HSEL + t * H:C_HSEL + (t + 1) * H], start=(t == 0), stop=(t == AT - 1))
            mm.then_inc(filled, 1)

        for (s, z) in PAIRS:
            pe.wait_ge(S("ops"), 4 * z + 4)
            for i in range(4):
                for g in range(2):
                    BK.wait_free(pe, ("gram", s, z, g, i))
                for c in range(2):
                    for g in range(2):
                        op = OPS[64 * g:64 * g + 64, z, i, s]
                        mm = pe.matmul(BK.bank(("gram", s, z, g, i))[:, c * 256:c * 256 + 256], op[:, 2 + c, :],
                                       op[:, 0:2, :], start=True, stop=True)
                        if c == 1:
                            mm.then_inc(filled, 1)
            for g in range(2):
                BK.wait_free(pe, ("L", s, z, g, 0))
            for i in range(4):
                for g in range(2):
                    op = OPS[64 * g:64 * g + 64, z, i, s]
                    mm = pe.matmul(BK.bank(("L", s, z, g, 0))[:, i * P:(i + 1) * P], op[:, 0, :], op[:, 2, :],
                                   start=True, stop=True)
                    if i == 3:
                        mm.then_inc(filled, 1)
            if s == 0 and z == 0:
                BK.wait_drained(pe, ("V", 1))
            if s == 1 and z == 0:
                pe.wait_ge(S("s0"), 1)
            for g in range(2):
                key = ("B", s, z, g)
                BK.wait_free(pe, key)
                BK.wait_drained(pe, ("gram", s, z, g, 3))
                for i in range(4):
                    h, t, b = 2 * i + g, i, 64 * g
                    dst = BK.bank(key)[:, i * HD:(i + 1) * HD]
                    mm = pe.matmul(dst, MAT[:, g, i, 2, :], VT[:, s, h * HD:(h + 1) * HD], start=True, stop=(s == 0))
                    if s == 1:
                        mm = pe.matmul(dst, OPS[b:b + 64, z, t, s, 0, :], S0[b:b + 64, z, t, :], start=False, stop=True)
                mm.then_inc(filled, 1)
            for j in range(LEVELS):
                for g in range(2):
                    lt = [MAT[:, g, i, 0, :] if j == 0 else LT[:, g, j % 2, i, :] for i in range(4)]
                    if j == 0:
                        BK.wait_drained(pe, ("B", s, z, g))
                        BK.wait_drained(pe, ("L", s, z, g, 0))
                    else:
                        BK.wait_drained(pe, ("LT", s, z, g, j))
                        BK.wait_drained(pe, ("X", s, z, g, j - 1))
                    key = ("X", s, z, g, j)
                    BK.wait_free(pe, key)
                    for i in range(4):
                        mm = pe.matmul(BK.bank(key)[:, i * HD:(i + 1) * HD], lt[i], XS[:, g, j % 2, i * HD:(i + 1) * HD],
                                       start=True, stop=True)
                    mm.then_inc(filled, 1)
                    if j < LEVELS - 1:
                        if j:
                            BK.wait_drained(pe, ("L", s, z, g, j))
                        key = ("L", s, z, g, j + 1)
                        BK.wait_free(pe, key)
                        for i in range(4):
                            mm = pe.matmul(BK.bank(key)[:, i * P:(i + 1) * P], lt[i], LS[:, g, j % 2, i, :],
                                           start=True, stop=True)
                        mm.then_inc(filled, 1)
                        key = ("LT", s, z, g, j + 1)
                        BK.wait_free(pe, key)
                        for i in range(4):
                            mm = pe.matmul(BK.bank(key)[:, i * P:(i + 1) * P], LS[:, g, j % 2, i, :], lt[i],
                                           start=True, stop=True)
                        mm.then_inc(filled, 1)
                    if g == 0 and (s, z, j) in fold_in:
                        fold(*fold_in[(s, z, j)])
                if (s, z, j) in mod_after:
                    mod(*mod_after[(s, z, j)])
            for g in range(2):
                BK.wait_drained(pe, ("X", s, z, g, LEVELS - 1))
                if s == 1 and (z or g):
                    pe.wait_ge(S("y_even"), z + 1) if g else pe.wait_ge(S("y_done"), 3)
                for i in range(4):
                    h, t, b = 2 * i + g, i, 64 * g
                    dst = ps[:, 6 + s, h * HD:(h + 1) * HD]
                    pe.matmul(dst, MAT[:, g, i, 1, :], XS[:, g, LEVELS % 2, i * HD:(i + 1) * HD],
                              start=(z == 0 and h == 0), stop=False, skip_group_check=True)
                    mm = pe.matmul(dst, MAT[:, g, i, 3, :], VT[:, s, h * HD:(h + 1) * HD],
                                   start=False, stop=(s == 0 and z == 1), skip_group_check=True)
                    if s == 1:
                        mm = pe.matmul(dst, OPS[b:b + 64, z, t, s, 1, :], S0[b:b + 64, z, t, :],
                                       start=False, stop=(z == 1), skip_group_check=True)
                if s == 1 and g == 0:
                    mm.then_inc(S("y_even"), 1)
            mm.then_inc(S("y_done"), 1)
            if s == 0:
                pe.wait_ge(S("fin"), z + 1)
                for g in range(2):
                    b = 64 * g
                    key = ("fT", z, g)
                    BK.wait_free(pe, key)
                    for i in range(4):
                        for c in range(2):
                            mm = pe.transpose(BK.bank(key)[:, (2 * i + c) * HD:(2 * i + c + 1) * HD],
                                              fint[b:b + 64, i, c, :], ident[b:b + 64, b:b + 64])
                    mm.then_inc(filled, 1)
                    key = ("st", z, g)
                    BK.wait_free(pe, key)
                    BK.wait_drained(pe, ("fT", z, g))
                    for i in range(4):
                        h, dst = 2 * i + g, BK.bank(key)[0:HD, i * HD:(i + 1) * HD]
                        pe.matmul(dst, XS[:, g, LEVELS % 2, i * HD:(i + 1) * HD], finq[:, g, i, 0, :],
                                  start=True, stop=False)
                        mm = pe.matmul(dst, VT[:, s, h * HD:(h + 1) * HD], finq[:, g, i, 1, :],
                                       start=False, stop=True)
                    mm.then_inc(filled, 1)
            if z == 1:
                key = ("g", s)
                BK.wait_free(pe, key)
                pe.wait_ge(S("lora"), 2)
                pe.matmul(BK.bank(key), PA[:, 2, s * T:(s + 1) * T], gup, start=True, stop=True).then_inc(filled, 1)

        for s in range(NS):
            pe.wait_ge(S("conv"), CONV_W * AT)
            transposes(("cT", s), [CONV[:, t, s * T:(s + 1) * T] for t in range(AT)])
        gate_rows(0, 0)
        for s in range(NS):
            for h2 in range(2):
                pe.wait_ge(S("mixed_a" if h2 == 0 else "mixed_b"), s + 1)
                src = VT if h2 == 0 else OB
                transposes(("oT", 0, s, h2), [src[:, s, t * P:(t + 1) * P] for t in range(AT)])
        project_out(0)

        def moe(l):
            for s in range(NS):
                pe.wait_ge(S("x_new"), norm_no(l, 0, s) + 1)
                for h2 in range(2):
                    transposes(("xT", f"e{l}", s, h2), [x[:, s, (4 * h2 + n) * P:(4 * h2 + n + 1) * P] for n in range(4)])
            wait_hT(f"e{l}")
            key = ("lg", l)
            BK.wait_free(pe, key)
            pe.wait_ge(S("ld_rw"), 16 * (l + 1))
            for s in range(NS):
                for k in range(KT):
                    mm = pe.matmul(BK.bank(key)[:, s * 64:s * 64 + 36], hT[:, k, s * T:(s + 1) * T], rw[:, k, :],
                                   start=(k == 0), stop=(k == KT - 1))
            mm.then_inc(filled, 1)
            for s in range(NS):
                for h2 in range(2):
                    transposes(("hb", l, s, h2), [hT[:, 4 * h2 + n, s * T:(s + 1) * T] for n in range(4)])
            gate_rows(l, 1)
            key = ("pos", l)
            BK.wait_free(pe, key)
            pe.wait_ge(S("chosen"), l + 1)
            bank, OH = BK.bank(key), rt_[:, R_OH:R_OH + 64]
            pe.matmul(bank[:, 0:32], SU, OH[:, 0:32], start=True, stop=True)
            pe.matmul(bank[:, 32:64], SU, OH[:, 32:64], start=True, stop=False)
            pe.matmul(bank[:, 32:64], ones, OH[:, 0:32], start=False, stop=True)
            pe.matmul(bank[0:32, 64:65], OH[:, 0:32], ones[:, 0:1], start=True, stop=False)
            pe.matmul(bank[0:32, 64:65], OH[:, 32:64], ones[:, 0:1], start=False, stop=True).then_inc(filled, 1)
            key = ("base", l)
            BK.wait_free(pe, key)
            pe.wait_ge(S("nchunks"), l + 1)
            bank, nb = BK.bank(key), rt_[0:32, R_NB:R_NB + P]
            pe.matmul(bank[:, 0:32], nb, SU[0:32, 0:32], start=True, stop=True)
            pe.matmul(bank[:, 32:33], nb, ones[0:32, 0:1], start=True, stop=True)
            pe.matmul(bank[0:32, 64:65], UI[0:32, 0:32], nb[:, 0:1], start=True, stop=True).then_inc(filled, 1)
            key = ("eid", l)
            BK.wait_free(pe, key)
            pe.wait_ge(S("ended"), l + 1)
            pe.matmul(BK.bank(key)[0:1, 0:40], ones[0:32, 0:1], rt_[0:32, R_CMP:R_CMP + 40], start=True, stop=True)\
                .then_inc(filled, 1)
            BK.wait_drained(pe, ("eid", l))
            BK.wait_drained(pe, ("gbc", l, 1, 1, 1))
            pe.wait_ge(S("zero"), l + 1)
            for n in range(4):
                mm = pe.matmul(ps[:, n, :], rt_[:, R_ZERO:R_ZERO + P], cst[:, 0:512], start=True, stop=False,
                               skip_group_check=True)
                if n == 0:
                    mm.then_inc(S(f"gu_done{l}"), 2)
                elif n == 1:
                    mm.then_inc(S(f"down{l}"), 4)

            def gather(n):
                pe.wait_ge(S(f"selected{l}"), n + 1)
                for k in range(KT):
                    for s in range(NS):
                        mm = pe.matmul(ps[:, 4 + k // 4, (k % 4) * P:(k % 4 + 1) * P], hb[:, s, k * P:(k + 1) * P],
                                       sel[:, s, :], start=(s == 0), stop=(s == 1))
                    if k % 4 == 3:
                        mm.then_inc(S(f"gathered{l}"), 1)

            def scatter(n, u, last=False):
                pe.wait_ge(S(f"y_read{l}"), n + 2)
                pe.wait_ge(S(f"y_read_dve{l}"), n + 2)
                for s in range(NS):
                    for half in range(2):
                        mm = pe.matmul(ps[:, 2 * s + half, :], tT[u][:, (2 + s) * P:(3 + s) * P],
                                       ysb[:, half * 512:(half + 1) * 512], start=False, stop=last,
                                       skip_group_check=True)
                return mm

            gather(0)
            pe.wait_ge(S(f"meta{l}"), 1)
            pairs, odd, even = (pe.value_load(meta[0:1, l, m:m + 1], min_val=lo, max_val=hi)
                                for m, lo, hi in ((0, 1, 10), (1, 0, 1), (2, 0, 1)))
            def step(n, it, u):
                pe.wait_ge(S(f"xg_act{l}"), n + 1)
                pe.wait_ge(S(f"xg_dve{l}"), n + 1)
                pe.wait_ge(S(f"gate_up_loaded{l}_{u}"), it * 32 + 32)
                for k in range(KT):
                    for c in range(2):
                        mm = pe.matmul(ps[64 * c:64 * c + 64, 6, :], xg[:, k, 64 * c:64 * c + 64],
                                       EW[:, 2 * u + c, k * 512:(k + 1) * 512],
                                       start=(k == 0), stop=(k == KT - 1), skip_group_check=True)
                mm.then_inc(S(f"gu_done{l}"), 1)
                pe.wait_ge(S(f"y_read{l}"), n + 1)
                pe.wait_ge(S(f"y_read_dve{l}"), n + 1)
                gather(n + 1)
                pe.wait_ge(S(f"gates{l}"), n + 1)
                for s in range(NS):
                    pe.transpose(ps[:, 7, (2 + s) * P:(3 + s) * P], gsel[:, 0, s, :], ident)
                pe.wait_ge(S(f"hid{l}"), n + 1)
                for f in range(2):
                    mm = pe.transpose(ps[:, 7, f * P:(f + 1) * P], hid[:, 1, f * P:(f + 1) * P], ident)
                mm.then_inc(S(f"turned{l}"), 1)
                scatter(n - 1, 1 - u)
                pe.wait_ge(S(f"tT{l}"), n + 1)
                pe.wait_ge(S(f"xg_act{l}"), n + 2)
                pe.wait_ge(S(f"xg_dve{l}"), n + 2)
                pe.wait_ge(S(f"down_loaded{l}_{u}"), it * 32 + 32)
                for half in range(2):
                    for f in range(2):
                        for c in range(2):
                            w = EW[:, 2 * u + c, 4096 + f * D + half * 512:4096 + f * D + half * 512 + 512]
                            mm = pe.matmul(ps[64 * c:64 * c + 64, 4 + half, :],
                                           tT[u][:, f * P + 64 * c:f * P + 64 * c + 64], w,
                                           start=(f == 0), stop=(f == 1), skip_group_check=True)
                    mm.then_inc(S(f"down{l}"), 1)

            with pe.Fori(0, pairs) as it:
                for u in range(2):
                    step(it * 2 + u, it, u)
            with pe.If(odd):
                step(pairs * 2, pairs, 0)
                scatter(pairs * 2, 0, last=True).then_inc(S("summed"), 1)
            with pe.If(even):
                scatter(pairs * 2 - 1, 1, last=True).then_inc(S("summed"), 1)

        moe(0)

        for s in range(NS):
            pe.wait_ge(S("x_new"), norm_no(0, 1, s) + 1)
            for h2 in range(2):
                transposes(("xT", "m1", s, h2), [x[:, s, (4 * h2 + n) * P:(4 * h2 + n + 1) * P] for n in range(4)])
        wait_hT("m1")
        for c in range(6):
            wait_chunk(pe, ("odin", c))
            for s in range(NS):
                key = ("qkv", s, c)
                BK.wait_free(pe, key)
                for k in range(KT):
                    mm = pe.matmul(BK.bank(key), hT[:, k, s * T:(s + 1) * T], slot(("odin", c))[:, k, :],
                                   start=(k == 0), stop=(k == KT - 1))
                mm.then_inc(filled, 1)
        pe.wait_ge(S("ld_cache"), 32)
        for h2 in range(2):
            transposes(("cT1", h2), [CK[:, (4 * h2 + n) * P:(4 * h2 + n + 1) * P] for n in range(4)])
        for s in range(NS):
            for q in range(2):
                if s == 0:
                    BK.wait_drained(pe, ("qkv", 0, 2 * q + 1))
                else:
                    pe.wait_ge(S("roped"), q + 1)
                src = QKV[:, 0, q * D:(q + 1) * D] if s == 0 else QR[:, q, :]
                for h2 in range(2):
                    transposes(("qkT", s, q, h2), [src[:, (4 * h2 + n) * P:(4 * h2 + n + 1) * P] for n in range(4)])
        for n in range(len(PAIRS1) + 1):
            if n < len(PAIRS1):
                s, hp = PAIRS1[n]
                BK.wait_drained(pe, ("qkT", s, 1, hp // 2))
                for z in range(2):
                    key = ("sc", s, hp, z)
                    BK.wait_free(pe, key)
                    for m in range(2):
                        h = 2 * hp + m
                        keys = KTp[64 * z:64 * z + 64, h, :] if s == 0 else KTs[64 * z:64 * z + 64, h, :]
                        mm = pe.matmul(BK.bank(key)[:, m * 256:m * 256 + T * (s + 1)], QT[64 * z:64 * z + 64, s, h, :],
                                       keys, start=True, stop=True)
                    mm.then_inc(filled, 1)
            if n >= 1:
                s, hp = PAIRS1[n - 1]
                b = (n - 1) % 2
                pe.wait_ge(S("attn"), 2 * n)
                transposes(("aT", s, hp), [AB[:, b, m, i * P:(i + 1) * P] for m in range(2) for i in range(s + 1)])
                if n % 2 == 0:
                    key = ("pv", s, hp // 2)
                    BK.wait_free(pe, key)
                    BK.wait_drained(pe, ("aT", s, hp))
                    for m in range(4):
                        hh = 2 * hp - 2 + m
                        for i in range(s + 1):
                            own_v = QKV[:, s, 2 * D + hh * P:2 * D + (hh + 1) * P]
                            vals = CV[:, hh * P:(hh + 1) * P] if (s, i) == (1, 0) else own_v
                            at = (m % 2) * (s + 1) + i
                            mm = pe.matmul(BK.bank(key)[:, m * P:(m + 1) * P], ATb[:, m // 2, at * P:(at + 1) * P], vals,
                                           start=(i == 0), stop=(i == s))
                    mm.then_inc(filled, 1)
        gate_rows(1, 0)
        for s in range(NS):
            pe.wait_ge(S("attended"), s + 1)
            for h2 in range(2):
                transposes(("oT", 1, s, h2), [OO[:, s, (4 * h2 + n) * P:(4 * h2 + n + 1) * P] for n in range(4)])
        project_out(1)
        moe(1)


    @block.scalar
    def _(act):
        A = nc.scalar.activation
        own = Steps(act, S("act_steps"))

        def take(key):
            BK.wait_filled(act, key)
            return BK.bank(key)

        def copy(key, out, n=512):
            BK.drained_by(A(out, take(key)[:, 0:n], ACT.Copy), key)

        def modulated(key, s, k0, l, part):
            bank = take(key)
            BK.wait_drained(act, ("modT", l, part + 1))
            for n in range(4):
                k = k0 + n
                ins = A(hT[:, k, s * T:(s + 1) * T], bank[:, n * P:(n + 1) * P], ACT.Identity,
                        bias=modT[:, l, part, k, s:s + 1], scale=modT[:, l, part + 1, k, s:s + 1])
            BK.drained_by(ins, key)

        def rsqrt(out, src, ready, n, done):
            act.wait_ge(S(ready), n)
            own.link(A(out, src, ACT.Ln))
            A(out, out, ACT.Exp, scale=-0.5).then_inc(S(done), 1)

        def gate_row(l, c):
            part, half = c // 2, c % 2
            if part in (2, 5):
                key, q = ("gate", l, c), 32 * gate_slot(l, part)
                BK.drained_by(A(gaterow[q:q + 2, half * 512:half * 512 + 512], take(key)[q:q + 2, :], ACT.Copy), key)

        def gate_rows(l, w):
            for s in range(NS):
                for n in range(2):
                    if s == 0 and n == 0 and w == 0 and l == 0:
                        act.wait_ge(S("convT"), 2)
                        act.wait_ge(S("mixed_a"), 2)
                    copy(("gbc", l, w, s, n), gbc[:, s, n * 512:(n + 1) * 512])

        act.wait_ge(S("ld_cond"), 16)
        A(condw[:, 0:16], condw[:, 32:48], ACT.Exp, scale=-1.0).then_inc(S("cond_exp"), 1)
        for s in range(NS):
            modulated(("xT", "m0", s, 0), s, 0, 0, 0)
        act.wait_ge(S("zeroed"), 1)
        act.wait_ge(S("vecs"), 1)
        def projected(i):
            key = ("pa", i)
            bank = take(key)
            if i >= 4:
                act.wait_ge(S("shifted"), i - 3)
            A(raw[:, i % 4, :, 1:129], bank[:, 0:256].rearrange("p (s n) -> p s n", s=NS), ACT.Copy)\
                .then_inc(S("act_raw"), 1)
            BK.drained_by(A(PA[:, i, :], bank[:, 0:256], ACT.Copy, scale=nvec[:, TILES[i]:TILES[i] + 1]), key)
            if i == 4:
                act.wait_ge(S("shifted"), 1)
                A(PA[:, 0, :], PA[:, 0, :], ACT.Exp, scale=-2.0).then_inc(S("lora_exp"), 1)
                act.wait_ge(S("shifted"), 3)
                A(PA[:, 2, :], PA[:, 2, :], ACT.Exp, scale=-1.0).then_inc(S("lora_exp"), 1)
            if i == 10:
                act.wait_ge(S("kk"), 1)
                A(sq, KK.rearrange("p t n -> p (t n)"), ACT.Square).then_inc(S("sq"), 1)

        def halved(t):
            bank = take(("pb", t))
            if t >= 2:
                BK.wait_drained(act, ("pb", t - 2))
            A(eg[:, t % 2, :], bank[:, 256:512], ACT.Exp, bias=nvec[:, 38 + 4 + t:39 + 4 + t], scale=-1.0)\
                .then_inc(S("eg"), 1)

        def decay(s, z):
            BK.wait_drained(act, ("w", s, z))
            A(lw[:, s, z, :], lw[:, s, z, :], ACT.Exp, scale=-1.0).then_inc(S("lw_exp"), 1)

        def key_norms():
            BK.wait_drained(act, ("ss", 1))
            own.link(A(sq, sq, ACT.Ln, scale=float(2 ** 32)))
            A(sq, sq, ACT.Exp, scale=-0.5).then_inc(S("rs"), 1)

        def learning_rate(z, tp):
            bank = take(("a", z, tp))
            for t2 in range(2):
                t = 2 * tp + t2
                ins = A(Ab[:, z, t, :], bank[:, t2 * 256:t2 * 256 + 256], ACT.Exp,
                        bias=nvec[:, 30 + 4 * z + t:31 + 4 * z + t], scale=-1.0)
            BK.drained_by(ins, ("a", z, tp))

        def decays(z, t):
            bank = take(("cum", z, t))
            act.wait_ge(S("centres"), z * AT + t + 1)
            for s in range(NS):
                own.inc(A(FG[:, 0, z, t, s, :], bank[:, s * 130:s * 130 + 129], ACT.Exp, bias=cb[:, 0, z, t, s:s + 1]))
                ins = A(FG[:, 1, z, t, s, :], bank[:, s * 130:s * 130 + 129], ACT.Exp,
                        bias=cb[:, 1, z, t, s:s + 1], scale=-1.0)
                if s == 0:
                    own.inc(ins)
            BK.drained_by(ins, ("cum", z, t))

        for i in range(11):
            projected(i)
        decay(0, 0)
        decay(0, 1)
        projected(11)
        decay(1, 0)
        decay(1, 1)
        projected(12)
        projected(13)
        for tp in range(2):
            learning_rate(0, tp)
        projected(14)
        key_norms()
        for tp in range(2):
            learning_rate(1, tp)
        for z in range(2):
            halved(z)
            for t in range(AT):
                decays(z, t)
        for s in range(NS):
            copy(("V", s), VT[:, s, :])
        for t in range(2, AT):
            halved(t)

        for (s, z) in PAIRS:
            for g in range(2):
                copy(("B", s, z, g), XS[:, g, 0, :], 256)
            for j in range(LEVELS - 1):
                for g in range(2):
                    copy(("L", s, z, g, j + 1), LS[:, g, (j + 1) % 2].rearrange("p i n -> p (i n)"))
                    if g == 0 and (s, z, j) in fold_in:
                        gate_row(*fold_in[(s, z, j)])
            if s == 0:
                for g in range(2):
                    copy(("fT", z, g), finq[:, g].rearrange("p t c n -> p (t c n)"))
                    key = ("st", z, g)
                    bank = take(key)
                    if z == 1:
                        act.wait_ge(S("state_out"), 16 * (g + 1)) if g == 1 else act.wait_ge(S("state_out"), 16)
                    if z == 1 and g == 0:
                        act.wait_ge(S("state_out"), 32)
                    BK.drained_by(A(STS[0:HD, g, :], bank[0:HD, 0:256], ACT.Copy), key)
            if z == 1:
                rsqrt(st8[:, 16:24], st8[:, 8:16], "gn_var", s + 1, "gn_rstd")
        for s in range(NS):
            rsqrt(st8[:, 32 + s:33 + s], st8[:, 34 + s:35 + s], "cln_var", s + 1, "cln_rstd")
            act.wait_ge(S("cln_y"), s + 1)
            A(tb, tb, ACT.Exp, scale=-1.0).then_inc(S("cln_exp"), 1)

        def norm_rsqrt(l, w, s):
            n = norm_no(l, w, s)
            rsqrt(lns[:, 8 + s:9 + s], lns[:, 4 + s:5 + s], "ln_var", n + 1, "ln_rstd")

        gate_rows(0, 0)
        for s in range(NS):
            copy3(act, BK, ("oT", 0, s, 0), hT, s, 0)
        for s in range(NS):
            norm_rsqrt(0, 0, s)

        def moe(l):
            for s in range(NS):
                modulated(("xT", f"e{l}", s, 0), s, 0, l, 3)
            act.wait_ge(S("routed1"), l + 1)
            A(rt_[:, R_EX:R_EX + 8], rt_[:, R_EX:R_EX + 8], ACT.Exp).then_inc(S("route_exp"), 1)
            for s in range(NS):
                for h2 in range(2):
                    copy(("hb", l, s, h2), hb[:, s, h2 * 512:(h2 + 1) * 512])
            act.wait_ge(S("routed2"), l + 1)
            A(rt_[:, R_S + 16:R_S + 18], rt_[:, R_S + 16:R_S + 18], ACT.Exp).then_inc(S("route_exp"), 1)
            gate_rows(l, 1)
            act.wait_ge(S(f"meta{l}"), 1)
            pairs, odd = (act.value_load(meta[0:1, l, m:m + 1], min_val=lo, max_val=hi)
                          for m, lo, hi in ((0, 1, 10), (1, 0, 1)))
            act.sem_inc(S(f"y_read{l}"), 1)

            def gathered(n):
                act.wait_ge(S(f"gathered{l}"), n * 2 + 1)
                A(xg[:, 0:4, :].rearrange("p k n -> p (k n)"), ps[:, 4, :], ACT.Copy).then_inc(S(f"xg_act{l}"), 1)

            gathered(0)
            def step(n, it, u):
                act.wait_ge(S(f"gu_done{l}"), n + 3)
                A(hid[:, 0, :], ps[:, 6, 0:256], ACT.Exp, scale=-1.0).then_inc(S(f"gate_exp{l}"), 1)
                gathered(n + 1)
                act.wait_ge(S(f"turned{l}"), n + 1)
                A(tT[u], ps[:, 7, :], ACT.Copy).then_inc(S(f"tT{l}"), 1)
                act.wait_ge(S(f"down{l}"), n * 2 + 5)
                A(ysb[:, 0:512], ps[:, 4, :], ACT.Copy).then_inc(S(f"y_read{l}"), 1)

            with act.Fori(0, pairs) as it:
                for u in range(2):
                    step(it * 2 + u, it, u)
            with act.If(odd):
                step(pairs * 2, pairs, 0)
            for s in range(NS):
                norm_rsqrt(l, 1, s)

        moe(0)

        for s in range(NS):
            modulated(("xT", "m1", s, 0), s, 0, 1, 0)
        for c in range(6):
            for s in range(NS):
                copy(("qkv", s, c), QKV[:, s, c * 512:(c + 1) * 512])
        act.wait_ge(S("lam_dot"), 1)
        A(lam[:, 2:4], lam[:, 0:2], ACT.Exp).then_inc(S("lam_exp"), 1)

        def keys_out(key, dst):
            BK.drained_by(A(dst, take(key).rearrange("p (h n) -> p h n", h=4), ACT.Copy), key)

        for h2 in range(2):
            keys_out(("cT1", h2), KTs[:, 4 * h2:4 * h2 + 4, 0:P])
        for s in range(NS):
            for q in range(2):
                for h2 in range(2):
                    hs = slice(4 * h2, 4 * h2 + 4)
                    dst = QT[:, s, hs, :] if q == 0 else (KTp[:, hs, :] if s == 0 else KTs[:, hs, P:2 * P])
                    keys_out(("qkT", s, q, h2), dst)
        for n in range(len(PAIRS1) + 1):
            if n < len(PAIRS1):
                s, hp = PAIRS1[n]
                nk = T * (s + 1)
                for z in range(2):
                    bank = take(("sc", s, hp, z))
                    act.wait_ge(S("smax"), 2 * n + z + 1)
                    if n >= 2:
                        act.wait_ge(S("attn"), 2 * n - 2)
                    for m in range(2):
                        ins = A(PB[:, n % 2, z, m, 0:nk], bank[:, m * 256:m * 256 + nk], ACT.Exp,
                                bias=sm1[:, n % 4, 4 + 2 * z + m:5 + 2 * z + m], scale=HD ** -0.5,
                                accum_out=sm1[:, n % 4, 8 + 2 * z + m:9 + 2 * z + m])
                        if m == 0:
                            own.inc(ins)
                    BK.drained_by(ins, ("sc", s, hp, z))
            if n >= 1:
                s, hp = PAIRS1[n - 1]
                b = (n - 1) % 2
                if n >= 3:
                    BK.wait_filled(act, ("pv", PAIRS1[n - 3][0], PAIRS1[n - 3][1] // 2))
                w = 2 * T * (s + 1)
                BK.drained_by(A(ATb[:, b, 0:w], take(("aT", s, hp))[:, 0:w], ACT.Copy), ("aT", s, hp))
        gate_rows(1, 0)
        for s in range(NS):
            rsqrt(st8[:, 16:24], st8[:, 8:16], "at_var", s + 1, "at_rstd")
            copy3(act, BK, ("oT", 1, s, 0), hT, s, 0)
        for s in range(NS):
            norm_rsqrt(1, 0, s)
        moe(1)

    @block.vector
    def _(dve):
        V = nc.vector
        TT, TS, STT = V.tensor_tensor, V.tensor_scalar, V.scalar_tensor_tensor
        own = Steps(dve, S("dve_steps"))
        mods = [0]

        def take(key):
            BK.wait_filled(dve, key)
            return BK.bank(key)

        def sig(ins, name):
            ins.then_inc(S(name), 1)

        def mod(l, c):
            n = mods[0]
            mods[0] += 1
            part, half = c // 2, c % 2
            bank = take(("mod", l, c))
            if n < 3:
                dve.wait_ge(S("ld_mbias_first"), 48)
            else:
                dve.wait_ge(S(f"ld_mbias{n % 3}"), 16 * (n // 3))
            dst = rowbuf[:, half * 512:half * 512 + 512]
            BK.drained_by(TT(dst, bank, mbias[:, n % 3, :], ALU.add), ("mod", l, c))

        def fold(l, c):
            part = c // 2
            if c % 2 and part not in (2, 5):
                key = ("modT", l, part)
                src = take(key)[:, 0:16]
                dst = modT[:, l, part].rearrange("p k s -> p (k s)")
                BK.drained_by(TS(dst, src, 1.0 if part in (1, 4) else 0.0, None, ALU.add), key)

        def modulated(key, s, k0, l, part):
            bank = take(key)
            BK.wait_drained(dve, ("modT", l, part + 1))
            for n in range(4):
                k = k0 + n
                ins = TS(hT[:, k, s * T:(s + 1) * T], bank[:, n * P:(n + 1) * P], modT[:, l, part + 1, k, s:s + 1],
                         modT[:, l, part, k, s:s + 1], ALU.mult, ALU.add)
            BK.drained_by(ins, key)

        def layer_norm(l, w, s, z, src):
            n = norm_no(l, w, s)
            if n == 0 or s == 0:
                BK.wait_drained(dve, ("gbc", l, w, 1, 1))
            for half in range(2):
                ins = TT(z[:, s, half * 512:(half + 1) * 512], gbc[:, s, half * 512:(half + 1) * 512], src(half), ALU.mult)
                if w == 0:
                    BK.drained_by(ins, ("mix", l, s, half))
                    BK.wait_drained(dve, ("mix", l, s, half))
                else:
                    own.link(ins)
            own.link(STT(z[:, s, :], x[:, s, :], ALPHA, z[:, s, :], ALU.mult, ALU.add))
            for half in range(2):
                own.inc(V.bn_stats(bns[:, half * 6:half * 6 + 6], z[:, s, half * 512:(half + 1) * 512]))
            own.wait()
            own.link(V.bn_aggr(lns[:, 0:2], bns[:, 0:12].rearrange("p (n c) -> p n c", c=6)))
            sig(TS(lns[:, 4 + s:5 + s], lns[:, 1:2], LN_EPS, None, ALU.add), "ln_var")
            dve.wait_ge(S("ln_rstd"), n + 1)
            own.link(TS(z[:, s, :], z[:, s, :], lns[:, 0:1], lns[:, 8 + s:9 + s], ALU.subtract, ALU.mult))
            dve.wait_ge(S("ld_ln"), 16 * (l * 2 + w + 1))
            own.link(TT(z[:, s, :], z[:, s, :], lnp[:, 0, :], ALU.mult))
            sig(TT(x[:, s, :], z[:, s, :], lnp[:, 1, :], ALU.add), "x_new")
            dve.wait_ge(S("x_new"), n + 1)

        V.memset(mbias, 0.0).then_inc(S("mbias_zero"), 1)
        dve.wait_ge(S("cond_exp"), 1)
        cw = condw[:, 0:16]
        own.link(TS(cw, cw, 1.0, None, ALU.add))
        own.link(V.reciprocal(condw[:, 16:32], cw))
        own.link(V.memset(cond, 0.0))
        pairs = lambda at: condw[:, at:at + 16].rearrange("p (k s) -> p k s", s=NS)
        sig(TT(cond[:, :, 0:NS], pairs(32), pairs(16), ALU.mult), "cond")
        for c in range(2):
            mod(0, c)
            fold(0, c)
        dve.wait_ge(S("ld_vec"), 16)
        own.inc(TS(nvec[:, 0:15], vec[:, V_MU:V_MU + 15], -1.0, 1.0, ALU.mult, ALU.add))
        own.inc(TS(nvec[:, 15:30], vec[:, V_MU:V_MU + 15], 0.5, None, ALU.mult))
        own.inc(TS(nvec[:, 30:38], vec[:, V_A0:V_A0 + 8], -1.0, None, ALU.mult))
        own.inc(TS(nvec[:, 38:46], vec[:, V_PW:V_PW + 8], -1.0, None, ALU.mult))
        sig(TS(nvec[:, 46:50], vec[:, V_KA:V_KA + 4], -1.0, 1.0, ALU.mult, ALU.add), "vecs")
        dve.wait_ge(S("vecs"), 1)
        for c in range(2, 4):
            mod(0, c)
            fold(0, c)
        for s in range(NS):
            modulated(("xT", "m0", s, 1), s, 4, 0, 0)

        def shifted(i):
            BK.wait_drained(dve, ("pa", i))
            nb = nbr[:, i % 2, :].rearrange("p (s n) -> p s n", s=NS)
            own.link(TT(nb, raw[:, i % 4, :, 0:128], raw[:, i % 4, :, 2:130], ALU.add))
            m = 15 + TILES[i]
            sig(STT(PA[:, i, :], nbr[:, i % 2, :], nvec[:, m:m + 1], PA[:, i, :], ALU.mult, ALU.add), "shifted")
            if i == 6:
                dve.wait_ge(S("lora_exp"), 2)
                for q in (0, 2):
                    own.link(TS(PA[:, q, :], PA[:, q, :], 1.0, None, ALU.add))
                    if q == 0:
                        own.link(V.reciprocal(PA[:, 0, :], PA[:, 0, :]))
                        sig(TS(PA[:, 0, :], PA[:, 0, :], 2.0, -1.0, ALU.mult, ALU.add), "lora")
                    else:
                        sig(V.reciprocal(PA[:, 2, :], PA[:, 2, :]), "lora")
                dve.wait_ge(S("shifted"), 7)
                for t in range(AT):
                    ins = TS(KK[:, t, :], K_[:, t, :], vec[:, V_KK + t:V_KK + t + 1], None, ALU.mult)
                    if t < AT - 1:
                        own.inc(ins)
                sig(ins, "kk")

        def gated(t):
            bank = take(("pb", t))
            dve.wait_ge(S("eg"), t + 1)
            e = eg[:, t % 2, :]
            own.link(TS(e, e, 1.0, None, ALU.add))
            own.link(V.reciprocal(e, e))
            dve.wait_ge(S("zeroed"), 2)
            ins = STT(glu[:, t, :, PADC:PADC + T], bank[:, 0:256].rearrange("p (s n) -> p s n", s=NS),
                      vec[:, V_PW + t:V_PW + t + 1], e.rearrange("p (s n) -> p s n", s=NS), ALU.add, ALU.mult)
            BK.drained_by(ins, ("pb", t))


        def add_w0(s, z):
            BK.drained_by(TT(lw[:, s, z, :], take(("w", s, z)), w0b[:, z, :], ALU.add), ("w", s, z))

        def decay(n):
            s, z = n // 2, n % 2
            dve.wait_ge(S("lw_exp"), n + 1)
            own.link(TS(lw[:, s, z, :], lw[:, s, z, :], 1.0, None, ALU.add))
            sig(V.reciprocal(lw[:, s, z, :], lw[:, s, z, :]), "sigw")

        def learning_rate(z):
            BK.wait_drained(dve, ("a", z, 1))
            az = Ab[:, z].rearrange("p t n -> p (t n)")
            own.link(TS(az, az, 1.0, None, ALU.add))
            own.link(V.reciprocal(az, az))

        def centres(z):
            for t in range(AT):
                bank = take(("cum", z, t))
                mid = bank[:, 0:260].rearrange("p (s n) -> p s n", s=NS)[:, :, 64:65].rearrange("p s n -> p (s n)")
                own.inc(TS(cb[:, 0, z, t, :], mid, -1.0, None, ALU.mult))
                sig(TS(cb[:, 1, z, t, :], mid, 1.0, None, ALU.mult), "centres")

        flat = lambda v: v.rearrange("p t n -> p (t n)")

        def keys(z):
            for t in range(AT):
                own.inc(TS(KZ[:, z, t, :], Ab[:, z, t, :], vec[:, V_KA + t:V_KA + t + 1], nvec[:, 46 + t:47 + t],
                           ALU.mult, ALU.add))
            own.wait()
            own.inc(TT(flat(KZ[:, z]), flat(KZ[:, z]), flat(K_), ALU.mult))
            own.link(STT(flat(Ab[:, z]), flat(KK), -1.0, flat(Ab[:, z]), ALU.mult, ALU.mult))

        for i in range(11):
            shifted(i)
        dve.wait_ge(S("ld_w0"), 16)
        add_w0(0, 0)
        add_w0(0, 1)
        decay(0)
        shifted(11)
        add_w0(1, 0)
        decay(1)
        add_w0(1, 1)
        shifted(12)
        decay(2)
        for tp in range(2):
            bank = take(("ss", tp))
            if tp == 0:
                BK.wait_filled(dve, ("ss", 1))
            BK.drained_by(TS(sq[:, tp * 512:(tp + 1) * 512], bank, 1e-24, None, ALU.max), ("ss", tp))
        shifted(13)
        decay(3)
        shifted(14)
        dve.wait_ge(S("rs"), 1)
        own.link(STT(flat(KK), flat(KK), float(2 ** 16), sq, ALU.mult, ALU.mult))
        gated(0)
        learning_rate(0)
        centres(0)
        gated(1)
        keys(0)
        centres(1)
        learning_rate(1)
        keys(1)
        own.link(TT(flat(prod), flat(KZ[:, 0]), flat(KZ[:, 1]), ALU.add))
        for t in range(AT):
            ins = STT(prod[:, t, :], R_[:, t, :], vec[:, V_RK + t:V_RK + t + 1], prod[:, t, :], ALU.mult, ALU.mult)
            if t < AT - 1:
                own.inc(ins)
        sig(ins, "prod")
        for t in range(2, AT):
            gated(t)
        BK.wait_drained(dve, ("cum", 1, 3))
        for z in range(2):
            for s in range(NS):
                f, at0 = (1, 0) if (z == 0) == (s == 1) else (0, 128)
                own.inc(V.tensor_copy(fsc[:, z, :, s], FG[:, f, z, :, s, at0]))
        BK.wait_drained(dve, ("pb", AT - 1))
        BK.wait_filled(dve, ("cum", 1, 3))
        for z in range(2):
            up, dn = ((0, slice(1, 129)), (1, slice(1, 129))) if z == 0 else ((1, slice(0, 128)), (0, slice(0, 128)))
            pre = (0, slice(0, 128)) if z == 0 else (1, slice(1, 129))
            for c, (src, (f, r)) in enumerate([(KK, pre), (R_, up), (Ab[:, z], dn), (KZ[:, z], dn)]):
                out = OPS[:, z, :, :, c, :].rearrange("p t s n -> p (t s) n")
                sig(TT(out, src.rearrange("p t (s n) -> p (t s) n", s=NS),
                       FG[:, f, z, :, :, r].rearrange("p t s n -> p (t s) n"), ALU.mult), "ops")
        dve.wait_ge(S("ops"), 8)
        dve.wait_ge(S("ld_s0"), 16)
        for z in range(2):
            for t in range(AT):
                ins = TS(S0[:, z, t, :], S0[:, z, t, :], fsc[:, z, t, 1:2], None, ALU.mult)
                if (z, t) != (1, 3):
                    own.inc(ins)
        sig(ins, "s0")
        BK.drained_by(V.tensor_copy(bon, take(("bonus",))[:, 0:16]), ("bonus",))
        BK.wait_drained(dve, ("bonus",))

        taps = [0]

        def conv(n):
            for _ in range(n):
                if taps[0] == CONV_W * AT:
                    return
                j, t = divmod(taps[0], AT)
                src, w = glu[:, t, :, j:j + T], vec[:, V_DW + j * AT + t:V_DW + j * AT + t + 1]
                out = CONV[:, t, :].rearrange("p (s n) -> p s n", s=NS)
                if j == 0:
                    ins = TS(out, src, w, vec[:, V_DB + t:V_DB + t + 1], ALU.mult, ALU.add)
                else:
                    dve.wait_ge(S("conv"), taps[0] - AT + 1)
                    ins = STT(out, src, w, out, ALU.mult, ALU.add)
                sig(ins, "conv")
                taps[0] += 1

        def group_norm(s):
            dve.wait_ge(S("y_done"), 2 * s + 2)
            BK.wait_filled(dve, ("fT", 1, 1))
            y3 = ps[:, 6 + s, :].rearrange("p (h n) -> p h n", h=H)
            yb3, tb3 = yb.rearrange("p (h n) -> p h n", h=H), tb.rearrange("p (h n) -> p h n", h=H)
            bc = lambda v: v.rearrange("p (h o) -> p h o", o=1).broadcast_to([P, H, HD])
            own.link(V.tensor_reduce(st8[:, 0:8], y3, AX, ALU.add))
            own.link(TS(st8[:, 0:8], st8[:, 0:8], 1.0 / HD, None, ALU.mult))
            own.link(TT(yb3, y3, bc(st8[:, 0:8]), ALU.subtract))
            own.link(TT(tb, yb, yb, ALU.mult))
            own.link(V.tensor_reduce(st8[:, 24:32], tb3, AX, ALU.add))
            sig(TS(st8[:, 8:16], st8[:, 24:32], 1.0 / HD, GN_EPS, ALU.mult, ALU.add), "gn_var")
            dve.wait_ge(S("gn_rstd"), s + 1)
            own.link(TT(yb3, yb3, bc(st8[:, 16:24]), ALU.mult))
            dve.wait_ge(S("ld_gn"), 16)
            own.inc(TT(yb, yb, gnp[:, 0, :], ALU.mult))
            own.link(TT(tb3, VT[:, s, :].rearrange("p (h n) -> p h n", h=H), bc(bon[:, s * 8:s * 8 + 8]), ALU.mult))
            own.link(TT(yb, yb, gnp[:, 1, :], ALU.add))
            own.link(TT(yb, yb, tb, ALU.add))
            bank = take(("g", s))
            BK.drained_by(TT(yb, yb, bank, ALU.mult), ("g", s))
            BK.wait_drained(dve, ("g", s))
            sig(V.tensor_copy(VT[:, s, :], yb), "mixed_a")

        mask_f = [[SU, UI], [SL, LI]]
        for (s, z) in PAIRS:
            m = cst[:, C_SU:C_SU + 512].rearrange("p (c n) -> p c n", c=4)[:, z::2, :]
            m = m.rearrange("p (o c) n -> p o c n", o=1).broadcast_to([P, 2, 2, P])
            for i in range(4):
                for g in range(2):
                    bank = take(("gram", s, z, g, i))
                    BK.drained_by(TT(MAT[:, g, i].rearrange("p (b c) n -> p b c n", b=2),
                                     bank.rearrange("p (b c n) -> p b c n", b=2, c=2), m, ALU.mult),
                                  ("gram", s, z, g, i))
            m = (SL if z == 0 else SU).rearrange("p (o n) -> p o n", o=1).broadcast_to([P, 4, P])
            for g in range(2):
                BK.drained_by(TT(LS[:, g, 0], take(("L", s, z, g, 0)).rearrange("p (i n) -> p i n", i=4), m, ALU.mult),
                              ("L", s, z, g, 0))
            for j in range(LEVELS):
                for g in range(2):
                    key = ("X", s, z, g, j)
                    bank = take(key)
                    if j == 0:
                        BK.wait_drained(dve, ("B", s, z, g))
                    else:
                        BK.wait_drained(dve, ("X", s, z, g, j - 1))
                    BK.drained_by(TT(XS[:, g, (j + 1) % 2, :], bank[:, 0:256], XS[:, g, j % 2, :], ALU.add), key)
                    if j < LEVELS - 1:
                        key = ("LT", s, z, g, j + 1)
                        BK.drained_by(V.tensor_copy(LT[:, g, (j + 1) % 2].rearrange("p i n -> p (i n)"), take(key)), key)
                    if g == 0 and (s, z, j) in fold_in:
                        fold(*fold_in[(s, z, j)])
                if (s, z, j) in mod_after:
                    mod(*mod_after[(s, z, j)])
                conv(5)
            if s == 0:
                if z == 1:
                    BK.wait_filled(dve, ("fT", 0, 1))
                for t in range(AT):
                    for c in range(2):
                        ins = TS(fint[:, t, c, :], OPS[:, z, t, 0, 2 + c, :], fsc[:, z, t, 0:1], None, ALU.mult)
                        if (t, c) != (AT - 1, 1):
                            own.inc(ins)
                sig(ins, "fin")
            if z == 1:
                if s == 1:
                    conv(CONV_W * AT)
                group_norm(s)
        dve.wait_ge(S("ld_cln"), 16)
        for s in range(NS):
            bank = take(("cT", s))
            own.link(V.bn_stats(bns[:, 12:18], bank))
            own.link(V.bn_aggr(st8[:, 36:38], bns[:, 12:18].rearrange("p (n c) -> p n c", c=6)))
            sig(TS(st8[:, 34 + s:35 + s], st8[:, 37:38], LN_EPS, None, ALU.add), "cln_var")
            dve.wait_ge(S("cln_rstd"), s + 1)
            BK.drained_by(TS(yb, bank, st8[:, 36:37], st8[:, 32 + s:33 + s], ALU.subtract, ALU.mult), ("cT", s))
            BK.wait_drained(dve, ("cT", s))
            own.link(TT(yb, yb, cln[:, 0, :], ALU.mult))
            own.link(TT(yb, yb, cln[:, 1, :], ALU.add))
            sig(TS(tb, yb, -80.0, None, ALU.max), "cln_y")
            dve.wait_ge(S("cln_exp"), s + 1)
            own.link(TS(tb, tb, 1.0, None, ALU.add))
            own.link(V.reciprocal(tb, tb))
            sig(TT(OB[:, s, :], yb, tb, ALU.mult), "mixed_b")
            dve.wait_ge(S("mixed_b"), s + 1)
            sig(TS(st8[:, 40:41], st8[:, 36:37], 1.0, None, ALU.mult), "convT")
        for s in range(NS):
            copy3(dve, BK, ("oT", 0, s, 1), hT, s, 4)
        for s in range(NS):
            layer_norm(0, 0, s, zl, lambda half: take(("mix", 0, s, half)))

        def moe(l):
            rv = lambda at, n, pattern=None, **z: (rt_[:, at:at + n].rearrange(pattern, **z) if pattern else rt_[:, at:at + n])
            if l == 0:
                pass
            for s in range(NS):
                modulated(("xT", f"e{l}", s, 1), s, 4, l, 3)
            lg = rv(R_LG, 72, "p (s n) -> p s n", s=NS)
            bank = take(("lg", l))
            dve.wait_ge(S("ld_rb"), 16 * (l + 1))
            rb3 = rb.rearrange("p (o n) -> p o n", o=1).broadcast_to([P, NS, 36])
            BK.drained_by(TT(lg, bank[:, 0:128].rearrange("p (s n) -> p s n", s=NS)[:, :, 0:36], rb3, ALU.add), ("lg", l))
            BK.wait_drained(dve, ("lg", l))
            sc = rt_[:, R_S:R_S + 64]
            two = lambda at: sc[:, at:at + 2]
            bc2 = lambda at, n: two(at).rearrange("p (s o) -> p s o", o=1).broadcast_to([P, NS, n])
            row = lambda at, n: cst[:, at:at + n].rearrange("p (o n) -> p o n", o=1).broadcast_to([P, NS, n])

            def first_max(v, n, best, onehot, at_iota):
                own.link(V.tensor_reduce(two(best), v, AX, ALU.max))
                own.link(TT(onehot, v, bc2(best, n), ALU.is_equal))
                own.link(STT(onehot, onehot, -1000.0, row(at_iota, n), ALU.mult, ALU.add))
                own.link(V.tensor_reduce(two(30), onehot, AX, ALU.min))
                own.link(TS(two(30), two(30), 1000.0, None, ALU.add))
                own.link(TT(onehot, row(at_iota, n), bc2(30, n), ALU.is_equal))

            ohg = rv(R_OHG, 8, "p (s n) -> p s n", s=NS)
            ex = rv(R_EX, 8, "p (s n) -> p s n", s=NS)
            first_max(lg[:, :, 0:4], 4, 0, ohg, C_G4)
            sig(TT(ex, lg[:, :, 0:4], bc2(0, 4), ALU.subtract), "routed1")
            t4 = rv(R_T4, 64)
            for s in range(NS):
                own.inc(TT(t4[:, s * 32:(s + 1) * 32].rearrange("p (g e) -> p g e", g=NG),
                           lg[:, s, 4:36].rearrange("p (g e) -> p g e", g=NG),
                           ohg[:, s, :].rearrange("p (g o) -> p g o", o=1).broadcast_to([P, NG, EPG]), ALU.mult))
            own.wait()
            ein = rv(R_EIN, 16, "p (s n) -> p s n", s=NS)
            for s in range(NS):
                own.inc(V.tensor_reduce(ein[:, s, :], t4[:, s * 32:(s + 1) * 32].rearrange("p (g e) -> p e g", g=NG), AX, ALU.add))
            own.wait()
            o1, o2 = rv(R_O1, 16, "p (s n) -> p s n", s=NS), rv(R_O2, 16, "p (s n) -> p s n", s=NS)
            first_max(ein, 8, 2, o1, C_G4 + 4)
            own.link(STT(ein, o1, -1e30, ein, ALU.mult, ALU.add))
            first_max(ein, 8, 4, o2, C_G4 + 4)
            sig(TT(two(16), two(4), two(2), ALU.subtract), "routed2")
            P1, P2 = rv(R_P1, 64), rv(R_P2, 64)
            for dst, oh in ((P1, o1), (P2, o2)):
                for s in range(NS):
                    own.inc(TT(dst[:, s * 32:(s + 1) * 32].rearrange("p (g e) -> p g e", g=NG),
                               ohg[:, s, :].rearrange("p (g o) -> p g o", o=1).broadcast_to([P, NG, EPG]),
                               oh[:, s, :].rearrange("p (o e) -> p o e", o=1).broadcast_to([P, NG, EPG]), ALU.mult))
            own.wait()
            sig(TT(rv(R_OH, 64), P1, P2, ALU.add), "chosen")
            own.link(V.memset(rv(R_ZERO, P), 0.0))
            sig(V.memset(sc[:, 60:62], 0.0), "zero")
            dve.wait_ge(S("route_exp"), 2 * l + 2)
            own.link(V.tensor_reduce(two(20), ex, AX, ALU.add))
            own.link(V.reciprocal(two(22), two(20)))
            own.link(TS(two(24), two(16), 1.0, None, ALU.add))
            own.link(V.reciprocal(two(26), two(24)))
            own.link(TT(two(26), two(26), two(22), ALU.mult))
            own.link(TT(two(28), two(26), two(16), ALU.mult))
            bank = take(("pos", l))
            slot_of = rv(R_SL, 64)
            own.link(V.tensor_copy(sc[0:32, 32:33], bank[0:32, 64:65]))
            own.link(TS(sc[0:32, 33:34], sc[0:32, 32:33], 0.5, None, ALU.is_gt))
            for m in range(1, NS * T // CH):
                own.link(STT(sc[0:32, 33:34], sc[0:32, 32:33], m * CH + 0.5, sc[0:32, 33:34], ALU.is_gt, ALU.add))
            sig(TS(rt_[0:32, R_NB:R_NB + P], ones[0:32, :], sc[0:32, 33:34], None, ALU.mult), "nchunks")
            BK.drained_by(V.tensor_copy(slot_of, bank[:, 0:64]), ("pos", l))
            BK.wait_drained(dve, ("pos", l))
            bank = take(("base", l))
            own.inc(V.tensor_copy(sc[:, 40:41], bank[:, 32:33]))
            own.link(V.tensor_copy(sc[0:32, 41:42], bank[0:32, 64:65]))
            sig(TS(rt_[0:32, R_CMP:R_CMP + 40], cst[0:32, C_G4 + 12:C_G4 + 52], sc[0:32, 41:42], None, ALU.is_ge), "ended")
            own.link(TS(rv(R_T, 32), bank[:, 0:32], float(CH), None, ALU.mult))
            for s in range(NS):
                ins = TT(slot_of[:, s * 32:(s + 1) * 32], slot_of[:, s * 32:(s + 1) * 32], rv(R_T, 32), ALU.add)
                if s == 0:
                    own.inc(ins)
            BK.drained_by(ins, ("base", l))
            BK.wait_drained(dve, ("base", l))
            for pick, oh in ((0, P1), (1, P2)):
                own.link(TT(rv(R_T, 64), oh, slot_of, ALU.mult))
                own.link(V.tensor_reduce(sc[:, 42 + 2 * pick:44 + 2 * pick], rv(R_T, 64, "p (s n) -> p s n", s=NS), AX, ALU.add))
            own.inc(TS(sc[0:1, 46:47], sc[0:1, 40:41], 2.5, None, ALU.subtract))
            own.link(TS(rt_[0:1, R_T + 16:R_T + 36], cst[0:1, C_G4 + 12:C_G4 + 52:2], sc[0:1, 40:41], None, ALU.is_lt))
            own.inc(V.tensor_reduce(sc[0:1, 51:52], rt_[0:1, R_T + 16:R_T + 36], AX, ALU.add))
            own.link(TS(rt_[0:1, R_T:R_T + 10], cst[0:1, C_G4 + 12:C_G4 + 52:4], sc[0:1, 46:47], None, ALU.is_lt))
            own.link(V.tensor_reduce(sc[0:1, 48:49], rt_[0:1, R_T:R_T + 10], AX, ALU.add))
            own.link(STT(sc[0:1, 49:50], sc[0:1, 48:49], -2.0, sc[0:1, 51:52], ALU.mult, ALU.add))
            own.link(TS(sc[0:1, 50:51], sc[0:1, 49:50], -1.0, 1.0, ALU.mult, ALU.add))
            own.link(V.tensor_copy(meta[0:1, l, 0:3], sc[0:1, 48:51]))
            own.link(TS(rt_[0:1, R_T:R_T + 40], take(("eid", l))[0:1, 0:40], float(NE - 1), None, ALU.min))
            BK.drained_by(V.tensor_copy(meta[0:1, l, 4:44], rt_[0:1, R_T:R_T + 40]), ("eid", l))
            BK.wait_drained(dve, ("eid", l))
            sig(V.memset(sc[:, 62:64], 0.0), f"meta{l}")
            dve.wait_ge(S(f"meta{l}"), 1)
            pairs, odd = (dve.value_load(meta[0:1, l, m:m + 1], min_val=lo, max_val=hi)
                          for m, lo, hi in ((0, 1, 10), (1, 0, 1)))
            loop = S(f"dve_loop{l}")

            def chained(m, ins):
                ins.then_inc(loop, 1)
                dve.wait_ge(loop, m)

            def choose(n, m):
                for s in range(NS):
                    TS(sel[:, s, :], iota, sc[:, 42 + s:43 + s], None, ALU.is_equal).then_inc(loop, 1)
                dve.wait_ge(loop, m + 2)
                for s in range(NS):
                    ins = STT(sel[:, s, :], iota, sc[:, 44 + s:45 + s], sel[:, s, :], ALU.is_equal, ALU.add)
                    if s == 0:
                        ins.then_inc(loop, 1)
                ins.then_inc(S(f"selected{l}"), 1)
                dve.wait_ge(loop, m + 3)
                dve.wait_ge(S(f"selected{l}"), n + 1)

            def gates(n, m):
                for s in range(NS):
                    TS(gsel[:, 0, s, :], iota, sc[:, 42 + s:43 + s], sc[:, 26 + s:27 + s], ALU.is_equal, ALU.mult)\
                        .then_inc(loop, 1)
                    TS(gsel[:, 1, s, :], iota, sc[:, 44 + s:45 + s], sc[:, 28 + s:29 + s], ALU.is_equal, ALU.mult)\
                        .then_inc(loop, 1)
                dve.wait_ge(loop, m + 4)
                TT(gsel[:, 0, :, :], gsel[:, 0, :, :], gsel[:, 1, :, :], ALU.add).then_inc(S(f"gates{l}"), 1)
                chained(m + 5, TS(sc[:, 42:46], sc[:, 42:46], float(P), None, ALU.subtract))
                dve.wait_ge(S(f"gates{l}"), n + 1)

            def gathered(n):
                dve.wait_ge(S(f"gathered{l}"), n * 2 + 2)
                V.tensor_copy(xg[:, 4:8, :].rearrange("p k n -> p (k n)"), ps[:, 5, :]).then_inc(S(f"xg_dve{l}"), 1)

            V.memset(tT[1][:, 256:512], 0.0)
            V.memset(ysb, 0.0).then_inc(S(f"y_read_dve{l}"), 1)
            choose(0, 0)
            gates(0, 3)
            gathered(0)
            choose(1, 8)
            def step(n, it, u):
                dve.wait_ge(S(f"gate_exp{l}"), n + 1)
                V.tensor_scalar(hid[:, 0, :], hid[:, 0, :], 1.0, None, ALU.add).then_inc(S(f"dve_hid{l}"), 1)
                dve.wait_ge(S(f"dve_hid{l}"), n * 3 + 1)
                V.reciprocal(hid[:, 0, :], hid[:, 0, :]).then_inc(S(f"dve_hid{l}"), 1)
                dve.wait_ge(S(f"dve_hid{l}"), n * 3 + 2)
                TT(hid[:, 0, :], hid[:, 0, :], ps[:, 6, 0:256], ALU.mult).then_inc(S(f"dve_hid{l}"), 1)
                dve.wait_ge(S(f"dve_hid{l}"), n * 3 + 3)
                TT(hid[:, 1, :], hid[:, 0, :], ps[:, 6, 256:512], ALU.mult).then_inc(S(f"hid{l}"), 1)
                gathered(n + 1)
                dve.wait_ge(S(f"turned{l}"), n + 1)
                gates(n + 1, n * 8 + 11)
                choose(n + 2, n * 8 + 16)
                dve.wait_ge(S(f"down{l}"), n * 2 + 6)
                V.tensor_copy(ysb[:, 512:1024], ps[:, 5, :]).then_inc(S(f"y_read_dve{l}"), 1)

            with dve.Fori(0, pairs) as it:
                for u in range(2):
                    step(it * 2 + u, it, u)
            with dve.If(odd):
                step(pairs * 2, pairs, 0)
            dve.wait_ge(S("summed"), l + 1)
            for s in range(NS):
                layer_norm(l, 1, s, zm, lambda half: ps[:, 2 * s + half, :])

        moe(0)

        for s in range(NS):
            modulated(("xT", "m1", s, 1), s, 4, 1, 0)
        dve.wait_ge(S("ld_sub"), 32)
        for q in range(2):
            own.link(TT(lqk[:, 2 * q, :], lqk[:, 2 * q, :], lqk[:, 2 * q + 1, :], ALU.mult))
            ins = V.tensor_reduce(lam[:, q:q + 1], lqk[:, 2 * q, :], AX, ALU.add)
            if q == 0:
                own.inc(ins)
        sig(ins, "lam_dot")
        dve.wait_ge(S("ld_rope"), 16)

        def halves(v):
            v = v.rearrange("p (h a b f) -> p h a b f", h=16, a=2, b=2)
            return v[:, :, :, 0, :], v[:, :, :, 1, :]

        cosb = rope[:, 0:32].rearrange("p (o a f) -> p o a f", o=1, a=2).broadcast_to([P, 16, 2, 16])
        sinb = rope[:, 32:64].rearrange("p (o a f) -> p o a f", o=1, a=2).broadcast_to([P, 16, 2, 16])
        rv4 = [rt[:, q, :].rearrange("p (h a f) -> p h a f", h=16, a=2) for q in range(4)]
        for q in range(2):
            BK.wait_drained(dve, ("qkv", 1, 2 * q + 1))
            x1, x2 = halves(QKV[:, 1, q * D:(q + 1) * D])
            y1, y2 = halves(QR[:, q, :])
            if q == 1:
                dve.wait_ge(S("roped"), 1)
            own.inc(TT(rv4[0], x1, cosb, ALU.mult))
            own.inc(TT(rv4[1], x2, sinb, ALU.mult))
            own.inc(TT(rv4[2], x1, sinb, ALU.mult))
            own.inc(TT(rv4[3], x2, cosb, ALU.mult))
            own.wait()
            own.inc(TT(y1, rv4[0], rv4[1], ALU.subtract))
            sig(TT(y2, rv4[2], rv4[3], ALU.add), "roped")
        dve.wait_ge(S("lam_exp"), 1)
        own.link(TT(lam[:, 4:5], lam[:, 2:3], lam[:, 3:4], ALU.subtract))
        own.link(TS(lam[:, 5:6], lam[:, 4:5], LAM_INIT, None, ALU.add))
        for n in range(len(PAIRS1) + 1):
            if n < len(PAIRS1):
                s, hp = PAIRS1[n]
                nk = T * (s + 1)
                q = sm1[:, n % 4]
                for z in range(2):
                    bank = take(("sc", s, hp, z))
                    own.link(V.tensor_reduce(q[:, 2 * z:2 * z + 2], bank.rearrange("p (m n) -> p m n", m=2)[:, :, 0:nk],
                                             AX, ALU.max))
                    sig(TS(q[:, 4 + 2 * z:6 + 2 * z], q[:, 2 * z:2 * z + 2], -HD ** -0.5, None, ALU.mult), "smax")
            if n >= 1:
                s, hp = PAIRS1[n - 1]
                b = (n - 1) % 2
                nk = T * (s + 1)
                q = sm1[:, (n - 1) % 4]
                BK.wait_drained(dve, ("sc", s, hp, 1))
                own.link(V.reciprocal(q[:, 12:16], q[:, 8:12]))
                own.link(TS(q[:, 14:16], q[:, 14:16], lam[:, 5:6], None, ALU.mult))
                for m in range(2):
                    own.inc(TS(PB[:, b, 1, m, 0:nk], PB[:, b, 1, m, 0:nk], q[:, 14 + m:15 + m], None, ALU.mult))
                own.wait()
                if n >= 3:
                    BK.wait_filled(dve, ("aT",) + PAIRS1[n - 3])
                for m in range(2):
                    sig(STT(AB[:, b, m, 0:nk], PB[:, b, 0, m, 0:nk], q[:, 12 + m:13 + m], PB[:, b, 1, m, 0:nk],
                            ALU.mult, ALU.subtract), "attn")
            if n >= 1 and n % 2 == 0:
                s, hp = PAIRS1[n - 1]
                key = ("pv", s, hp // 2)
                BK.drained_by(V.tensor_copy(OO[:, s, (hp // 2) * 512:(hp // 2 + 1) * 512], take(key)), key)
        for s in range(NS):
            BK.wait_drained(dve, ("pv", 1, 1))
            o3 = OO[:, s, :].rearrange("p (h n) -> p h n", h=H)
            own.link(TT(t1k, OO[:, s, :], OO[:, s, :], ALU.mult))
            own.link(V.tensor_reduce(st8[:, 24:32], t1k.rearrange("p (h n) -> p h n", h=H), AX, ALU.add))
            sig(TS(st8[:, 8:16], st8[:, 24:32], 1.0 / P, RMS_EPS, ALU.mult, ALU.add), "at_var")
            dve.wait_ge(S("at_rstd"), s + 1)
            own.link(TT(o3, o3, st8[:, 16:24].rearrange("p (h o) -> p h o", o=1).broadcast_to([P, H, P]), ALU.mult))
            sg = subg.rearrange("p (o n) -> p o n", o=1).broadcast_to([P, H, P])
            sig(STT(o3, o3, 1.0 - LAM_INIT, sg, ALU.mult, ALU.mult), "attended")
            copy3(dve, BK, ("oT", 1, s, 1), hT, s, 4)
        for s in range(NS):
            layer_norm(1, 0, s, zl1, lambda half: take(("mix", 1, s, half)))
        moe(1)

    ctx.close()


def kernel(**inputs):
    import concourse.bacc as bacc
    from concourse.bass_utils import run_bass_kernel_spmd

    a = {k: np.asarray(v) for k, v in inputs.items()}
    tile = lambda w: np.ascontiguousarray(w.reshape(*w.shape[:-2], KT, P, w.shape[-1]).swapaxes(-3, -2))
    cut = lambda w: np.stack([tile(w[:, c:c + 512]) for c in range(0, w.shape[1], 512)]).reshape(-1, P, 4096)
    col = lambda v: np.ascontiguousarray(v.reshape(-1, P).T)
    ev = a["ev_in_w"][0]
    evc = np.concatenate([ev[:, t * P:(t + 1) * P] for t in TILES], 1)
    evp = np.concatenate([tile(evc[:, c:c + 512]).reshape(P, -1) for c in range(0, evc.shape[1], 512)], 1)
    vec = np.concatenate([
        col(a["ev_ts_mu"][0]), col(a["ev_pw_b"][0]), col(a["ev_a0"][0].reshape(-1)), col(a["ev_k_k"][0]),
        col(a["ev_k_a"][0]), col(a["ev_r_k"][0].reshape(-1)), col(a["ev_dw_b"][0]), col(a["ev_dw_w"][0].reshape(-1))], 1)
    s0 = a["state_wkv"][0, 0].transpose(0, 1, 3, 2)
    s0 = s0.reshape(2, AT, P, HD).transpose(2, 0, 1, 3)
    gate = a["ffn_w_gate"].reshape(2, NE, KT, P, FF)
    up = a["ffn_w_up"].reshape(2, NE, KT, P, FF)
    down = a["ffn_w_down"].reshape(2, NE, 2, P, D)
    exp = np.concatenate([
        np.concatenate([gate, up], -1).transpose(0, 1, 3, 2, 4).reshape(2, NE, P, KT * 2 * FF),
        down.transpose(0, 1, 3, 2, 4).reshape(2, NE, P, 2 * D)], -1)
    arrays = {
        "cst": constants(), "rope": rope_tables(), "vec": vec,
        "cond": np.stack([a["c_ctx"], a["c"][0]]).reshape(2, KT, P).transpose(2, 1, 0),
        "x_prompt": a["x_prompt"][0], "x_sample": a["x_sample"][0],
        "mod_w": np.stack([cut(a["mod_w"][l]) for l in range(2)]), "mod_b": a["mod_b"],
        "ev_in_w": evp, "ev_w_up": a["ev_w_up"][0].reshape(P, AW), "ev_a_up": a["ev_a_up"][0].reshape(P, AW),
        "ev_g_up": a["ev_g_up"][0], "s0t": s0, "ev_w0": a["ev_w0"][0],
        "ev_cln": np.stack([a["ev_cln_g"][0], a["ev_cln_b"][0]]), "ev_gn": np.stack([a["ev_gn_g"][0], a["ev_gn_b"][0]]),
        "ev_out_w": cut(a["ev_out_w"][0]), "od_in_w": cut(a["od_in_w"][0]), "od_out_w": cut(a["od_out_w"][0]),
        "ln": np.stack([np.stack([a[f"ln{w}_g"][l], a[f"ln{w}_b"][l]]) for l in range(2) for w in (1, 2)]),
        "lqk": np.stack([a["od_lq1"][0], a["od_lk1"][0], a["od_lq2"][0], a["od_lk2"][0]]),
        "subln": a["od_subln_g"][0],
        "cache_k": a["cache_k"][0, 0].reshape(T, D), "cache_v": a["cache_v"][0, 0].reshape(T, D),
        "r_w": np.stack([tile(np.concatenate([a["rg_w"][l], a["re_w"][l]], 1)).reshape(P, -1) for l in range(2)]),
        "r_b": np.concatenate([a["rg_b"], a["re_b"]], 1), "w_exp": exp,
    }
    outs = {"y": (NS, T, D), "state": (2, H, HD, HD), "cache_k": (T, D), "cache_v": (T, D)}
    nc = bacc.Bacc("TRN2", target_bir_lowering=False, num_devices=1)
    arrays = {f"in_{k}": np.ascontiguousarray(v) for k, v in arrays.items()}
    ins = {k[3:]: nc.dram_tensor(k, v.shape, F32, kind="ExternalInput").ap() for k, v in arrays.items()}
    o = {k: nc.dram_tensor(f"out_{k}", v, F32, kind="ExternalOutput").ap() for k, v in outs.items()}
    build(nc, ins, o)
    r = run_bass_kernel_spmd(nc, [arrays], core_ids=[0]).results[0]
    y = r["out_y"]
    return (y[0:1], y[1:2], r["out_state"].reshape(1, 1, 2, H, HD, HD),
            r["out_cache_k"].reshape(1, 1, T, H, P), r["out_cache_v"].reshape(1, 1, T, H, P))
```

```python
from contextlib import ExitStack

import numpy as np
import concourse.bass as bass
from concourse import mybir

F32 = mybir.dt.float32
I32 = mybir.dt.int32
ALU = mybir.AluOpType
ACT = mybir.ActivationFunctionType
AX = mybir.AxisListType.X

P = 128
D = 1024
KT = D // P
T = 128
NS = 2
H = 8
HD = 64
AW = 512
AT = AW // P
CONV_W = 31
PADC = CONV_W // 2
GN_EPS = 64e-5
LN_EPS = 1e-5
RMS_EPS = 1e-5
ALPHA = 4 ** 0.25
NG, EPG = 4, 8
NE = NG * EPG
FF = 256
CH = 64
GRID_W = 64
ROPE_BASE = 10000.0
LAM_INIT = 0.8 - 0.6 * float(np.exp(-0.3))
E_HALF = float(np.exp(-0.5))

WD, AD, GD = 12, 13, 14
TILES = [WD, AD, GD] + [4, 5, 6, 7] + [0, 1, 2, 3] + [8, 9, 10, 11]
for _t in range(AT):
    TILES += [15 + _t, 19 + _t]
NPA = 15

V_MU, V_PW, V_A0, V_KK, V_KA, V_RK, V_DB, V_DW = 0, 15, 23, 31, 35, 39, 43, 47
NVEC = V_DW + CONV_W * AT

C_ID, C_SU, C_SL, C_UI, C_LI = 0, 128, 256, 384, 512
C_CUM, C_BLK, C_HSEL, C_IOTA, C_ONE = 640, 770, 898, 930, 1058
C_SEL, C_G4 = 1186, 1442
NCST = C_G4 + 64


def constants():
    c = np.zeros((P, NCST), np.float32)
    r, q = np.arange(P)[:, None], np.arange(P)[None, :]
    c[:, C_ID:C_ID + P] = r == q
    c[:, C_SU:C_SU + P] = r < q
    c[:, C_SL:C_SL + P] = r > q
    c[:, C_UI:C_UI + P] = r <= q
    c[:, C_LI:C_LI + P] = r >= q
    c[:, C_CUM:C_CUM + T + 1] = -E_HALF * (r < np.arange(T + 1)[None, :])
    c[:, C_BLK:C_BLK + P] = (r // HD) == (q // HD)
    for t in range(AT):
        for h in range(H):
            c[:, C_HSEL + t * H + h] = (2 * t + np.arange(P) // HD) == h
    c[:, C_IOTA:C_IOTA + P] = q
    c[:, C_ONE:C_ONE + P] = 1.0
    for s in range(NS):
        c[s::32, C_SEL + s * P:C_SEL + (s + 1) * P] = 1.0
    c[:, C_G4:C_G4 + 4] = np.arange(4)
    c[:, C_G4 + 4:C_G4 + 12] = np.arange(8)
    c[:, C_G4 + 12:C_G4 + 52] = np.arange(40)
    return c


def rope_tables():
    nf = HD // 4
    inv = ROPE_BASE ** (-np.arange(nf, dtype=np.float64) / nf)
    tok = np.arange(T)
    pos = np.stack([tok // GRID_W, tok % GRID_W], 1)
    ang = pos[:, :, None] * inv[None, None, :]
    return np.stack([np.cos(ang), np.sin(ang)], 1).reshape(T, 4 * nf).astype(np.float32)


class Banks:

    def __init__(self, ps, banks, filled, drained):
        self.ps, self.banks, self.filled, self.drained = ps, banks, filled, drained
        self.no, self.by, self.nth, self.order = {}, {}, {}, []
        self.count = {e: 0 for e in drained}
        self.seen = {}

    def add(self, key, by):
        assert key not in self.no, key
        self.no[key] = len(self.order)
        self.order.append(key)
        self.by[key] = by
        self.count[by] += 1
        self.nth[key] = self.count[by]

    def bank(self, key):
        return self.ps[:, self.banks[self.no[key] % len(self.banks)], :]

    def wait_free(self, pe, key):
        n = self.no[key] - len(self.banks)
        if n >= 0:
            old = self.order[n]
            pe.wait_ge(self.drained[self.by[old]], self.nth[old])

    def wait_filled(self, eng, key):
        eng.wait_ge(self.filled, self.no[key] + 1)

    def drained_by(self, ins, key):
        by = self.by[key]
        self.seen[by] = self.seen.get(by, 0) + 1
        assert self.seen[by] == self.nth[key], key
        ins.then_inc(self.drained[by], 1)

    def wait_drained(self, eng, key):
        eng.wait_ge(self.drained[self.by[key]], self.nth[key])


def copy3(eng, BK, key, hT, s, k0):
    BK.wait_filled(eng, key)
    dst = hT[:, k0:k0 + 4, s * T:(s + 1) * T]
    src = BK.bank(key).rearrange("p (k n) -> p k n", k=4)
    if BK.by[key] == "act":
        BK.drained_by(eng.activation(dst, src, ACT.Copy), key)
    else:
        BK.drained_by(eng.tensor_copy(dst, src), key)


class Steps:

    def __init__(self, eng, sem):
        self.eng, self.sem, self.n = eng, sem, 0

    def inc(self, ins):
        self.n += 1
        ins.then_inc(self.sem, 1)
        return self.n

    def wait(self, n=None):
        self.eng.wait_ge(self.sem, self.n if n is None else n)

    def link(self, ins):
        self.inc(ins)
        self.wait()


ARENA = 53110


def build(nc, a, o):
    ctx = ExitStack()
    sems = {}

    def S(name):
        if name not in sems:
            sems[name] = ctx.enter_context(nc.semaphore(name))
        return sems[name]

    arena = ctx.enter_context(nc.sbuf_tensor("arena", [P, ARENA], F32))
    meta = ctx.enter_context(nc.sbuf_tensor("meta", [1, 2, 48], I32))
    ps = ctx.enter_context(nc.psum_tensor("ps", [P, 8, 512], F32))
    top = [0]

    def region(n):
        at = top[0]
        top[0] += n
        assert top[0] <= ARENA, top[0]
        return at

    def view(at, n, pattern=None, **sizes):
        v = arena[:, at:at + n]
        return v.rearrange(pattern, **sizes) if pattern else v

    cst = view(region(NCST), NCST)
    vec = view(region(NVEC), NVEC)
    nvec = view(region(64), 64)
    x = view(region(2 * D), 2 * D, "p (s n) -> p s n", s=NS)
    hT = view(region(KT * 256), KT * 256, "p (k n) -> p k n", k=KT)
    rowbuf = view(region(D), D)
    gaterow = view(region(D), D)
    mbias = view(region(3 * 512), 3 * 512, "p (g n) -> p g n", g=3)
    gbc_at = region(2 * D)
    gbc = view(gbc_at, 2 * D, "p (s n) -> p s n", s=NS)
    lnp_at = region(2 * D)
    lnp = view(lnp_at, 2 * D, "p (g n) -> p g n", g=2)
    modT = view(region(192), 192, "p (l m k s) -> p l m k s", l=2, m=6, s=NS)
    condw = view(region(48), 48)
    cond = view(region(KT * 32), KT * 32, "p (k n) -> p k n", k=KT)
    small = view(region(320), 320)
    rope = view(region(64), 64)
    ring_at = region(3 * 4096)
    ring = view(ring_at, 3 * 4096, "p (g n) -> p g n", g=3)
    scr = top[0]
    SCR = ARENA - scr

    def sv(at, n, pattern=None, **sizes):
        assert at + n <= SCR, (at + n, SCR)
        return view(scr + at, n, pattern, **sizes)

    ident = cst[:, C_ID:C_ID + P]
    SU, SL = cst[:, C_SU:C_SU + P], cst[:, C_SL:C_SL + P]
    UI, LI = cst[:, C_UI:C_UI + P], cst[:, C_LI:C_LI + P]
    blk = cst[:, C_BLK:C_BLK + P]
    iota = cst[:, C_IOTA:C_IOTA + P]
    ones = cst[:, C_ONE:C_ONE + P]

    filled = S("filled")
    BK = Banks(ps, [0, 1, 2, 3, 4, 5], filled, {"act": S("drained_act"), "dve": S("drained_dve")})

    chunks = []

    def chunk(name, src, cols, last):
        chunks.append((name, src, cols, last))

    for c in range(4):
        chunk(("mod", 0, c), a["mod_w"][0, c], 512, ("mod", 0, c))
    for c in range(6):
        n = min(4, 23 - 4 * c) * P
        last = 4 * c + n // P - 1
        key = ("pa", last) if last < NPA else ("pb", (last - NPA - 1) // 2 if (last - NPA) % 2 else (last - NPA) // 2)
        src = a["ev_in_w"][:, c * 4096:c * 4096 + 8 * n]
        chunk(("evin", c), src, n, key)
    for c in range(4, 12):
        chunk(("mod", 0, c), a["mod_w"][0, c], 512, ("mod", 0, c))
    for c in range(4):
        chunk(("mod", 1, c), a["mod_w"][1, c], 512, ("mod", 1, c))
    for c in range(4, 12):
        chunk(("mod", 1, c), a["mod_w"][1, c], 512, ("mod", 1, c))
    for c in range(2):
        chunk(("out", 0, c), a["ev_out_w"][c], 512, ("mix", 0, 1, c))
    FIRST_OF_1 = len(chunks)
    for c in range(6):
        chunk(("odin", c), a["od_in_w"][c], 512, ("qkv", 1, c))
    for c in range(2):
        chunk(("out", 1, c), a["od_out_w"][c], 512, ("mix", 1, 1, c))
    at_chunk = {name: i for i, (name, *_) in enumerate(chunks)}
    ring_ld = [S(f"ring_loaded{i}") for i in range(3)]

    ASIDE = {("mod", 0, 3): 8192, ("evin", 0): 0, ("evin", 1): 4096}
    in_ring = [i for i, (name, *_) in enumerate(chunks) if name not in ASIDE]
    turn = {i: r for r, i in enumerate(in_ring)}

    def slot(name):
        i = at_chunk[name]
        cols = chunks[i][2]
        v = sv(PRE + ASIDE[name], 4096) if name in ASIDE else ring[:, turn[i] % 3, :]
        return v[:, 0:8 * cols].rearrange("p (k n) -> p k n", k=KT)

    def wait_chunk(pe, name):
        if name in ASIDE:
            pe.wait_ge(S("loaded_" + "_".join(map(str, name))), 16)
        else:
            r = turn[at_chunk[name]]
            pe.wait_ge(ring_ld[r % 3], 16 * (r // 3 + 1))

    def load_chunk(sp, i):
        name, src, cols, _ = chunks[i]
        if name in ASIDE:
            sp.dma_start(sv(PRE + ASIDE[name], 8 * cols), src).then_inc(S("loaded_" + "_".join(map(str, name))), 16)
            return
        r = turn[i]
        if r >= 3:
            BK.wait_filled(sp, chunks[in_ring[r - 3]][3])
        sp.dma_start(ring[:, r % 3, 0:8 * cols], src).then_inc(ring_ld[r % 3], 16)

    def plan_mod(l, c):
        BK.add(("mod", l, c), "dve")

    def plan_fold(l, c):
        if c // 2 in (2, 5):
            BK.add(("gate", l, c), "act")
        elif c % 2:
            BK.add(("modT", l, c // 2), "dve")

    def gate_slot(l, part):
        return {(0, 2): 0, (0, 5): 1, (1, 2): 2, (1, 5): 3}[(l, part)]

    for c in range(4):
        plan_mod(0, c)
        plan_fold(0, c)
    for s in range(NS):
        for h2 in range(2):
            BK.add(("xT", "m0", s, h2), "act" if h2 == 0 else "dve")
    pa, cum = (lambda *n: [("pa", i) for i in n]), (lambda z: [("cum", z, t) for t in range(AT)])
    PROJECTION = (pa(*range(11)) + [("w", 0, 0), ("w", 0, 1)] + pa(11) + [("w", 1, 0), ("w", 1, 1)] + pa(12)
                  + [("ss", 0), ("ss", 1)] + pa(13) + [("a", 0, 0), ("a", 0, 1)] + pa(14) + [("a", 1, 0), ("a", 1, 1)]
                  + [("pb", 0)] + cum(0) + [("pb", 1), ("pb", 2)] + cum(1) + [("pb", 3), ("V", 0), ("V", 1), ("bonus",)])
    for key in PROJECTION:
        BK.add(key, {"pb": "dve", "w": "dve", "ss": "dve", "bonus": "dve"}.get(key[0], "act"))
    PAIRS = [(s, z) for s in range(NS) for z in range(2)]
    LEVELS = 7
    slots = [(s, z, j) for (s, z) in PAIRS for j in range(LEVELS - 2)]
    rest = [(0, c) for c in range(4, 12)] + [(1, c) for c in range(12)]
    mod_after = dict(zip(slots, rest))
    conv_out = {(1, 1, 0): 0, (1, 1, 1): 1}
    TAPS = 7
    fold_in = {(s, z, j + 1): lc for (s, z, j), lc in mod_after.items()}
    for (s, z) in PAIRS:
        for i in range(4):
            for g in range(2):
                BK.add(("gram", s, z, g, i), "dve")
        for g in range(2):
            BK.add(("L", s, z, g, 0), "dve")
        for g in range(2):
            BK.add(("B", s, z, g), "act")
        for j in range(LEVELS):
            for g in range(2):
                BK.add(("X", s, z, g, j), "dve")
                if j < LEVELS - 2:
                    BK.add(("L", s, z, g, j + 1), "act")
                if j < LEVELS - 1:
                    BK.add(("LT", s, z, g, j + 1), "dve")
                if g == 0 and (s, z, j) in fold_in:
                    plan_fold(*fold_in[(s, z, j)])
            if (s, z, j) in mod_after:
                plan_mod(*mod_after[(s, z, j)])
            if (s, z, j) in conv_out:
                BK.add(("cT", conv_out[(s, z, j)]), "dve")
        if s == 0:
            for g in range(2):
                BK.add(("fT", z, g), "act")
                BK.add(("st", z, g), "act")
        if (s, z) == (1, 1):
            for h2 in range(2):
                BK.add(("oT", 0, 0, h2), "act" if h2 == 0 else "dve")
        if z == 1:
            BK.add(("g", s), "dve")
    for s in range(NS):
        if s == 1:
            for h2 in range(2):
                BK.add(("oT", 0, 1, h2), "act" if h2 == 0 else "dve")
        for n in range(2):
            BK.add(("gbc", 0, 0, s, n), "act")
        for n in range(2):
            BK.add(("mix", 0, s, n), "dve")

    def plan_moe(l):
        for s in range(NS):
            for h2 in range(2):
                BK.add(("xT", f"e{l}", s, h2), "act" if s == 0 or h2 == 0 else "dve")
            BK.add(("lg", l, s), "dve")
            for h2 in range(2):
                BK.add(("hb", l, s, h2), "act")
        BK.add(("pos", l), "dve")
        BK.add(("base", l), "dve")
        BK.add(("eid", l), "dve")
        for s in range(NS):
            for n in range(2):
                BK.add(("gbc", l, 1, s, n), "act")

    plan_moe(0)
    for s in range(NS):
        for h2 in range(2):
            BK.add(("xT", "m1", s, h2), "act" if s == 0 or h2 == 0 else "dve")
        BK.add(("qkv", s, 0), "act")
    for c in range(1, 6):
        for s in range(NS):
            BK.add(("qkv", s, c), "act")
    for h2 in range(2):
        BK.add(("cT1", h2), "act")
    for s in range(NS):
        for q in range(2):
            for h2 in range(2):
                BK.add(("qkT", s, q, h2), "act")
    PAIRS1 = [(s, hp) for s in range(NS) for hp in range(H // 2)]
    beside = {1 + 2 * s + n: [("gbc", 1, 0, s, n)] for s in range(NS) for n in range(2)}
    beside.update({6: [("oT", 1, 0, 0), ("oT", 1, 0, 1)], 7: [("mix", 1, 0, 0)], 8: [("mix", 1, 0, 1)]})
    for n in range(len(PAIRS1) + 1):
        if n < len(PAIRS1):
            for z in range(2):
                BK.add(("sc",) + PAIRS1[n] + (z,), "act")
        if n >= 1:
            BK.add(("aT",) + PAIRS1[n - 1], "act")
            if n % 2 == 0:
                BK.add(("pv", PAIRS1[n - 1][0], PAIRS1[n - 1][1] // 2), "dve")
        for key in beside.get(n, []):
            BK.add(key, {"gbc": "act", "mix": "dve"}.get(key[0], "act" if key[-1] == 0 else "dve"))
    for h2 in range(2):
        BK.add(("oT", 1, 1, h2), "act" if h2 == 0 else "dve")
    for n in range(2):
        BK.add(("mix", 1, 1, n), "dve")
    plan_moe(1)

    MOD_ORDER = [(k[1], k[2]) for k in BK.order if k[0] == "mod"]
    MODS = [("mod", l, c) for l, c in MOD_ORDER]
    assert MODS == [n for n, *_ in chunks if n[0] == "mod"]

    OPS = sv(0, 8192, "p (z t s c n) -> p z t s c n", z=2, t=AT, s=NS, c=4)
    wup, aup = sv(0, 512), sv(512, 512)
    lw = sv(1024, 2048, "p (s z n) -> p s z n", s=NS, z=2)
    raw = sv(3072, 4 * 260, "p (b s n) -> p b s n", b=4, s=NS)
    nbr = sv(4112, 512, "p (b n) -> p b n", b=2)
    eg = sv(4624, 512, "p (b n) -> p b n", b=2)
    sq = sv(5136, 1024)
    mbias3 = sv(5136, 512)
    PA_at = 8192
    PA = sv(PA_at, 3840, "p (t n) -> p t n", t=NPA)
    K_, R_, V_ = PA[:, 3:7, :], PA[:, 7:11, :], PA[:, 11:15, :]
    cln = sv(PA_at + 768, 1024, "p (g n) -> p g n", g=2)
    gnp = sv(PA_at + 1792, 1024, "p (g n) -> p g n", g=2)
    fint = view(gbc_at + 1024, 1024, "p (t c n) -> p t c n", t=AT, c=2)
    finq = sv(PA_at + 2816, 1024, "p (g t c n) -> p g t c n", g=2, t=AT, c=2)
    OB = sv(12032, 1024, "p (s n) -> p s n", s=NS)
    VT = sv(13056, 1024, "p (s n) -> p s n", s=NS)
    PRE = 14080
    FG = sv(PRE, 4128, "p (f z t s n) -> p f z t s n", f=2, z=2, t=AT, s=NS)
    Ab = sv(PRE + 4128, 2048, "p (z t n) -> p z t n", z=2, t=AT)
    KZ = sv(PRE + 6176, 2048, "p (z t n) -> p z t n", z=2, t=AT)
    KK = sv(PRE + 8224, 1024, "p (t n) -> p t n", t=AT)
    MAT = sv(PRE, 4096, "p (g i c n) -> p g i c n", g=2, i=4, c=4)
    LS = sv(PRE + 4096, 2048, "p (g b i n) -> p g b i n", g=2, b=2, i=4)
    LT = sv(PRE + 6144, 2048, "p (g b i n) -> p g b i n", g=2, b=2, i=4)
    XS = sv(PRE + 8192, 1024, "p (g b n) -> p g b n", g=2, b=2)
    S0 = sv(PRE + 9248, 512, "p (z t n) -> p z t n", z=2, t=AT)
    STS = sv(PRE + 9760, 512, "p (b n) -> p b n", b=2)
    w0b = view(gbc_at, 1024, "p (z n) -> p z n", z=2)
    CONV = view(gbc_at, 1024, "p (t n) -> p t n", t=AT)
    prod = view(gbc_at + 1024, 1024, "p (t n) -> p t n", t=AT)
    yb, tb = view(gbc_at + 1024, 512), view(gbc_at + 1536, 512)
    sigb = [tb, yb]
    glu = view(lnp_at, 1264, "p (t s n) -> p t s n", t=AT, s=NS)
    gup = view(lnp_at + 1264, 512)
    cb = small[:, 0:32].rearrange("p (g z t s) -> p g z t s", g=2, z=2, t=AT)
    bon = small[:, 32:48]
    fsc = small[:, 48:64].rearrange("p (z t s) -> p z t s", z=2, t=AT)
    st8 = small[:, 64:112]
    bns = small[:, 112:144]
    lns = small[:, 144:160]
    zl = sv(0, 2048, "p (s n) -> p s n", s=NS)

    QKV = sv(0, 6144, "p (s n) -> p s n", s=NS)
    QR = sv(6144, 2048, "p (q n) -> p q n", q=2)
    rt = sv(8192, 2048, "p (q n) -> p q n", q=4)
    QT = sv(10240, 2048, "p (s h n) -> p s h n", s=NS, h=H)
    KTp = sv(12288, 1024, "p (h n) -> p h n", h=H)
    KTs = sv(13312, 2048, "p (h n) -> p h n", h=H)
    CV = sv(15360, 1024)
    CK = sv(16384, 1024)
    PB = sv(17408, 2048, "p (b z m n) -> p b z m n", b=2, z=2, m=2)
    AB = sv(19456, 1024, "p (b m n) -> p b m n", b=2, m=2)
    ATb = sv(20480, 1024, "p (b n) -> p b n", b=2)
    OO = sv(21504, 2048, "p (s n) -> p s n", s=NS)
    t1k = sv(8192, 1024)
    subg = sv(23552, 128)
    lqk = sv(23680, 256, "p (g n) -> p g n", g=4)
    lam = small[:, 160:168]
    sm1 = small[:, 168:232].rearrange("p (n c) -> p n c", c=16)
    zl1 = sv(6144, 2048, "p (s n) -> p s n", s=NS)

    assert turn[FIRST_OF_1] % 3 == 2
    EW = sv(0, 4 * 6144, "p (b n) -> p b n", b=4)
    er = ring_at

    def ev(at, n, pattern=None, **sizes):
        assert at + n <= 8192
        return view(er + at, n, pattern, **sizes)

    hb = ev(0, 2048, "p (s n) -> p s n", s=NS)
    xg = ev(2048, 1024, "p (k n) -> p k n", k=KT)
    ysb = ev(3072, 1024)
    zm = ev(3072, 2048, "p (s n) -> p s n", s=NS)
    sel = ev(5120, 256, "p (s n) -> p s n", s=NS)
    gsel = ev(5376, 512, "p (c s n) -> p c s n", c=2, s=NS)
    hid = ev(5888, 512, "p (c n) -> p c n", c=2)
    tT = [ev(6400, 512), sv(24576, 512)]
    rw = ev(6912, 288, "p (k n) -> p k n", k=KT)
    rb = ev(7200, 36)
    rt_ = ev(7240, 952)
    R_LG, R_A, R_OHG, R_EX, R_T4, R_EIN, R_O1, R_O2, R_OH, R_NB, R_CMP, R_SL, R_ZERO, R_S, R_P1 = (
        0, 72, 80, 88, 96, 160, 176, 192, 208, 272, 400, 440, 504, 632, 696)
    R_P2, R_T = 760, 824


    block = ctx.enter_context(nc.Block())

    def norm_no(l, w, s):
        return (l * 2 + w) * 2 + s

    def bias_at(n):
        return mbias3 if n == 3 else mbias[:, n % 3, :]

    def bias_dma(eng, n):
        l, c = MOD_ORDER[n]
        eng.dma_start(bias_at(n)[0:2, :], a["mod_b"][l:l + 1, c * 512:(c + 1) * 512].partition_broadcast(2))\
            .then_inc(S(f"ld_mbias{n % 3}" if n >= 4 else "ld_mbias_first"), 16)

    @block.sync
    def _(sp):
        sp.dma_start(condw[:, 32:48], a["cond"].rearrange("p k s -> p (k s)")).then_inc(S("ld_cond"), 16)
        load_chunk(sp, 0)
        sp.wait_ge(S("mbias_zero"), 2)
        for n in range(4):
            bias_dma(sp, n)
        sp.dma_start(cst, a["cst"]).then_inc(S("ld_cst"), 16)
        load_chunk(sp, 1)
        load_chunk(sp, 2)
        sp.dma_start(x[:, 0, :], a["x_prompt"]).then_inc(S("ld_x"), 16)
        sp.dma_start(x[:, 1, :], a["x_sample"]).then_inc(S("ld_x"), 16)
        load_chunk(sp, 3)
        sp.dma_start(vec, a["vec"]).then_inc(S("ld_vec"), 16)
        for i in range(4, 6):
            load_chunk(sp, i)
        sp.dma_start(wup, a["ev_w_up"]).then_inc(S("ld_up"), 16)
        sp.dma_start(aup, a["ev_a_up"]).then_inc(S("ld_up"), 16)
        sp.dma_start(gup, a["ev_g_up"]).then_inc(S("ld_up"), 16)
        for i in range(6, FIRST_OF_1 + 1):
            if i == 8:
                BK.wait_filled(sp, ("mod", 0, 3))
                sp.dma_start(S0, a["s0t"]).then_inc(S("ld_s0"), 16)
            load_chunk(sp, i)
        for l in range(2):
            BK.wait_filled(sp, ("mix", l, 1, 1))
            sp.dma_start(rw, a["r_w"][l].rearrange("p (k n) -> p k n", k=KT)).then_inc(S("ld_rw"), 16)
            sp.wait_ge(S("x_new"), norm_no(l, 0, 1) + 1)
            sp.wait_ge(S(f"meta{l}"), 1)
            if l == 1:
                sp.wait_ge(S("cache_out"), 32)
            pairs = sp.value_load(meta[0:1, l, 0:1], min_val=1, max_val=10)

            def step(n, it, u):
                expert = []
                for part, (lo, hi), done, each in (("gate_up", (0, 4096), "gu_done", 1), ("down", (4096, 6144), "down", 2)):
                    sp.wait_ge(S(f"{done}{l}"), (it * 2 + (u + 1)) * each)
                    for c in range(2):
                        if part == "gate_up":
                            expert.append(sp.value_load(meta[0:1, l, bass.ds(it * 4 + (2 * u + c + 4), 1)],
                                                        min_val=0, max_val=NE - 1))
                        sp.dma_start(EW[:, 2 * u + c, lo:hi],
                                     a["w_exp"][l, bass.ds(expert[c], 1), :, lo:hi].rearrange("e p n -> p (e n)"))\
                            .then_inc(S(f"{part}_loaded{l}_{u}"), 16)

            with sp.Fori(0, pairs) as it:
                for u in range(2):
                    step(it * 2 + u, it, u)
            odd = sp.value_load(meta[0:1, l, 1:2], min_val=0, max_val=1)
            with sp.If(odd):
                step(pairs * 2, pairs, 0)
            if l == 0:
                sp.wait_ge(S("x_new"), norm_no(0, 1, 1) + 1)
                sp.dma_start(CK, a["cache_k"]).then_inc(S("ld_cache"), 16)
                sp.dma_start(CV, a["cache_v"]).then_inc(S("ld_cache"), 16)
                for i in range(FIRST_OF_1 + 1, len(chunks)):
                    load_chunk(sp, i)
        for s in range(NS):
            sp.wait_ge(S("x_new"), norm_no(1, 1, s) + 1)
            sp.dma_start(o["y"][s], x[:, s, :]).then_inc(S("y_out"), 16)
        sp.wait_ge(S("y_out"), 32)

    @block.gpsimd
    def _(pool):
        def bias_load(n):
            BK.wait_drained(pool, MODS[n - 3])
            bias_dma(pool, n)

        pool.memset(raw, 0.0).then_inc(S("zeroed"), 1)
        pool.memset(glu, 0.0).then_inc(S("zeroed"), 1)
        pool.dma_start(w0b, a["ev_w0"].partition_broadcast(P)).then_inc(S("ld_w0"), 16)
        pool.dma_start(rope, a["rope"]).then_inc(S("ld_rope"), 16)
        for n in range(4, 7):
            bias_load(n)
        pool.wait_ge(S("ops"), 8)
        pool.wait_ge(S("prod"), 1)
        BK.wait_filled(pool, ("V", 1))
        pool.dma_start(cln, a["ev_cln"].partition_broadcast(P)).then_inc(S("ld_cln"), 16)
        pool.dma_start(gnp, a["ev_gn"].partition_broadcast(P)).then_inc(S("ld_gn"), 16)
        states = 0
        for n, (l, c) in enumerate(MOD_ORDER[7:], 7):
            bias_load(n)
            while states < 4 and BK.no[("st", states // 2, states % 2)] < BK.no[("mod", l, c)]:
                z, g = states // 2, states % 2
                BK.wait_drained(pool, ("st", z, g))
                pool.dma_start(o["state"][z, g::2].rearrange("h v k -> v h k"),
                               STS[0:HD, states % 2, :].rearrange("v (h k) -> v h k", h=4))\
                    .then_inc(S("state_out"), 16)
                states += 1

        def ln_load(l, w):
            n = l * 2 + w
            if n == 0:
                pool.wait_ge(S("conv"), CONV_W * AT)
                BK.wait_drained(pool, ("g", 1))
            else:
                pool.wait_ge(S("x_new"), 2 * n)
            pool.dma_start(lnp, a["ln"][n].partition_broadcast(P)).then_inc(S("ld_ln"), 16)

        ln_load(0, 0)
        for l in range(2):
            BK.wait_filled(pool, ("mix", l, 1, 1))
            pool.dma_start(rb, a["r_b"][l].partition_broadcast(P)).then_inc(S("ld_rb"), 16)
            ln_load(l, 1)
            if l == 0:
                ln_load(1, 0)
                pool.dma_start(subg, a["subln"].partition_broadcast(P)).then_inc(S("ld_sub"), 16)
                pool.dma_start(lqk, a["lqk"].partition_broadcast(P)).then_inc(S("ld_sub"), 16)
                BK.wait_drained(pool, ("qkv", 0, 3))
                pool.dma_start(o["cache_k"], QKV[:, 0, D:2 * D]).then_inc(S("cache_out"), 16)
                BK.wait_drained(pool, ("qkv", 0, 5))
                pool.dma_start(o["cache_v"], QKV[:, 0, 2 * D:3 * D]).then_inc(S("cache_out"), 16)
        pool.wait_ge(S("state_out"), 64)
        pool.wait_ge(S("cache_out"), 32)

    @block.tensor
    def _(pe):
        def mod(l, c):
            key = ("mod", l, c)
            wait_chunk(pe, key)
            BK.wait_free(pe, key)
            w, bank = slot(key), BK.bank(key)
            for k in range(KT):
                q = 32 * (k % 4)
                mm = pe.matmul(bank[q:q + 32, :], cond[:, k, :], w[:, k, :], start=(k < 4), stop=(k >= 4),
                               skip_group_check=True)
            mm.then_inc(filled, 1)

        def fold(l, c):
            part, half = c // 2, c % 2
            pick = cst[:, C_SEL:C_SEL + 2 * P:P]
            if part in (2, 5):
                key = ("gate", l, c)
                BK.wait_free(pe, key)
                BK.wait_drained(pe, ("mod", l, c))
                q = 32 * gate_slot(l, part)
                pe.matmul(BK.bank(key)[q:q + 2, :], pick, rowbuf[:, half * 512:half * 512 + 512], start=True, stop=True)\
                    .then_inc(filled, 1)
            elif half:
                key = ("modT", l, part)
                BK.wait_free(pe, key)
                BK.wait_drained(pe, ("mod", l, c))
                for k in range(KT):
                    mm = pe.matmul(BK.bank(key)[:, 2 * k:2 * k + 2], rowbuf[:, k * P:(k + 1) * P], pick,
                                   start=True, stop=True)
                mm.then_inc(filled, 1)

        def transposes(key, tiles):
            BK.wait_free(pe, key)
            bank = BK.bank(key)
            for n, t in enumerate(tiles):
                mm = pe.transpose(bank[:, n * P:(n + 1) * P], t, ident)
            mm.then_inc(filled, 1)

        def x_transposes(tag):
            for s in range(NS):
                for h2 in range(2):
                    transposes(("xT", tag, s, h2), [x[:, s, (4 * h2 + n) * P:(4 * h2 + n + 1) * P] for n in range(4)])

        def wait_hT(tag):
            for h2 in range(2):
                BK.wait_drained(pe, ("xT", tag, 1, h2))

        def gate_row(l, w, s, n):
            part, key = (2 if w == 0 else 5), ("gbc", l, w, s, n)
            BK.wait_free(pe, key)
            if s == 0:
                BK.wait_drained(pe, ("gate", l, 2 * part + n))
            q = 32 * gate_slot(l, part)
            pe.matmul(BK.bank(key), cst[q:q + 2, C_SEL + s * P:C_SEL + (s + 1) * P],
                      gaterow[q:q + 2, n * 512:(n + 1) * 512], start=True, stop=True).then_inc(filled, 1)

        def gate_rows(l, w):
            for s in range(NS):
                for n in range(2):
                    gate_row(l, w, s, n)

        def project_out(l, s, n):
            if n == 0:
                for h2 in range(2):
                    BK.wait_drained(pe, ("oT", l, s, h2))
            key = ("mix", l, s, n)
            if s == 0:
                wait_chunk(pe, ("out", l, n))
            BK.wait_free(pe, key)
            for k in range(KT):
                mm = pe.matmul(BK.bank(key), hT[:, k, s * T:(s + 1) * T], slot(("out", l, n))[:, k, :],
                               start=(k == 0), stop=(k == KT - 1))
            mm.then_inc(filled, 1)

        def out_tiles_0(s):
            for h2 in range(2):
                pe.wait_ge(S("mixed_a" if h2 == 0 else "mixed_b"), s + 1)
                src = VT if h2 == 0 else OB
                transposes(("oT", 0, s, h2), [src[:, s, t * P:(t + 1) * P] for t in range(AT)])

        pe.wait_ge(S("cond"), 1)
        pe.wait_ge(S("ld_cst"), 16)
        for c in range(4):
            mod(0, c)
            fold(0, c)
        pe.wait_ge(S("ld_x"), 32)
        x_transposes("m0")
        wait_hT("m0")
        for key in PROJECTION:
            kind = key[0]
            if key == ("w", 0, 0):
                pe.wait_ge(S("ld_up"), 48)
                pe.wait_ge(S("lora"), 1)
            elif key == ("ss", 0):
                pe.wait_ge(S("sq"), 1)
            elif key == ("cum", 0, 0):
                pe.wait_ge(S("sigw"), 4)
            elif key == ("V", 0):
                pe.wait_ge(S("shifted"), NPA)
            elif kind == "bonus":
                pe.wait_ge(S("prod"), 1)
            if kind == "V":
                transposes(key, [V_[:, t, key[1] * T:(key[1] + 1) * T] for t in range(AT)])
                continue
            BK.wait_free(pe, key)
            bank = BK.bank(key)
            if kind in ("pa", "pb"):
                tiles = [key[1]] if kind == "pa" else [NPA + 2 * key[1], NPA + 2 * key[1] + 1]
                for n, i in enumerate(tiles):
                    wait_chunk(pe, ("evin", i // 4))
                    for k in range(KT):
                        mm = pe.matmul(bank[:, n * 256:n * 256 + 256],
                                       slot(("evin", i // 4))[:, k, (i % 4) * P:(i % 4 + 1) * P],
                                       hT[:, k, :], start=(k == 0), stop=(k == KT - 1))
            elif kind == "w":
                _, s, z = key
                mm = pe.matmul(bank, PA[64 * z:64 * z + 64, 0, s * T:(s + 1) * T], wup[64 * z:64 * z + 64, :],
                               start=True, stop=True)
            elif kind == "ss":
                mm = pe.matmul(bank, blk, sq[:, key[1] * 512:(key[1] + 1) * 512], start=True, stop=True)
            elif kind == "a":
                _, z, tp = key
                for t2 in range(2):
                    t = 2 * tp + t2
                    mm = pe.matmul(bank[:, t2 * 256:t2 * 256 + 256], aup[64 * z:64 * z + 64, t * P:(t + 1) * P],
                                   PA[64 * z:64 * z + 64, 1, :], start=True, stop=True)
            elif kind == "cum":
                _, z, t = key
                for s in range(NS):
                    mm = pe.matmul(bank[:, s * 130:s * 130 + 129], lw[:, s, z, t * P:(t + 1) * P],
                                   cst[:, C_CUM:C_CUM + T + 1], start=True, stop=True)
            else:
                for s in range(NS):
                    for t in range(AT):
                        mm = pe.matmul(bank[:, s * 8:s * 8 + 8], prod[:, t, s * T:(s + 1) * T],
                                       cst[:, C_HSEL + t * H:C_HSEL + (t + 1) * H], start=(t == 0), stop=(t == AT - 1))
            mm.then_inc(filled, 1)

        for (s, z) in PAIRS:
            pe.wait_ge(S("ops"), 4 * z + 4)
            for i in range(4):
                for g in range(2):
                    BK.wait_free(pe, ("gram", s, z, g, i))
                for c in range(2):
                    for g in range(2):
                        op = OPS[64 * g:64 * g + 64, z, i, s]
                        mm = pe.matmul(BK.bank(("gram", s, z, g, i))[:, c * 256:c * 256 + 256], op[:, 2 + c, :],
                                       op[:, 0:2, :], start=True, stop=True)
                        if c == 1:
                            mm.then_inc(filled, 1)
            for g in range(2):
                BK.wait_free(pe, ("L", s, z, g, 0))
            for i in range(4):
                for g in range(2):
                    op = OPS[64 * g:64 * g + 64, z, i, s]
                    mm = pe.matmul(BK.bank(("L", s, z, g, 0))[:, i * P:(i + 1) * P], op[:, 0, :], op[:, 2, :],
                                   start=True, stop=True)
                    if i == 3:
                        mm.then_inc(filled, 1)
            if s == 0 and z == 0:
                BK.wait_drained(pe, ("V", 1))
            if s == 1 and z == 0:
                pe.wait_ge(S("s0"), 1)
            for g in range(2):
                key = ("B", s, z, g)
                BK.wait_free(pe, key)
                BK.wait_drained(pe, ("gram", s, z, g, 3))
                for i in range(4):
                    h, t, b = 2 * i + g, i, 64 * g
                    dst = BK.bank(key)[:, i * HD:(i + 1) * HD]
                    mm = pe.matmul(dst, MAT[:, g, i, 2, :], VT[:, s, h * HD:(h + 1) * HD], start=True, stop=(s == 0))
                    if s == 1:
                        mm = pe.matmul(dst, OPS[b:b + 64, z, t, s, 0, :], S0[b:b + 64, z, t, :], start=False, stop=True)
                mm.then_inc(filled, 1)
            for j in range(LEVELS):
                for g in range(2):
                    lt = [MAT[:, g, i, 0, :] if j == 0 else LT[:, g, j % 2, i, :] for i in range(4)]
                    if j == 0:
                        BK.wait_drained(pe, ("B", s, z, g))
                        BK.wait_drained(pe, ("L", s, z, g, 0))
                    else:
                        BK.wait_drained(pe, ("LT", s, z, g, j))
                        BK.wait_drained(pe, ("X", s, z, g, j - 1))
                    key = ("X", s, z, g, j)
                    BK.wait_free(pe, key)
                    for i in range(4):
                        mm = pe.matmul(BK.bank(key)[:, i * HD:(i + 1) * HD], lt[i], XS[:, g, j % 2, i * HD:(i + 1) * HD],
                                       start=True, stop=True)
                    mm.then_inc(filled, 1)
                    if j < LEVELS - 1:
                        if j:
                            BK.wait_drained(pe, ("L", s, z, g, j))
                        key = ("L", s, z, g, j + 1)
                        if j < LEVELS - 2:
                            BK.wait_free(pe, key)
                            for i in range(4):
                                mm = pe.matmul(BK.bank(key)[:, i * P:(i + 1) * P], lt[i], LS[:, g, j % 2, i, :],
                                               start=True, stop=True)
                            mm.then_inc(filled, 1)
                        key = ("LT", s, z, g, j + 1)
                        BK.wait_free(pe, key)
                        for i in range(4):
                            mm = pe.matmul(BK.bank(key)[:, i * P:(i + 1) * P], LS[:, g, j % 2, i, :], lt[i],
                                           start=True, stop=True)
                        mm.then_inc(filled, 1)
                    if g == 0 and (s, z, j) in fold_in:
                        fold(*fold_in[(s, z, j)])
                if (s, z, j) in mod_after:
                    mod(*mod_after[(s, z, j)])
                if (s, z, j) in conv_out:
                    c = conv_out[(s, z, j)]
                    pe.wait_ge(S("conv"), CONV_W * AT)
                    transposes(("cT", c), [CONV[:, t, c * T:(c + 1) * T] for t in range(AT)])
            for g in range(2):
                BK.wait_drained(pe, ("X", s, z, g, LEVELS - 1))
                if s == 1 and (z or g):
                    pe.wait_ge(S("y_even"), z + 1) if g else pe.wait_ge(S("y_done"), 3)
                for i in range(4):
                    h, t, b = 2 * i + g, i, 64 * g
                    dst = ps[:, 6 + s, h * HD:(h + 1) * HD]
                    pe.matmul(dst, MAT[:, g, i, 1, :], XS[:, g, LEVELS % 2, i * HD:(i + 1) * HD],
                              start=(z == 0 and h == 0), stop=False, skip_group_check=True)
                    mm = pe.matmul(dst, MAT[:, g, i, 3, :], VT[:, s, h * HD:(h + 1) * HD],
                                   start=False, stop=(s == 0 and z == 1), skip_group_check=True)
                    if s == 1:
                        mm = pe.matmul(dst, OPS[b:b + 64, z, t, s, 1, :], S0[b:b + 64, z, t, :],
                                       start=False, stop=(z == 1), skip_group_check=True)
                if s == 1 and g == 0:
                    mm.then_inc(S("y_even"), 1)
            mm.then_inc(S("y_done"), 1)
            if s == 0:
                pe.wait_ge(S("fin"), z + 1)
                for g in range(2):
                    b = 64 * g
                    key = ("fT", z, g)
                    BK.wait_free(pe, key)
                    for i in range(4):
                        for c in range(2):
                            mm = pe.transpose(BK.bank(key)[:, (2 * i + c) * HD:(2 * i + c + 1) * HD],
                                              fint[b:b + 64, i, c, :], ident[b:b + 64, b:b + 64])
                    mm.then_inc(filled, 1)
                    key = ("st", z, g)
                    BK.wait_free(pe, key)
                    BK.wait_drained(pe, ("fT", z, g))
                    for i in range(4):
                        h, dst = 2 * i + g, BK.bank(key)[0:HD, i * HD:(i + 1) * HD]
                        pe.matmul(dst, XS[:, g, LEVELS % 2, i * HD:(i + 1) * HD], finq[:, g, i, 0, :],
                                  start=True, stop=False)
                        mm = pe.matmul(dst, VT[:, s, h * HD:(h + 1) * HD], finq[:, g, i, 1, :],
                                       start=False, stop=True)
                    mm.then_inc(filled, 1)
            if (s, z) == (1, 1):
                out_tiles_0(0)
            if z == 1:
                key = ("g", s)
                BK.wait_free(pe, key)
                pe.wait_ge(S("lora"), 2)
                pe.matmul(BK.bank(key), PA[:, 2, s * T:(s + 1) * T], gup, start=True, stop=True).then_inc(filled, 1)

        for s in range(NS):
            if s == 1:
                out_tiles_0(1)
            for n in range(2):
                gate_row(0, 0, s, n)
            for n in range(2):
                project_out(0, s, n)

        def moe(l):
            for s in range(NS):
                pe.wait_ge(S("x_new"), norm_no(l, 0, s) + 1)
                for h2 in range(2):
                    transposes(("xT", f"e{l}", s, h2), [x[:, s, (4 * h2 + n) * P:(4 * h2 + n + 1) * P] for n in range(4)])
                for h2 in range(2):
                    BK.wait_drained(pe, ("xT", f"e{l}", s, h2))
                key = ("lg", l, s)
                BK.wait_free(pe, key)
                pe.wait_ge(S("ld_rw"), 16 * (l + 1))
                for k in range(KT):
                    mm = pe.matmul(BK.bank(key)[:, 0:36], hT[:, k, s * T:(s + 1) * T], rw[:, k, :],
                                   start=(k == 0), stop=(k == KT - 1))
                mm.then_inc(filled, 1)
                for h2 in range(2):
                    transposes(("hb", l, s, h2), [hT[:, 4 * h2 + n, s * T:(s + 1) * T] for n in range(4)])
            key = ("pos", l)
            BK.wait_free(pe, key)
            pe.wait_ge(S("chosen"), l + 1)
            bank, OH = BK.bank(key), rt_[:, R_OH:R_OH + 64]
            pe.matmul(bank[:, 0:32], SU, OH[:, 0:32], start=True, stop=True)
            pe.matmul(bank[:, 32:64], SU, OH[:, 32:64], start=True, stop=False)
            pe.matmul(bank[:, 32:64], ones, OH[:, 0:32], start=False, stop=True)
            pe.matmul(bank[0:32, 64:65], OH[:, 0:32], ones[:, 0:1], start=True, stop=False)
            pe.matmul(bank[0:32, 64:65], OH[:, 32:64], ones[:, 0:1], start=False, stop=True).then_inc(filled, 1)
            key = ("base", l)
            BK.wait_free(pe, key)
            pe.wait_ge(S("nchunks"), l + 1)
            bank, nb = BK.bank(key), rt_[0:32, R_NB:R_NB + P]
            pe.matmul(bank[:, 0:32], nb, SU[0:32, 0:32], start=True, stop=True)
            pe.matmul(bank[:, 32:33], nb, ones[0:32, 0:1], start=True, stop=True)
            pe.matmul(bank[0:32, 64:65], UI[0:32, 0:32], nb[:, 0:1], start=True, stop=True).then_inc(filled, 1)
            key = ("eid", l)
            BK.wait_free(pe, key)
            pe.wait_ge(S("ended"), l + 1)
            pe.matmul(BK.bank(key)[0:1, 0:40], ones[0:32, 0:1], rt_[0:32, R_CMP:R_CMP + 40], start=True, stop=True)\
                .then_inc(filled, 1)
            pe.sem_inc(S(f"gu_done{l}"), 2)
            pe.sem_inc(S(f"down{l}"), 4)
            gate_rows(l, 1)
            BK.wait_drained(pe, ("eid", l))
            BK.wait_drained(pe, ("gbc", l, 1, 1, 1))
            pe.wait_ge(S("zero"), l + 1)
            for n in range(4):
                pe.matmul(ps[:, n, :], rt_[:, R_ZERO:R_ZERO + P], cst[:, 0:512], start=True, stop=False,
                          skip_group_check=True)

            def gather(n):
                pe.wait_ge(S(f"selected{l}"), n + 1)
                for k in range(KT):
                    for s in range(NS):
                        mm = pe.matmul(ps[:, 4 + k // 4, (k % 4) * P:(k % 4 + 1) * P], hb[:, s, k * P:(k + 1) * P],
                                       sel[:, s, :], start=(s == 0), stop=(s == 1))
                    if k % 4 == 3:
                        mm.then_inc(S(f"gathered{l}"), 1)

            def scatter(n, u, last=False):
                pe.wait_ge(S(f"y_read{l}"), n + 2)
                pe.wait_ge(S(f"y_read_dve{l}"), n + 2)
                for s in range(NS):
                    for half in range(2):
                        mm = pe.matmul(ps[:, 2 * s + half, :], tT[u][:, (2 + s) * P:(3 + s) * P],
                                       ysb[:, half * 512:(half + 1) * 512], start=False, stop=last,
                                       skip_group_check=True)
                return mm

            gather(0)
            pe.wait_ge(S(f"meta{l}"), 1)
            pairs, odd, even = (pe.value_load(meta[0:1, l, m:m + 1], min_val=lo, max_val=hi)
                                for m, lo, hi in ((0, 1, 10), (1, 0, 1), (2, 0, 1)))
            def step(n, it, u):
                pe.wait_ge(S(f"xg_act{l}"), n + 1)
                pe.wait_ge(S(f"xg_dve{l}"), n + 1)
                pe.wait_ge(S(f"gate_up_loaded{l}_{u}"), it * 32 + 32)
                for k in range(KT):
                    for c in range(2):
                        mm = pe.matmul(ps[64 * c:64 * c + 64, 6, :], xg[:, k, 64 * c:64 * c + 64],
                                       EW[:, 2 * u + c, k * 512:(k + 1) * 512],
                                       start=(k == 0), stop=(k == KT - 1), skip_group_check=True)
                mm.then_inc(S(f"gu_done{l}"), 1)
                pe.wait_ge(S(f"y_read{l}"), n + 1)
                pe.wait_ge(S(f"y_read_dve{l}"), n + 1)
                gather(n + 1)
                pe.wait_ge(S(f"gates{l}"), n + 1)
                for s in range(NS):
                    pe.transpose(ps[:, 7, (2 + s) * P:(3 + s) * P], gsel[:, 0, s, :], ident)
                pe.wait_ge(S(f"hid{l}"), n + 1)
                for f in range(2):
                    mm = pe.transpose(ps[:, 7, f * P:(f + 1) * P], hid[:, 1, f * P:(f + 1) * P], ident)
                mm.then_inc(S(f"turned{l}"), 1)
                scatter(n - 1, 1 - u)
                pe.wait_ge(S(f"tT{l}"), n + 1)
                pe.wait_ge(S(f"xg_act{l}"), n + 2)
                pe.wait_ge(S(f"xg_dve{l}"), n + 2)
                pe.wait_ge(S(f"down_loaded{l}_{u}"), it * 32 + 32)
                for half in range(2):
                    for f in range(2):
                        for c in range(2):
                            w = EW[:, 2 * u + c, 4096 + f * D + half * 512:4096 + f * D + half * 512 + 512]
                            mm = pe.matmul(ps[64 * c:64 * c + 64, 4 + half, :],
                                           tT[u][:, f * P + 64 * c:f * P + 64 * c + 64], w,
                                           start=(f == 0), stop=(f == 1), skip_group_check=True)
                    mm.then_inc(S(f"down{l}"), 1)

            with pe.Fori(0, pairs) as it:
                for u in range(2):
                    step(it * 2 + u, it, u)
            with pe.If(odd):
                step(pairs * 2, pairs, 0)
                scatter(pairs * 2, 0, last=True).then_inc(S("summed"), 1)
            with pe.If(even):
                scatter(pairs * 2 - 1, 1, last=True).then_inc(S("summed"), 1)

        moe(0)

        def project_in(s, c):
            key = ("qkv", s, c)
            wait_chunk(pe, ("odin", c))
            BK.wait_free(pe, key)
            for k in range(KT):
                mm = pe.matmul(BK.bank(key), hT[:, k, s * T:(s + 1) * T], slot(("odin", c))[:, k, :],
                               start=(k == 0), stop=(k == KT - 1))
            mm.then_inc(filled, 1)

        pe.wait_ge(S("sums_read"), NS)
        for s in range(NS):
            pe.wait_ge(S("x_new"), norm_no(0, 1, s) + 1)
            for h2 in range(2):
                transposes(("xT", "m1", s, h2), [x[:, s, (4 * h2 + n) * P:(4 * h2 + n + 1) * P] for n in range(4)])
            for h2 in range(2):
                BK.wait_drained(pe, ("xT", "m1", s, h2))
            project_in(s, 0)
        for c in range(1, 6):
            for s in range(NS):
                project_in(s, c)
        pe.wait_ge(S("ld_cache"), 32)
        for h2 in range(2):
            transposes(("cT1", h2), [CK[:, (4 * h2 + n) * P:(4 * h2 + n + 1) * P] for n in range(4)])
        for s in range(NS):
            for q in range(2):
                if s == 0:
                    BK.wait_drained(pe, ("qkv", 0, 2 * q + 1))
                else:
                    pe.wait_ge(S("roped"), q + 1)
                src = QKV[:, 0, q * D:(q + 1) * D] if s == 0 else QR[:, q, :]
                for h2 in range(2):
                    transposes(("qkT", s, q, h2), [src[:, (4 * h2 + n) * P:(4 * h2 + n + 1) * P] for n in range(4)])
        def out_tiles(s):
            pe.wait_ge(S("attended"), s + 1)
            for h2 in range(2):
                transposes(("oT", 1, s, h2), [OO[:, s, (4 * h2 + n) * P:(4 * h2 + n + 1) * P] for n in range(4)])

        for n in range(len(PAIRS1) + 1):
            if n < len(PAIRS1):
                s, hp = PAIRS1[n]
                BK.wait_drained(pe, ("qkT", s, 1, hp // 2))
                for z in range(2):
                    key = ("sc", s, hp, z)
                    BK.wait_free(pe, key)
                    for m in range(2):
                        h = 2 * hp + m
                        keys = KTp[64 * z:64 * z + 64, h, :] if s == 0 else KTs[64 * z:64 * z + 64, h, :]
                        mm = pe.matmul(BK.bank(key)[:, m * 256:m * 256 + T * (s + 1)], QT[64 * z:64 * z + 64, s, h, :],
                                       keys, start=True, stop=True)
                    mm.then_inc(filled, 1)
            if n >= 1:
                s, hp = PAIRS1[n - 1]
                b = (n - 1) % 2
                pe.wait_ge(S("attn"), 2 * n)
                transposes(("aT", s, hp), [AB[:, b, m, i * P:(i + 1) * P] for m in range(2) for i in range(s + 1)])
                if n % 2 == 0:
                    key = ("pv", s, hp // 2)
                    BK.wait_free(pe, key)
                    BK.wait_drained(pe, ("aT", s, hp))
                    for m in range(4):
                        hh = 2 * hp - 2 + m
                        for i in range(s + 1):
                            own_v = QKV[:, s, 2 * D + hh * P:2 * D + (hh + 1) * P]
                            vals = CV[:, hh * P:(hh + 1) * P] if (s, i) == (1, 0) else own_v
                            at = (m % 2) * (s + 1) + i
                            mm = pe.matmul(BK.bank(key)[:, m * P:(m + 1) * P], ATb[:, m // 2, at * P:(at + 1) * P], vals,
                                           start=(i == 0), stop=(i == s))
                    mm.then_inc(filled, 1)
            for key in beside.get(n, []):
                if key[0] == "gbc":
                    gate_row(*key[1:])
                elif key[0] == "mix":
                    project_out(*key[1:])
                elif key[-1] == 0:
                    out_tiles(0)
        out_tiles(1)
        for n in range(2):
            project_out(1, 1, n)
        moe(1)


    @block.scalar
    def _(act):
        A = nc.scalar.activation
        own = Steps(act, S("act_steps"))

        def take(key):
            BK.wait_filled(act, key)
            return BK.bank(key)

        def copy(key, out, n=512):
            BK.drained_by(A(out, take(key)[:, 0:n], ACT.Copy), key)

        def modulated(key, s, k0, l, part):
            bank = take(key)
            BK.wait_drained(act, ("modT", l, part + 1))
            for n in range(4):
                k = k0 + n
                ins = A(hT[:, k, s * T:(s + 1) * T], bank[:, n * P:(n + 1) * P], ACT.Identity,
                        bias=modT[:, l, part, k, s:s + 1], scale=modT[:, l, part + 1, k, s:s + 1])
            BK.drained_by(ins, key)

        def rsqrt(out, src, ready, n, done):
            act.wait_ge(S(ready), n)
            own.link(A(out, src, ACT.Ln))
            A(out, out, ACT.Exp, scale=-0.5).then_inc(S(done), 1)

        def gate_row(l, c):
            part, half = c // 2, c % 2
            if part in (2, 5):
                key, q = ("gate", l, c), 32 * gate_slot(l, part)
                BK.drained_by(A(gaterow[q:q + 2, half * 512:half * 512 + 512], take(key)[q:q + 2, :], ACT.Copy), key)

        def gate_rows(l, w):
            for s in range(NS):
                for n in range(2):
                    copy(("gbc", l, w, s, n), gbc[:, s, n * 512:(n + 1) * 512])

        act.wait_ge(S("ld_cond"), 16)
        A(condw[:, 0:16], condw[:, 32:48], ACT.Exp, scale=-1.0).then_inc(S("cond_exp"), 1)
        for s in range(NS):
            modulated(("xT", "m0", s, 0), s, 0, 0, 0)
        act.wait_ge(S("zeroed"), 1)
        act.wait_ge(S("vecs"), 1)
        def projected(i):
            key = ("pa", i)
            bank = take(key)
            if i >= 4:
                act.wait_ge(S("shifted"), i - 3)
            A(raw[:, i % 4, :, 1:129], bank[:, 0:256].rearrange("p (s n) -> p s n", s=NS), ACT.Copy)\
                .then_inc(S("act_raw"), 1)
            BK.drained_by(A(PA[:, i, :], bank[:, 0:256], ACT.Copy, scale=nvec[:, TILES[i]:TILES[i] + 1]), key)
            if i == 4:
                act.wait_ge(S("shifted"), 1)
                A(PA[:, 0, :], PA[:, 0, :], ACT.Exp, scale=-2.0).then_inc(S("lora_exp"), 1)
                act.wait_ge(S("shifted"), 3)
                A(PA[:, 2, :], PA[:, 2, :], ACT.Exp, scale=-1.0).then_inc(S("lora_exp"), 1)
            if i == 10:
                act.wait_ge(S("kk"), 1)
                A(sq, KK.rearrange("p t n -> p (t n)"), ACT.Square).then_inc(S("sq"), 1)

        def halved(t):
            bank = take(("pb", t))
            if t >= 2:
                BK.wait_drained(act, ("pb", t - 2))
            A(eg[:, t % 2, :], bank[:, 256:512], ACT.Exp, bias=nvec[:, 38 + 4 + t:39 + 4 + t], scale=-1.0)\
                .then_inc(S("eg"), 1)

        def decay(s, z):
            BK.wait_drained(act, ("w", s, z))
            A(lw[:, s, z, :], lw[:, s, z, :], ACT.Exp, scale=-1.0).then_inc(S("lw_exp"), 1)

        def key_norms():
            BK.wait_drained(act, ("ss", 1))
            own.link(A(sq, sq, ACT.Ln, scale=float(2 ** 32)))
            A(sq, sq, ACT.Exp, scale=-0.5).then_inc(S("rs"), 1)

        def learning_rate(z, tp):
            bank = take(("a", z, tp))
            for t2 in range(2):
                t = 2 * tp + t2
                ins = A(Ab[:, z, t, :], bank[:, t2 * 256:t2 * 256 + 256], ACT.Exp,
                        bias=nvec[:, 30 + 4 * z + t:31 + 4 * z + t], scale=-1.0)
            BK.drained_by(ins, ("a", z, tp))

        def decays(z, t):
            bank = take(("cum", z, t))
            act.wait_ge(S("centres"), z * AT + t + 1)
            for s in range(NS):
                own.inc(A(FG[:, 0, z, t, s, :], bank[:, s * 130:s * 130 + 129], ACT.Exp, bias=cb[:, 0, z, t, s:s + 1]))
                ins = A(FG[:, 1, z, t, s, :], bank[:, s * 130:s * 130 + 129], ACT.Exp,
                        bias=cb[:, 1, z, t, s:s + 1], scale=-1.0)
                if s == 0:
                    own.inc(ins)
            BK.drained_by(ins, ("cum", z, t))

        for i in range(11):
            projected(i)
        decay(0, 0)
        decay(0, 1)
        projected(11)
        decay(1, 0)
        decay(1, 1)
        projected(12)
        projected(13)
        for tp in range(2):
            learning_rate(0, tp)
        projected(14)
        key_norms()
        for tp in range(2):
            learning_rate(1, tp)
        halved(0)
        for t in range(AT):
            decays(0, t)
        halved(1)
        halved(2)
        for t in range(AT):
            decays(1, t)
        halved(3)
        for s in range(NS):
            copy(("V", s), VT[:, s, :])

        for (s, z) in PAIRS:
            for g in range(2):
                copy(("B", s, z, g), XS[:, g, 0, :], 256)
            for j in range(LEVELS - 1):
                for g in range(2):
                    if j < LEVELS - 2:
                        copy(("L", s, z, g, j + 1), LS[:, g, (j + 1) % 2].rearrange("p i n -> p (i n)"))
                    if g == 0 and (s, z, j) in fold_in:
                        gate_row(*fold_in[(s, z, j)])
                if (s, z) == (1, 1) and j in (1, 2):
                    rsqrt(st8[:, 31 + j:32 + j], st8[:, 33 + j:34 + j], "cln_var", j, "cln_rstd")
                if (s, z) == (1, 1) and j in (2, 3):
                    act.wait_ge(S("cln_y"), j - 1)
                    A(sigb[j - 2], sigb[j - 2], ACT.Exp, scale=-1.0).then_inc(S("cln_exp"), 1)
            if s == 0:
                for g in range(2):
                    copy(("fT", z, g), finq[:, g].rearrange("p t c n -> p (t c n)"))
                    key = ("st", z, g)
                    bank = take(key)
                    if z == 1:
                        act.wait_ge(S("state_out"), 16 * (g + 1)) if g == 1 else act.wait_ge(S("state_out"), 16)
                    if z == 1 and g == 0:
                        act.wait_ge(S("state_out"), 32)
                    BK.drained_by(A(STS[0:HD, g, :], bank[0:HD, 0:256], ACT.Copy), key)
            if (s, z) == (1, 1):
                copy3(act, BK, ("oT", 0, 0, 0), hT, 0, 0)
            if z == 1:
                rsqrt(st8[:, 16:24], st8[:, 8:16], "gn_var", s + 1, "gn_rstd")

        def norm_rsqrt(l, w, s):
            n = norm_no(l, w, s)
            rsqrt(lns[:, 8 + s:9 + s], lns[:, 4 + s:5 + s], "ln_var", n + 1, "ln_rstd")

        for s in range(NS):
            if s == 0:
                BK.wait_filled(act, ("cT", 1))
            else:
                copy3(act, BK, ("oT", 0, 1, 0), hT, 1, 0)
                act.wait_ge(S("mixed_a"), 2)
            for n in range(2):
                copy(("gbc", 0, 0, s, n), gbc[:, s, n * 512:(n + 1) * 512])

        def moe(l):
            norm_rsqrt(l, 0, 0)
            for h2 in range(2):
                modulated(("xT", f"e{l}", 0, h2), 0, 4 * h2, l, 3)
            norm_rsqrt(l, 0, 1)
            for h2 in range(2):
                copy(("hb", l, 0, h2), hb[:, 0, h2 * 512:(h2 + 1) * 512])
            modulated(("xT", f"e{l}", 1, 0), 1, 0, l, 3)
            act.wait_ge(S("routed1"), l + 1)
            A(rt_[:, R_EX:R_EX + 8], rt_[:, R_EX:R_EX + 8], ACT.Exp).then_inc(S("route_exp"), 1)
            for h2 in range(2):
                copy(("hb", l, 1, h2), hb[:, 1, h2 * 512:(h2 + 1) * 512])
            act.wait_ge(S("routed2"), l + 1)
            A(rt_[:, R_S + 16:R_S + 18], rt_[:, R_S + 16:R_S + 18], ACT.Exp).then_inc(S("route_exp"), 1)
            gate_rows(l, 1)
            act.wait_ge(S(f"meta{l}"), 1)
            pairs, odd = (act.value_load(meta[0:1, l, m:m + 1], min_val=lo, max_val=hi)
                          for m, lo, hi in ((0, 1, 10), (1, 0, 1)))
            act.sem_inc(S(f"y_read{l}"), 1)

            def gathered(n):
                act.wait_ge(S(f"gathered{l}"), n * 2 + 1)
                A(xg[:, 0:4, :].rearrange("p k n -> p (k n)"), ps[:, 4, :], ACT.Copy).then_inc(S(f"xg_act{l}"), 1)

            gathered(0)
            def step(n, it, u):
                act.wait_ge(S(f"gu_done{l}"), n + 3)
                A(hid[:, 0, :], ps[:, 6, 0:256], ACT.Exp, scale=-1.0).then_inc(S(f"gate_exp{l}"), 1)
                gathered(n + 1)
                act.wait_ge(S(f"turned{l}"), n + 1)
                A(tT[u], ps[:, 7, :], ACT.Copy).then_inc(S(f"tT{l}"), 1)
                act.wait_ge(S(f"down{l}"), n * 2 + 5)
                A(ysb[:, 0:512], ps[:, 4, :], ACT.Copy).then_inc(S(f"y_read{l}"), 1)

            with act.Fori(0, pairs) as it:
                for u in range(2):
                    step(it * 2 + u, it, u)
            with act.If(odd):
                step(pairs * 2, pairs, 0)
            norm_rsqrt(l, 1, 0)
            if l == 0:
                for h2 in range(2):
                    modulated(("xT", "m1", 0, h2), 0, 4 * h2, 1, 0)
            norm_rsqrt(l, 1, 1)

        moe(0)

        copy(("qkv", 0, 0), QKV[:, 0, 0:512])
        modulated(("xT", "m1", 1, 0), 1, 0, 1, 0)
        copy(("qkv", 1, 0), QKV[:, 1, 0:512])
        for c in range(1, 6):
            for s in range(NS):
                copy(("qkv", s, c), QKV[:, s, c * 512:(c + 1) * 512])
        act.wait_ge(S("lam_dot"), 1)
        A(lam[:, 2:4], lam[:, 0:2], ACT.Exp).then_inc(S("lam_exp"), 1)

        def keys_out(key, dst):
            BK.drained_by(A(dst, take(key).rearrange("p (h n) -> p h n", h=4), ACT.Copy), key)

        for h2 in range(2):
            keys_out(("cT1", h2), KTs[:, 4 * h2:4 * h2 + 4, 0:P])
        for s in range(NS):
            for q in range(2):
                for h2 in range(2):
                    hs = slice(4 * h2, 4 * h2 + 4)
                    dst = QT[:, s, hs, :] if q == 0 else (KTp[:, hs, :] if s == 0 else KTs[:, hs, P:2 * P])
                    keys_out(("qkT", s, q, h2), dst)
        for n in range(len(PAIRS1) + 1):
            if n < len(PAIRS1):
                s, hp = PAIRS1[n]
                nk = T * (s + 1)
                for z in range(2):
                    bank = take(("sc", s, hp, z))
                    act.wait_ge(S("smax"), 2 * n + z + 1)
                    if n >= 2:
                        act.wait_ge(S("attn"), 2 * n - 2)
                    for m in range(2):
                        ins = A(PB[:, n % 2, z, m, 0:nk], bank[:, m * 256:m * 256 + nk], ACT.Exp,
                                bias=sm1[:, n % 4, 4 + 2 * z + m:5 + 2 * z + m], scale=HD ** -0.5,
                                accum_out=sm1[:, n % 4, 8 + 2 * z + m:9 + 2 * z + m])
                        if m == 0:
                            own.inc(ins)
                    BK.drained_by(ins, ("sc", s, hp, z))
            if n >= 1:
                s, hp = PAIRS1[n - 1]
                b = (n - 1) % 2
                if n >= 3:
                    BK.wait_filled(act, ("pv", PAIRS1[n - 3][0], PAIRS1[n - 3][1] // 2))
                w = 2 * T * (s + 1)
                BK.drained_by(A(ATb[:, b, 0:w], take(("aT", s, hp))[:, 0:w], ACT.Copy), ("aT", s, hp))
            if n in (4, 8):
                rsqrt(st8[:, 16:24], st8[:, 8:16], "at_var", n // 4, "at_rstd")
            for key in beside.get(n, []):
                if key[0] == "gbc":
                    _, _, _, s, half = key
                    copy(key, gbc[:, s, half * 512:(half + 1) * 512])
                elif key[0] == "oT" and key[-1] == 0:
                    copy3(act, BK, key, hT, 0, 0)
        copy3(act, BK, ("oT", 1, 1, 0), hT, 1, 0)
        moe(1)

    @block.vector
    def _(dve):
        V = nc.vector
        TT, TS, STT = V.tensor_tensor, V.tensor_scalar, V.scalar_tensor_tensor
        own = Steps(dve, S("dve_steps"))
        mods = [0]

        def take(key):
            BK.wait_filled(dve, key)
            return BK.bank(key)

        def sig(ins, name):
            ins.then_inc(S(name), 1)

        def mod(l, c):
            n = mods[0]
            mods[0] += 1
            part, half = c // 2, c % 2
            bank = take(("mod", l, c))
            if n < 4:
                dve.wait_ge(S("ld_mbias_first"), 64)
            else:
                dve.wait_ge(S(f"ld_mbias{n % 3}"), 16 * ((n - 1) // 3))
            dst = rowbuf[:, half * 512:half * 512 + 512]
            BK.drained_by(TT(dst, bank, bias_at(n), ALU.add), ("mod", l, c))

        def fold(l, c):
            part = c // 2
            if c % 2 and part not in (2, 5):
                key = ("modT", l, part)
                src = take(key)[:, 0:16]
                dst = modT[:, l, part].rearrange("p k s -> p (k s)")
                BK.drained_by(TS(dst, src, 1.0 if part in (1, 4) else 0.0, None, ALU.add), key)

        def modulated(key, s, k0, l, part):
            bank = take(key)
            BK.wait_drained(dve, ("modT", l, part + 1))
            for n in range(4):
                k = k0 + n
                ins = TS(hT[:, k, s * T:(s + 1) * T], bank[:, n * P:(n + 1) * P], modT[:, l, part + 1, k, s:s + 1],
                         modT[:, l, part, k, s:s + 1], ALU.mult, ALU.add)
            BK.drained_by(ins, key)

        def gated_half(l, w, s, z, half, src):
            if half == 0:
                BK.wait_drained(dve, ("gbc", l, w, s, 1))
            ins = TT(z[:, s, half * 512:(half + 1) * 512], gbc[:, s, half * 512:(half + 1) * 512], src, ALU.mult)
            if w == 0:
                BK.drained_by(ins, ("mix", l, s, half))
                BK.wait_drained(dve, ("mix", l, s, half))
            elif half == 0:
                own.inc(ins)
            else:
                sig(ins, "sums_read")
                dve.wait_ge(S("sums_read"), l * NS + s + 1)
                own.wait()

        def layer_norm(l, w, s, z, src=None):
            n = norm_no(l, w, s)
            for half in range(2 if src else 0):
                gated_half(l, w, s, z, half, src(half))
            own.link(STT(z[:, s, :], x[:, s, :], ALPHA, z[:, s, :], ALU.mult, ALU.add))
            for half in range(2):
                own.inc(V.bn_stats(bns[:, half * 6:half * 6 + 6], z[:, s, half * 512:(half + 1) * 512]))
            own.wait()
            own.link(V.bn_aggr(lns[:, 0:2], bns[:, 0:12].rearrange("p (n c) -> p n c", c=6)))
            sig(TS(lns[:, 4 + s:5 + s], lns[:, 1:2], LN_EPS, None, ALU.add), "ln_var")
            dve.wait_ge(S("ld_ln"), 16 * (l * 2 + w + 1))
            own.link(STT(z[:, s, :], z[:, s, :], lns[:, 0:1], lnp[:, 0, :], ALU.subtract, ALU.mult))
            dve.wait_ge(S("ln_rstd"), n + 1)
            sig(STT(x[:, s, :], z[:, s, :], lns[:, 8 + s:9 + s], lnp[:, 1, :], ALU.mult, ALU.add), "x_new")
            dve.wait_ge(S("x_new"), n + 1)

        V.memset(mbias3, 0.0).then_inc(S("mbias_zero"), 1)
        V.memset(mbias, 0.0).then_inc(S("mbias_zero"), 1)
        dve.wait_ge(S("cond_exp"), 1)
        cw = condw[:, 0:16]
        own.link(TS(cw, cw, 1.0, None, ALU.add))
        own.link(V.reciprocal(condw[:, 16:32], cw))
        own.link(V.memset(cond, 0.0))
        pairs = lambda at: condw[:, at:at + 16].rearrange("p (k s) -> p k s", s=NS)
        sig(TT(cond[:, :, 0:NS], pairs(32), pairs(16), ALU.mult), "cond")
        for c in range(2):
            mod(0, c)
            fold(0, c)
        dve.wait_ge(S("ld_vec"), 16)
        own.inc(TS(nvec[:, 0:15], vec[:, V_MU:V_MU + 15], -1.0, 1.0, ALU.mult, ALU.add))
        own.inc(TS(nvec[:, 15:30], vec[:, V_MU:V_MU + 15], 0.5, None, ALU.mult))
        own.inc(TS(nvec[:, 30:38], vec[:, V_A0:V_A0 + 8], -1.0, None, ALU.mult))
        own.inc(TS(nvec[:, 38:46], vec[:, V_PW:V_PW + 8], -1.0, None, ALU.mult))
        sig(TS(nvec[:, 46:50], vec[:, V_KA:V_KA + 4], -1.0, 1.0, ALU.mult, ALU.add), "vecs")
        dve.wait_ge(S("vecs"), 1)
        for c in range(2, 4):
            mod(0, c)
            fold(0, c)
        for s in range(NS):
            modulated(("xT", "m0", s, 1), s, 4, 0, 0)

        def shifted(i):
            BK.wait_drained(dve, ("pa", i))
            nb = nbr[:, i % 2, :].rearrange("p (s n) -> p s n", s=NS)
            own.link(TT(nb, raw[:, i % 4, :, 0:128], raw[:, i % 4, :, 2:130], ALU.add))
            m = 15 + TILES[i]
            sig(STT(PA[:, i, :], nbr[:, i % 2, :], nvec[:, m:m + 1], PA[:, i, :], ALU.mult, ALU.add), "shifted")
            if i == 6:
                dve.wait_ge(S("lora_exp"), 2)
                for q in (0, 2):
                    own.link(TS(PA[:, q, :], PA[:, q, :], 1.0, None, ALU.add))
                    if q == 0:
                        own.link(V.reciprocal(PA[:, 0, :], PA[:, 0, :]))
                        sig(TS(PA[:, 0, :], PA[:, 0, :], 2.0, -1.0, ALU.mult, ALU.add), "lora")
                    else:
                        sig(V.reciprocal(PA[:, 2, :], PA[:, 2, :]), "lora")
                dve.wait_ge(S("shifted"), 7)
                for t in range(AT):
                    ins = TS(KK[:, t, :], K_[:, t, :], vec[:, V_KK + t:V_KK + t + 1], None, ALU.mult)
                    if t < AT - 1:
                        own.inc(ins)
                sig(ins, "kk")

        def gated(t):
            bank = take(("pb", t))
            dve.wait_ge(S("eg"), t + 1)
            e = eg[:, t % 2, :]
            own.link(TS(e, e, 1.0, None, ALU.add))
            own.link(V.reciprocal(e, e))
            dve.wait_ge(S("zeroed"), 2)
            ins = STT(glu[:, t, :, PADC:PADC + T], bank[:, 0:256].rearrange("p (s n) -> p s n", s=NS),
                      vec[:, V_PW + t:V_PW + t + 1], e.rearrange("p (s n) -> p s n", s=NS), ALU.add, ALU.mult)
            BK.drained_by(ins, ("pb", t))


        def add_w0(s, z):
            BK.drained_by(TT(lw[:, s, z, :], take(("w", s, z)), w0b[:, z, :], ALU.add), ("w", s, z))

        def decay(n):
            s, z = n // 2, n % 2
            dve.wait_ge(S("lw_exp"), n + 1)
            own.link(TS(lw[:, s, z, :], lw[:, s, z, :], 1.0, None, ALU.add))
            sig(V.reciprocal(lw[:, s, z, :], lw[:, s, z, :]), "sigw")

        def learning_rate(z):
            BK.wait_drained(dve, ("a", z, 1))
            az = Ab[:, z].rearrange("p t n -> p (t n)")
            own.link(TS(az, az, 1.0, None, ALU.add))
            own.link(V.reciprocal(az, az))

        def centres(z):
            for t in range(AT):
                bank = take(("cum", z, t))
                mid = bank[:, 0:260].rearrange("p (s n) -> p s n", s=NS)[:, :, 64:65].rearrange("p s n -> p (s n)")
                own.inc(TS(cb[:, 0, z, t, :], mid, -1.0, None, ALU.mult))
                sig(TS(cb[:, 1, z, t, :], mid, 1.0, None, ALU.mult), "centres")

        flat = lambda v: v.rearrange("p t n -> p (t n)")

        def keys(z):
            for t in range(AT):
                own.inc(TS(KZ[:, z, t, :], Ab[:, z, t, :], vec[:, V_KA + t:V_KA + t + 1], nvec[:, 46 + t:47 + t],
                           ALU.mult, ALU.add))
            own.wait()
            own.inc(TT(flat(KZ[:, z]), flat(KZ[:, z]), flat(K_), ALU.mult))
            own.link(STT(flat(Ab[:, z]), flat(KK), -1.0, flat(Ab[:, z]), ALU.mult, ALU.mult))

        for i in range(11):
            shifted(i)
        dve.wait_ge(S("ld_w0"), 16)
        add_w0(0, 0)
        add_w0(0, 1)
        decay(0)
        shifted(11)
        add_w0(1, 0)
        decay(1)
        add_w0(1, 1)
        shifted(12)
        decay(2)
        for tp in range(2):
            bank = take(("ss", tp))
            if tp == 0:
                BK.wait_filled(dve, ("ss", 1))
            BK.drained_by(TS(sq[:, tp * 512:(tp + 1) * 512], bank, 1e-24, None, ALU.max), ("ss", tp))
        shifted(13)
        decay(3)
        shifted(14)
        dve.wait_ge(S("rs"), 1)
        own.link(STT(flat(KK), flat(KK), float(2 ** 16), sq, ALU.mult, ALU.mult))
        gated(0)
        learning_rate(0)
        centres(0)
        gated(1)
        keys(0)
        gated(2)
        centres(1)
        learning_rate(1)
        keys(1)
        own.link(TT(flat(prod), flat(KZ[:, 0]), flat(KZ[:, 1]), ALU.add))
        for t in range(AT):
            ins = STT(prod[:, t, :], R_[:, t, :], vec[:, V_RK + t:V_RK + t + 1], prod[:, t, :], ALU.mult, ALU.mult)
            if t < AT - 1:
                own.inc(ins)
        sig(ins, "prod")
        gated(3)
        BK.wait_drained(dve, ("cum", 1, 3))
        for z in range(2):
            for s in range(NS):
                f, at0 = (1, 0) if (z == 0) == (s == 1) else (0, 128)
                own.inc(V.tensor_copy(fsc[:, z, :, s], FG[:, f, z, :, s, at0]))
        BK.wait_drained(dve, ("pb", AT - 1))
        BK.wait_filled(dve, ("cum", 1, 3))
        for z in range(2):
            up, dn = ((0, slice(1, 129)), (1, slice(1, 129))) if z == 0 else ((1, slice(0, 128)), (0, slice(0, 128)))
            pre = (0, slice(0, 128)) if z == 0 else (1, slice(1, 129))
            for c, (src, (f, r)) in enumerate([(KK, pre), (R_, up), (Ab[:, z], dn), (KZ[:, z], dn)]):
                out = OPS[:, z, :, :, c, :].rearrange("p t s n -> p (t s) n")
                sig(TT(out, src.rearrange("p t (s n) -> p (t s) n", s=NS),
                       FG[:, f, z, :, :, r].rearrange("p t s n -> p (t s) n"), ALU.mult), "ops")
        dve.wait_ge(S("ops"), 8)
        dve.wait_ge(S("ld_s0"), 16)
        for z in range(2):
            for t in range(AT):
                ins = TS(S0[:, z, t, :], S0[:, z, t, :], fsc[:, z, t, 1:2], None, ALU.mult)
                if (z, t) != (1, 3):
                    own.inc(ins)
        sig(ins, "s0")
        BK.drained_by(V.tensor_copy(bon, take(("bonus",))[:, 0:16]), ("bonus",))
        BK.wait_drained(dve, ("bonus",))

        taps = [0]

        def conv(n):
            for _ in range(n):
                if taps[0] == CONV_W * AT:
                    return
                j, t = divmod(taps[0], AT)
                src, w = glu[:, t, :, j:j + T], vec[:, V_DW + j * AT + t:V_DW + j * AT + t + 1]
                out = CONV[:, t, :].rearrange("p (s n) -> p s n", s=NS)
                if j == 0:
                    ins = TS(out, src, w, vec[:, V_DB + t:V_DB + t + 1], ALU.mult, ALU.add)
                else:
                    dve.wait_ge(S("conv"), taps[0] - AT + 1)
                    ins = STT(out, src, w, out, ALU.mult, ALU.add)
                sig(ins, "conv")
                taps[0] += 1

        def group_norm(s):
            dve.wait_ge(S("y_done"), 2 * s + 2)
            BK.wait_filled(dve, ("fT", 1, 1))
            y3 = ps[:, 6 + s, :].rearrange("p (h n) -> p h n", h=H)
            yb3, tb3 = yb.rearrange("p (h n) -> p h n", h=H), tb.rearrange("p (h n) -> p h n", h=H)
            bc = lambda v: v.rearrange("p (h o) -> p h o", o=1).broadcast_to([P, H, HD])
            own.link(V.tensor_reduce(st8[:, 0:8], y3, AX, ALU.add))
            own.link(TS(st8[:, 0:8], st8[:, 0:8], 1.0 / HD, None, ALU.mult))
            own.link(TT(yb3, y3, bc(st8[:, 0:8]), ALU.subtract))
            own.link(TT(tb, yb, yb, ALU.mult))
            own.link(V.tensor_reduce(st8[:, 24:32], tb3, AX, ALU.add))
            sig(TS(st8[:, 8:16], st8[:, 24:32], 1.0 / HD, GN_EPS, ALU.mult, ALU.add), "gn_var")
            dve.wait_ge(S("gn_rstd"), s + 1)
            own.link(TT(yb3, yb3, bc(st8[:, 16:24]), ALU.mult))
            dve.wait_ge(S("ld_gn"), 16)
            own.inc(TT(yb, yb, gnp[:, 0, :], ALU.mult))
            own.link(TT(tb3, VT[:, s, :].rearrange("p (h n) -> p h n", h=H), bc(bon[:, s * 8:s * 8 + 8]), ALU.mult))
            own.link(TT(yb, yb, gnp[:, 1, :], ALU.add))
            own.link(TT(yb, yb, tb, ALU.add))
            bank = take(("g", s))
            BK.drained_by(TT(yb, yb, bank, ALU.mult), ("g", s))
            BK.wait_drained(dve, ("g", s))
            sig(V.tensor_copy(VT[:, s, :], yb), "mixed_a")

        def cln_stats(s):
            bank = take(("cT", s))
            own.link(V.bn_stats(bns[:, 12:18], bank))
            own.link(V.bn_aggr(st8[:, 36 + 2 * s:38 + 2 * s], bns[:, 12:18].rearrange("p (n c) -> p n c", c=6)))
            sig(TS(st8[:, 34 + s:35 + s], st8[:, 37 + 2 * s:38 + 2 * s], LN_EPS, None, ALU.add), "cln_var")
            BK.drained_by(V.tensor_copy(OB[:, s, :], bank), ("cT", s))

        def cln_norm(s):
            y = OB[:, s, :]
            dve.wait_ge(S("ld_cln"), 16)
            BK.wait_drained(dve, ("cT", s))
            own.link(STT(y, y, st8[:, 36 + 2 * s:37 + 2 * s], cln[:, 0, :], ALU.subtract, ALU.mult))
            dve.wait_ge(S("cln_rstd"), s + 1)
            own.link(STT(y, y, st8[:, 32 + s:33 + s], cln[:, 1, :], ALU.mult, ALU.add))
            sig(TS(sigb[s], y, -80.0, None, ALU.max), "cln_y")

        def cln_silu(s):
            dve.wait_ge(S("cln_exp"), s + 1)
            own.link(TS(sigb[s], sigb[s], 1.0, None, ALU.add))
            own.link(V.reciprocal(sigb[s], sigb[s]))
            sig(TT(OB[:, s, :], OB[:, s, :], sigb[s], ALU.mult), "mixed_b")
            dve.wait_ge(S("mixed_b"), s + 1)

        for (s, z) in PAIRS:
            m = cst[:, C_SU:C_SU + 512].rearrange("p (c n) -> p c n", c=4)[:, z::2, :]
            m = m.rearrange("p (o c) n -> p o c n", o=1).broadcast_to([P, 2, 2, P])
            for i in range(4):
                for g in range(2):
                    bank = take(("gram", s, z, g, i))
                    BK.drained_by(TT(MAT[:, g, i].rearrange("p (b c) n -> p b c n", b=2),
                                     bank.rearrange("p (b c n) -> p b c n", b=2, c=2), m, ALU.mult),
                                  ("gram", s, z, g, i))
            m = (SL if z == 0 else SU).rearrange("p (o n) -> p o n", o=1).broadcast_to([P, 4, P])
            for g in range(2):
                BK.drained_by(TT(LS[:, g, 0], take(("L", s, z, g, 0)).rearrange("p (i n) -> p i n", i=4), m, ALU.mult),
                              ("L", s, z, g, 0))
            for j in range(LEVELS):
                for g in range(2):
                    key = ("X", s, z, g, j)
                    bank = take(key)
                    if j == 0:
                        BK.wait_drained(dve, ("B", s, z, g))
                    else:
                        BK.wait_drained(dve, ("X", s, z, g, j - 1))
                    BK.drained_by(TT(XS[:, g, (j + 1) % 2, :], bank[:, 0:256], XS[:, g, j % 2, :], ALU.add), key)
                    if j < LEVELS - 1:
                        key = ("LT", s, z, g, j + 1)
                        BK.drained_by(V.tensor_copy(LT[:, g, (j + 1) % 2].rearrange("p i n -> p (i n)"), take(key)), key)
                    if g == 0 and (s, z, j) in fold_in:
                        fold(*fold_in[(s, z, j)])
                if (s, z, j) in mod_after:
                    mod(*mod_after[(s, z, j)])
                if (s, z, j) in conv_out:
                    cln_stats(conv_out[(s, z, j)])
                if (s, z) == (1, 1) and j in (2, 3):
                    cln_norm(j - 2)
                if (s, z, j) == (1, 1, LEVELS - 1):
                    for n in range(NS):
                        cln_silu(n)
                conv(TAPS)
            if s == 0:
                if z == 1:
                    BK.wait_filled(dve, ("fT", 0, 1))
                for t in range(AT):
                    for c in range(2):
                        ins = TS(fint[:, t, c, :], OPS[:, z, t, 0, 2 + c, :], fsc[:, z, t, 0:1], None, ALU.mult)
                        if (t, c) != (AT - 1, 1):
                            own.inc(ins)
                sig(ins, "fin")
            if (s, z) == (1, 1):
                copy3(dve, BK, ("oT", 0, 0, 1), hT, 0, 4)
            if z == 1:
                group_norm(s)
        for n in range(2):
            gated_half(0, 0, 0, zl, n, take(("mix", 0, 0, n)))
        copy3(dve, BK, ("oT", 0, 1, 1), hT, 1, 4)
        layer_norm(0, 0, 0, zl)
        layer_norm(0, 0, 1, zl, lambda half: take(("mix", 0, 1, half)))

        def moe(l):
            rv = lambda at, n, pattern=None, **z: (rt_[:, at:at + n].rearrange(pattern, **z) if pattern else rt_[:, at:at + n])
            lg = rv(R_LG, 72, "p (s n) -> p s n", s=NS)
            dve.wait_ge(S("ld_rb"), 16 * (l + 1))
            for s in range(NS):
                if s == 1:
                    modulated(("xT", f"e{l}", 1, 1), 1, 4, l, 3)
                BK.drained_by(TT(lg[:, s, :], take(("lg", l, s))[:, 0:36], rb, ALU.add), ("lg", l, s))
            BK.wait_drained(dve, ("lg", l, 1))
            sc = rt_[:, R_S:R_S + 64]
            two = lambda at: sc[:, at:at + 2]
            bc2 = lambda at, n: two(at).rearrange("p (s o) -> p s o", o=1).broadcast_to([P, NS, n])
            row = lambda at, n: cst[:, at:at + n].rearrange("p (o n) -> p o n", o=1).broadcast_to([P, NS, n])

            def first_max(v, n, best, onehot, at_iota):
                own.link(V.tensor_reduce(two(best), v, AX, ALU.max))
                own.link(TT(onehot, v, bc2(best, n), ALU.is_equal))
                own.link(STT(onehot, onehot, -1000.0, row(at_iota, n), ALU.mult, ALU.add))
                own.link(V.tensor_reduce(two(30), onehot, AX, ALU.min))
                own.link(TS(two(30), two(30), 1000.0, None, ALU.add))
                own.link(TT(onehot, row(at_iota, n), bc2(30, n), ALU.is_equal))

            ohg = rv(R_OHG, 8, "p (s n) -> p s n", s=NS)
            ex = rv(R_EX, 8, "p (s n) -> p s n", s=NS)
            first_max(lg[:, :, 0:4], 4, 0, ohg, C_G4)
            sig(TT(ex, lg[:, :, 0:4], bc2(0, 4), ALU.subtract), "routed1")
            t4 = rv(R_T4, 64)
            for s in range(NS):
                own.inc(TT(t4[:, s * 32:(s + 1) * 32].rearrange("p (g e) -> p g e", g=NG),
                           lg[:, s, 4:36].rearrange("p (g e) -> p g e", g=NG),
                           ohg[:, s, :].rearrange("p (g o) -> p g o", o=1).broadcast_to([P, NG, EPG]), ALU.mult))
            own.wait()
            ein = rv(R_EIN, 16, "p (s n) -> p s n", s=NS)
            for s in range(NS):
                own.inc(V.tensor_reduce(ein[:, s, :], t4[:, s * 32:(s + 1) * 32].rearrange("p (g e) -> p e g", g=NG), AX, ALU.add))
            own.wait()
            o1, o2 = rv(R_O1, 16, "p (s n) -> p s n", s=NS), rv(R_O2, 16, "p (s n) -> p s n", s=NS)
            first_max(ein, 8, 2, o1, C_G4 + 4)
            own.link(STT(ein, o1, -1e30, ein, ALU.mult, ALU.add))
            first_max(ein, 8, 4, o2, C_G4 + 4)
            sig(TT(two(16), two(4), two(2), ALU.subtract), "routed2")
            P1, P2 = rv(R_P1, 64), rv(R_P2, 64)
            for dst, oh in ((P1, o1), (P2, o2)):
                for s in range(NS):
                    own.inc(TT(dst[:, s * 32:(s + 1) * 32].rearrange("p (g e) -> p g e", g=NG),
                               ohg[:, s, :].rearrange("p (g o) -> p g o", o=1).broadcast_to([P, NG, EPG]),
                               oh[:, s, :].rearrange("p (o e) -> p o e", o=1).broadcast_to([P, NG, EPG]), ALU.mult))
            own.wait()
            sig(TT(rv(R_OH, 64), P1, P2, ALU.add), "chosen")
            own.link(V.memset(rv(R_ZERO, P), 0.0))
            sig(V.memset(sc[:, 60:62], 0.0), "zero")
            dve.wait_ge(S("route_exp"), 2 * l + 2)
            own.link(V.tensor_reduce(two(20), ex, AX, ALU.add))
            own.link(V.reciprocal(two(22), two(20)))
            own.link(TS(two(24), two(16), 1.0, None, ALU.add))
            own.link(V.reciprocal(two(26), two(24)))
            own.link(TT(two(26), two(26), two(22), ALU.mult))
            own.link(TT(two(28), two(26), two(16), ALU.mult))
            bank = take(("pos", l))
            slot_of = rv(R_SL, 64)
            own.link(V.tensor_copy(sc[0:32, 32:33], bank[0:32, 64:65]))
            own.link(TS(sc[0:32, 33:34], sc[0:32, 32:33], 0.5, None, ALU.is_gt))
            for m in range(1, NS * T // CH):
                own.link(STT(sc[0:32, 33:34], sc[0:32, 32:33], m * CH + 0.5, sc[0:32, 33:34], ALU.is_gt, ALU.add))
            sig(TS(rt_[0:32, R_NB:R_NB + P], ones[0:32, :], sc[0:32, 33:34], None, ALU.mult), "nchunks")
            BK.drained_by(V.tensor_copy(slot_of, bank[:, 0:64]), ("pos", l))
            BK.wait_drained(dve, ("pos", l))
            bank = take(("base", l))
            own.inc(V.tensor_copy(sc[:, 40:41], bank[:, 32:33]))
            own.link(V.tensor_copy(sc[0:32, 41:42], bank[0:32, 64:65]))
            sig(TS(rt_[0:32, R_CMP:R_CMP + 40], cst[0:32, C_G4 + 12:C_G4 + 52], sc[0:32, 41:42], None, ALU.is_ge), "ended")
            own.link(TS(rv(R_T, 32), bank[:, 0:32], float(CH), None, ALU.mult))
            for s in range(NS):
                ins = TT(slot_of[:, s * 32:(s + 1) * 32], slot_of[:, s * 32:(s + 1) * 32], rv(R_T, 32), ALU.add)
                if s == 0:
                    own.inc(ins)
            BK.drained_by(ins, ("base", l))
            BK.wait_drained(dve, ("base", l))
            own.inc(TS(sc[0:1, 46:47], sc[0:1, 40:41], 2.5, None, ALU.subtract))
            own.link(TS(rt_[0:1, R_T + 16:R_T + 36], cst[0:1, C_G4 + 12:C_G4 + 52:2], sc[0:1, 40:41], None, ALU.is_lt))
            own.inc(V.tensor_reduce(sc[0:1, 51:52], rt_[0:1, R_T + 16:R_T + 36], AX, ALU.add))
            own.link(TS(rt_[0:1, R_T:R_T + 10], cst[0:1, C_G4 + 12:C_G4 + 52:4], sc[0:1, 46:47], None, ALU.is_lt))
            own.link(V.tensor_reduce(sc[0:1, 48:49], rt_[0:1, R_T:R_T + 10], AX, ALU.add))
            own.link(STT(sc[0:1, 49:50], sc[0:1, 48:49], -2.0, sc[0:1, 51:52], ALU.mult, ALU.add))
            own.link(TS(sc[0:1, 50:51], sc[0:1, 49:50], -1.0, 1.0, ALU.mult, ALU.add))
            own.link(V.tensor_copy(meta[0:1, l, 0:3], sc[0:1, 48:51]))
            own.link(TS(rt_[0:1, R_T:R_T + 40], take(("eid", l))[0:1, 0:40], float(NE - 1), None, ALU.min))
            BK.drained_by(V.tensor_copy(meta[0:1, l, 4:44], rt_[0:1, R_T:R_T + 40]), ("eid", l))
            BK.wait_drained(dve, ("eid", l))
            sig(V.memset(sc[:, 62:64], 0.0), f"meta{l}")
            dve.wait_ge(S(f"meta{l}"), 1)
            for pick, oh in ((0, P1), (1, P2)):
                own.link(TT(rv(R_T, 64), oh, slot_of, ALU.mult))
                own.link(V.tensor_reduce(sc[:, 42 + 2 * pick:44 + 2 * pick], rv(R_T, 64, "p (s n) -> p s n", s=NS), AX, ALU.add))
            pairs, odd = (dve.value_load(meta[0:1, l, m:m + 1], min_val=lo, max_val=hi)
                          for m, lo, hi in ((0, 1, 10), (1, 0, 1)))
            loop = S(f"dve_loop{l}")

            def chained(m, ins):
                ins.then_inc(loop, 1)
                dve.wait_ge(loop, m)

            def choose(n, m):
                for s in range(NS):
                    TS(sel[:, s, :], iota, sc[:, 42 + s:43 + s], None, ALU.is_equal).then_inc(loop, 1)
                dve.wait_ge(loop, m + 2)
                for s in range(NS):
                    ins = STT(sel[:, s, :], iota, sc[:, 44 + s:45 + s], sel[:, s, :], ALU.is_equal, ALU.add)
                    if s == 0:
                        ins.then_inc(loop, 1)
                ins.then_inc(S(f"selected{l}"), 1)
                dve.wait_ge(loop, m + 3)
                dve.wait_ge(S(f"selected{l}"), n + 1)

            def gates(n, m):
                for s in range(NS):
                    TS(gsel[:, 0, s, :], iota, sc[:, 42 + s:43 + s], sc[:, 26 + s:27 + s], ALU.is_equal, ALU.mult)\
                        .then_inc(loop, 1)
                    TS(gsel[:, 1, s, :], iota, sc[:, 44 + s:45 + s], sc[:, 28 + s:29 + s], ALU.is_equal, ALU.mult)\
                        .then_inc(loop, 1)
                dve.wait_ge(loop, m + 4)
                TT(gsel[:, 0, :, :], gsel[:, 0, :, :], gsel[:, 1, :, :], ALU.add).then_inc(S(f"gates{l}"), 1)
                chained(m + 5, TS(sc[:, 42:46], sc[:, 42:46], float(P), None, ALU.subtract))
                dve.wait_ge(S(f"gates{l}"), n + 1)

            def gathered(n):
                dve.wait_ge(S(f"gathered{l}"), n * 2 + 2)
                V.tensor_copy(xg[:, 4:8, :].rearrange("p k n -> p (k n)"), ps[:, 5, :]).then_inc(S(f"xg_dve{l}"), 1)

            V.memset(tT[1][:, 256:512], 0.0)
            V.memset(ysb, 0.0).then_inc(S(f"y_read_dve{l}"), 1)
            choose(0, 0)
            gates(0, 3)
            gathered(0)
            choose(1, 8)
            def step(n, it, u):
                dve.wait_ge(S(f"gate_exp{l}"), n + 1)
                V.tensor_scalar(hid[:, 0, :], hid[:, 0, :], 1.0, None, ALU.add).then_inc(S(f"dve_hid{l}"), 1)
                dve.wait_ge(S(f"dve_hid{l}"), n * 3 + 1)
                V.reciprocal(hid[:, 0, :], hid[:, 0, :]).then_inc(S(f"dve_hid{l}"), 1)
                dve.wait_ge(S(f"dve_hid{l}"), n * 3 + 2)
                TT(hid[:, 0, :], hid[:, 0, :], ps[:, 6, 0:256], ALU.mult).then_inc(S(f"dve_hid{l}"), 1)
                dve.wait_ge(S(f"dve_hid{l}"), n * 3 + 3)
                TT(hid[:, 1, :], hid[:, 0, :], ps[:, 6, 256:512], ALU.mult).then_inc(S(f"hid{l}"), 1)
                gathered(n + 1)
                dve.wait_ge(S(f"turned{l}"), n + 1)
                gates(n + 1, n * 8 + 11)
                choose(n + 2, n * 8 + 16)
                dve.wait_ge(S(f"down{l}"), n * 2 + 6)
                V.tensor_copy(ysb[:, 512:1024], ps[:, 5, :]).then_inc(S(f"y_read_dve{l}"), 1)

            with dve.Fori(0, pairs) as it:
                for u in range(2):
                    step(it * 2 + u, it, u)
            with dve.If(odd):
                step(pairs * 2, pairs, 0)
            dve.wait_ge(S("summed"), l + 1)
            for s in range(NS):
                layer_norm(l, 1, s, zm, lambda half: ps[:, 2 * s + half, :])

        moe(0)

        modulated(("xT", "m1", 1, 1), 1, 4, 1, 0)
        dve.wait_ge(S("ld_sub"), 32)
        for q in range(2):
            own.link(TT(lqk[:, 2 * q, :], lqk[:, 2 * q, :], lqk[:, 2 * q + 1, :], ALU.mult))
            ins = V.tensor_reduce(lam[:, q:q + 1], lqk[:, 2 * q, :], AX, ALU.add)
            if q == 0:
                own.inc(ins)
        sig(ins, "lam_dot")
        dve.wait_ge(S("ld_rope"), 16)

        def halves(v):
            v = v.rearrange("p (h a b f) -> p h a b f", h=16, a=2, b=2)
            return v[:, :, :, 0, :], v[:, :, :, 1, :]

        cosb = rope[:, 0:32].rearrange("p (o a f) -> p o a f", o=1, a=2).broadcast_to([P, 16, 2, 16])
        sinb = rope[:, 32:64].rearrange("p (o a f) -> p o a f", o=1, a=2).broadcast_to([P, 16, 2, 16])
        rv4 = [rt[:, q, :].rearrange("p (h a f) -> p h a f", h=16, a=2) for q in range(4)]
        for q in range(2):
            BK.wait_drained(dve, ("qkv", 1, 2 * q + 1))
            x1, x2 = halves(QKV[:, 1, q * D:(q + 1) * D])
            y1, y2 = halves(QR[:, q, :])
            if q == 1:
                dve.wait_ge(S("roped"), 1)
            own.inc(TT(rv4[0], x1, cosb, ALU.mult))
            own.inc(TT(rv4[1], x2, sinb, ALU.mult))
            own.inc(TT(rv4[2], x1, sinb, ALU.mult))
            own.inc(TT(rv4[3], x2, cosb, ALU.mult))
            own.wait()
            own.inc(TT(y1, rv4[0], rv4[1], ALU.subtract))
            sig(TT(y2, rv4[2], rv4[3], ALU.add), "roped")
        dve.wait_ge(S("lam_exp"), 1)
        own.link(TT(lam[:, 4:5], lam[:, 2:3], lam[:, 3:4], ALU.subtract))
        own.link(TS(lam[:, 5:6], lam[:, 4:5], LAM_INIT, None, ALU.add))

        def head_norm_stats(s):
            own.link(TT(t1k, OO[:, s, :], OO[:, s, :], ALU.mult))
            own.link(V.tensor_reduce(st8[:, 24:32], t1k.rearrange("p (h n) -> p h n", h=H), AX, ALU.add))
            sig(TS(st8[:, 8:16], st8[:, 24:32], 1.0 / P, RMS_EPS, ALU.mult, ALU.add), "at_var")

        def head_norm(s):
            o3 = OO[:, s, :].rearrange("p (h n) -> p h n", h=H)
            dve.wait_ge(S("at_rstd"), s + 1)
            own.link(TT(o3, o3, st8[:, 16:24].rearrange("p (h o) -> p h o", o=1).broadcast_to([P, H, P]), ALU.mult))
            sg = subg.rearrange("p (o n) -> p o n", o=1).broadcast_to([P, H, P])
            sig(STT(o3, o3, 1.0 - LAM_INIT, sg, ALU.mult, ALU.mult), "attended")

        for n in range(len(PAIRS1) + 1):
            if n < len(PAIRS1):
                s, hp = PAIRS1[n]
                nk = T * (s + 1)
                q = sm1[:, n % 4]
                for z in range(2):
                    bank = take(("sc", s, hp, z))
                    own.link(V.tensor_reduce(q[:, 2 * z:2 * z + 2], bank.rearrange("p (m n) -> p m n", m=2)[:, :, 0:nk],
                                             AX, ALU.max))
                    sig(TS(q[:, 4 + 2 * z:6 + 2 * z], q[:, 2 * z:2 * z + 2], -HD ** -0.5, None, ALU.mult), "smax")
            if n >= 1:
                s, hp = PAIRS1[n - 1]
                b = (n - 1) % 2
                nk = T * (s + 1)
                q = sm1[:, (n - 1) % 4]
                BK.wait_drained(dve, ("sc", s, hp, 1))
                own.link(V.reciprocal(q[:, 12:16], q[:, 8:12]))
                own.link(TS(q[:, 14:16], q[:, 14:16], lam[:, 5:6], None, ALU.mult))
                for m in range(2):
                    own.inc(TS(PB[:, b, 1, m, 0:nk], PB[:, b, 1, m, 0:nk], q[:, 14 + m:15 + m], None, ALU.mult))
                own.wait()
                if n >= 3:
                    BK.wait_filled(dve, ("aT",) + PAIRS1[n - 3])
                for m in range(2):
                    sig(STT(AB[:, b, m, 0:nk], PB[:, b, 0, m, 0:nk], q[:, 12 + m:13 + m], PB[:, b, 1, m, 0:nk],
                            ALU.mult, ALU.subtract), "attn")
            if n == 8:
                gated_half(1, 0, 0, zl1, 0, take(("mix", 1, 0, 0)))
            if n >= 1 and n % 2 == 0:
                s, hp = PAIRS1[n - 1]
                key = ("pv", s, hp // 2)
                BK.drained_by(V.tensor_copy(OO[:, s, (hp // 2) * 512:(hp // 2 + 1) * 512], take(key)), key)
                BK.wait_drained(dve, key)
            if n in (4, 8):
                head_norm_stats(n // 4 - 1)
            if n in (5, 8):
                head_norm((n - 4) // 4)
            if n == 6:
                copy3(dve, BK, ("oT", 1, 0, 1), hT, 0, 4)
            if n == 8:
                gated_half(1, 0, 0, zl1, 1, take(("mix", 1, 0, 1)))
        copy3(dve, BK, ("oT", 1, 1, 1), hT, 1, 4)
        layer_norm(1, 0, 0, zl1)
        layer_norm(1, 0, 1, zl1, lambda half: take(("mix", 1, 1, half)))
        moe(1)

    ctx.close()


def kernel(**inputs):
    import concourse.bacc as bacc
    from concourse.bass_utils import run_bass_kernel_spmd

    a = {k: np.asarray(v) for k, v in inputs.items()}
    tile = lambda w: np.ascontiguousarray(w.reshape(*w.shape[:-2], KT, P, w.shape[-1]).swapaxes(-3, -2))
    cut = lambda w: np.stack([tile(w[:, c:c + 512]) for c in range(0, w.shape[1], 512)]).reshape(-1, P, 4096)
    col = lambda v: np.ascontiguousarray(v.reshape(-1, P).T)
    ev = a["ev_in_w"][0]
    evc = np.concatenate([ev[:, t * P:(t + 1) * P] for t in TILES], 1)
    evp = np.concatenate([tile(evc[:, c:c + 512]).reshape(P, -1) for c in range(0, evc.shape[1], 512)], 1)
    vec = np.concatenate([
        col(a["ev_ts_mu"][0]), col(a["ev_pw_b"][0]), col(a["ev_a0"][0].reshape(-1)), col(a["ev_k_k"][0]),
        col(a["ev_k_a"][0]), col(a["ev_r_k"][0].reshape(-1)), col(a["ev_dw_b"][0]), col(a["ev_dw_w"][0].reshape(-1))], 1)
    s0 = a["state_wkv"][0, 0].transpose(0, 1, 3, 2)
    s0 = s0.reshape(2, AT, P, HD).transpose(2, 0, 1, 3)
    gate = a["ffn_w_gate"].reshape(2, NE, KT, P, FF)
    up = a["ffn_w_up"].reshape(2, NE, KT, P, FF)
    down = a["ffn_w_down"].reshape(2, NE, 2, P, D)
    exp = np.concatenate([
        np.concatenate([gate, up], -1).transpose(0, 1, 3, 2, 4).reshape(2, NE, P, KT * 2 * FF),
        down.transpose(0, 1, 3, 2, 4).reshape(2, NE, P, 2 * D)], -1)
    arrays = {
        "cst": constants(), "rope": rope_tables(), "vec": vec,
        "cond": np.stack([a["c_ctx"], a["c"][0]]).reshape(2, KT, P).transpose(2, 1, 0),
        "x_prompt": a["x_prompt"][0], "x_sample": a["x_sample"][0],
        "mod_w": np.stack([cut(a["mod_w"][l]) for l in range(2)]), "mod_b": a["mod_b"],
        "ev_in_w": evp, "ev_w_up": a["ev_w_up"][0].reshape(P, AW), "ev_a_up": a["ev_a_up"][0].reshape(P, AW),
        "ev_g_up": a["ev_g_up"][0], "s0t": s0, "ev_w0": a["ev_w0"][0],
        "ev_cln": np.stack([a["ev_cln_g"][0], a["ev_cln_b"][0]]), "ev_gn": np.stack([a["ev_gn_g"][0], a["ev_gn_b"][0]]),
        "ev_out_w": cut(a["ev_out_w"][0]), "od_in_w": cut(a["od_in_w"][0]), "od_out_w": cut(a["od_out_w"][0]),
        "ln": np.stack([np.stack([a[f"ln{w}_g"][l], a[f"ln{w}_b"][l]]) for l in range(2) for w in (1, 2)]),
        "lqk": np.stack([a["od_lq1"][0], a["od_lk1"][0], a["od_lq2"][0], a["od_lk2"][0]]),
        "subln": a["od_subln_g"][0],
        "cache_k": a["cache_k"][0, 0].reshape(T, D), "cache_v": a["cache_v"][0, 0].reshape(T, D),
        "r_w": np.stack([tile(np.concatenate([a["rg_w"][l], a["re_w"][l]], 1)).reshape(P, -1) for l in range(2)]),
        "r_b": np.concatenate([a["rg_b"], a["re_b"]], 1), "w_exp": exp,
    }
    outs = {"y": (NS, T, D), "state": (2, H, HD, HD), "cache_k": (T, D), "cache_v": (T, D)}
    nc = bacc.Bacc("TRN2", target_bir_lowering=False, num_devices=1)
    arrays = {f"in_{k}": np.ascontiguousarray(v) for k, v in arrays.items()}
    ins = {k[3:]: nc.dram_tensor(k, v.shape, F32, kind="ExternalInput").ap() for k, v in arrays.items()}
    o = {k: nc.dram_tensor(f"out_{k}", v, F32, kind="ExternalOutput").ap() for k, v in outs.items()}
    build(nc, ins, o)
    r = run_bass_kernel_spmd(nc, [arrays], core_ids=[0]).results[0]
    y = r["out_y"]
    return (y[0:1], y[1:2], r["out_state"].reshape(1, 1, 2, H, HD, HD),
            r["out_cache_k"].reshape(1, 1, T, H, P), r["out_cache_v"].reshape(1, 1, T, H, P))
```
